# Optimizing a Trainium2 kernel written in Bass

```python
import math
import jax, jax.numpy as jnp
from jax import lax
import numpy as np

D_MODEL = 1024
BATCH = 1
SEQ = 1024
DEPTH = 1
DEC_BATCH = 8
DEC_SEQ = 4
PAST_LEN = 2048
PAGE_SIZE = 128

MIX_DIM = D_MODEL
DN_K_DIM = 128
DN_V_DIM = 128
DN_HEADS = (MIX_DIM // 2) // DN_V_DIM
DN_DIM = DN_HEADS * DN_K_DIM
SB_HEAD_DIM = 64
SB_HEADS = (MIX_DIM // 2) // SB_HEAD_DIM
SB_DIM = SB_HEADS * SB_HEAD_DIM
SB_BIAS_INIT = -6.0
CONV_W = 4
CHUNK = 64
Q_BLOCK = 128
D_FF = 2816
QKV_COLS = 3 * DN_DIM
IN_COLS = QKV_COLS + DN_HEADS * DN_V_DIM + 2 * DN_HEADS + 3 * SB_DIM
EPS = 1e-6

kernel_name = "hymba_deltanet_stickbreak_macaron_step"

def rms_norm(x, gain):
    xf = x.astype(jnp.float32)
    y = xf * lax.rsqrt(jnp.mean(xf * xf, axis=-1, keepdims=True) + EPS)
    return (y * gain.astype(jnp.float32)).astype(x.dtype)

def l2_normalize(x):
    xf = x.astype(jnp.float32)
    return xf * lax.rsqrt(jnp.sum(xf * xf, axis=-1, keepdims=True) + EPS)

def swiglu_ffn(x, w_gate_up, w_down):
    gate, up = jnp.split(x @ w_gate_up, 2, axis=-1)
    return (jax.nn.silu(gate) * up) @ w_down

def causal_short_conv(x, hist, w):
    L = x.shape[1]
    xp = jnp.concatenate([hist.astype(x.dtype), x], axis=1)
    y = xp[:, 0:L] * w[0]
    for j in range(1, CONV_W):
        y = y + xp[:, j:j + L] * w[j]
    return jax.nn.silu(y), xp[:, xp.shape[1] - (CONV_W - 1):]

def gated_delta_rule(q, k, v, g, beta, s0):
    B, L, H, dk = q.shape
    dv = v.shape[-1]
    C = min(CHUNK, L)
    n = -(-L // C)
    pad = n * C - L

    def chunks(t):
        t = jnp.pad(t.astype(jnp.float32), [(0, 0), (0, pad)] + [(0, 0)] * (t.ndim - 2))
        t = t.reshape((B, n, C) + t.shape[2:])
        return jnp.moveaxis(jnp.moveaxis(t, 1, 0), 3, 2)

    qc, kc, vc = chunks(q), chunks(k), chunks(v)
    gc, bc = chunks(g), chunks(beta)
    G = jnp.cumsum(gc, axis=-1)
    idx = jnp.arange(C)
    incl = idx[:, None] >= idx[None, :]
    strict = idx[:, None] > idx[None, :]
    decay = jnp.exp(jnp.where(incl, G[..., :, None] - G[..., None, :], -jnp.inf))
    kb = kc * bc[..., None]
    m = jnp.where(strict, jnp.einsum('nbhtk,nbhsk->nbhts', kb, kc) * decay, 0.0)
    rhs = jnp.concatenate([vc * bc[..., None], kb * jnp.exp(G)[..., None]], axis=-1)
    sol = lax.linalg.triangular_solve(m + jnp.eye(C, dtype=m.dtype), rhs,
                                      left_side=True, lower=True, unit_diagonal=True)
    u_base, w_state = sol[..., :dv], sol[..., dv:]
    qk = jnp.einsum('nbhtk,nbhsk->nbhts', qc, kc) * decay

    def step(s, inp):
        q_i, k_i, u_i, w_i, g_i, qk_i = inp
        u = u_i - jnp.einsum('bhck,bhkv->bhcv', w_i, s)
        o = (jnp.einsum('bhck,bhkv->bhcv', q_i * jnp.exp(g_i)[..., None], s)
             + jnp.einsum('bhts,bhsv->bhtv', qk_i, u))
        g_last = g_i[..., -1]
        s = (s * jnp.exp(g_last)[..., None, None]
             + jnp.einsum('bhck,bhcv->bhkv', k_i * jnp.exp(g_last[..., None] - g_i)[..., None], u))
        return s, o

    s, o = lax.scan(step, s0.astype(jnp.float32), (qc, kc, u_base, w_state, G, qk))
    o = jnp.swapaxes(jnp.moveaxis(o, 0, 1), 2, 3).reshape(B, n * C, H, dv)[:, :L]
    return o, s

def stick_breaking_block(q_blk, q_pos, k, v, k_pos, bias):
    z = (jnp.einsum('bqhd,bkhd->bhqk', q_blk.astype(jnp.float32), k.astype(jnp.float32)) * (SB_HEAD_DIM ** -0.5)
         + bias.astype(jnp.float32)[None, :, None, None])
    mask = k_pos[None, :] < q_pos[:, None]
    log_not = jnp.where(mask, jax.nn.log_sigmoid(-z), 0.0)
    between = lax.cumsum(log_not, axis=3, reverse=True) - log_not
    a = jnp.where(mask, jnp.exp(jax.nn.log_sigmoid(z) + between), 0.0)
    return jnp.einsum('bhqk,bkhd->bqhd', a, v.astype(jnp.float32))

def stick_breaking_attention(q, k, v, q_start, bias):
    B, L, H, d = q.shape
    qb = min(Q_BLOCK, L)
    nb = -(-L // qb)
    pad = nb * qb - L
    qp = jnp.moveaxis(jnp.pad(q, ((0, 0), (0, pad), (0, 0), (0, 0))).reshape(B, nb, qb, H, d), 1, 0)
    pos = (q_start + jnp.arange(nb * qb)).reshape(nb, qb)
    k_pos = jnp.arange(k.shape[1])
    o = lax.map(lambda a: stick_breaking_block(a[0], a[1], k, v, k_pos, bias), (qp, pos))
    return jnp.moveaxis(o, 0, 1).reshape(B, nb * qb, H, d)[:, :L]

def token_mixer(u, conv_hist, s0, k_past, v_past, w_in, conv_w, a_log, dt_bias, dn_norm, sb_bias, sb_norm, w_o):
    B, L, _ = u.shape
    proj = u @ w_in
    cuts = np.cumsum([QKV_COLS, DN_HEADS * DN_V_DIM, DN_HEADS, DN_HEADS, SB_DIM, SB_DIM]).tolist()
    qkv_dn, z, a, b, q_sb, k_sb, v_sb = jnp.split(proj, cuts, axis=-1)
    qkv_dn, new_conv = causal_short_conv(qkv_dn, conv_hist, conv_w)
    q_dn, k_dn, v_dn = jnp.split(qkv_dn, 3, axis=-1)
    q_dn = l2_normalize(q_dn.reshape(B, L, DN_HEADS, DN_K_DIM)) * (DN_K_DIM ** -0.5)
    k_dn = l2_normalize(k_dn.reshape(B, L, DN_HEADS, DN_K_DIM))
    v_dn = v_dn.reshape(B, L, DN_HEADS, DN_V_DIM)
    g = -jnp.exp(a_log.astype(jnp.float32)) * jax.nn.softplus(a.astype(jnp.float32) + dt_bias.astype(jnp.float32))
    beta = jax.nn.sigmoid(b.astype(jnp.float32))
    o_dn, s_new = gated_delta_rule(q_dn, k_dn, v_dn, g, beta, s0)
    o_dn = rms_norm(o_dn, dn_norm) * jax.nn.silu(z.reshape(B, L, DN_HEADS, DN_V_DIM).astype(jnp.float32))
    q_sb = q_sb.reshape(B, L, SB_HEADS, SB_HEAD_DIM)
    k_sb = k_sb.reshape(B, L, SB_HEADS, SB_HEAD_DIM)
    v_sb = v_sb.reshape(B, L, SB_HEADS, SB_HEAD_DIM)
    k_all = jnp.concatenate([k_past.astype(k_sb.dtype), k_sb], axis=1)
    v_all = jnp.concatenate([v_past.astype(v_sb.dtype), v_sb], axis=1)
    o_sb = rms_norm(stick_breaking_attention(q_sb, k_all, v_all, k_past.shape[1], sb_bias), sb_norm)
    mixed = jnp.concatenate([o_dn.reshape(B, L, DN_HEADS * DN_V_DIM), o_sb.reshape(B, L, SB_DIM)], axis=-1)
    return mixed.astype(u.dtype) @ w_o, k_sb, v_sb, s_new, new_conv

def decoder_layer(x, conv_hist, s0, k_past, v_past, norms, f1_gu, f1_d, w_in, conv_w, a_log, dt_bias,
                  dn_norm, sb_bias, sb_norm, w_o, f2_gu, f2_d):
    h = x + 0.5 * rms_norm(swiglu_ffn(rms_norm(x, norms[0]), f1_gu, f1_d), norms[1])
    mix, k_new, v_new, s_new, conv_new = token_mixer(rms_norm(h, norms[2]), conv_hist, s0, k_past, v_past,
                                                     w_in, conv_w, a_log, dt_bias, dn_norm, sb_bias, sb_norm, w_o)
    h = h + rms_norm(mix, norms[3])
    h = h + 0.5 * rms_norm(swiglu_ffn(rms_norm(h, norms[4]), f2_gu, f2_d), norms[5])
    return h, k_new, v_new, s_new, conv_new

def run_group(x, conv_state, delta_state, past_k, past_v, norms, ffn1_w_gate_up, ffn1_w_down, w_in, conv_w,
              a_log, dt_bias, dn_out_norm, sb_logit_bias, sb_out_norm, w_o, ffn2_w_gate_up, ffn2_w_down):
    ks, vs, ss, cs = [], [], [], []
    for l in range(DEPTH):
        x, k_new, v_new, s_new, c_new = decoder_layer(
            x, conv_state[l], delta_state[l], past_k(l), past_v(l), norms[l], ffn1_w_gate_up[l], ffn1_w_down[l],
            w_in[l], conv_w[l], a_log[l], dt_bias[l], dn_out_norm[l], sb_logit_bias[l], sb_out_norm[l], w_o[l],
            ffn2_w_gate_up[l], ffn2_w_down[l])
        ks.append(k_new); vs.append(v_new); ss.append(s_new); cs.append(c_new)
    return x, jnp.stack(ks, axis=2), jnp.stack(vs, axis=2), jnp.stack(ss, axis=0), jnp.stack(cs, axis=0)

def setup_inputs(seed: int = 0) -> dict:
    key = jax.random.key(seed)
    ks = jax.random.split(key, 21)
    f32 = jnp.float32
    n_pages = PAST_LEN // PAGE_SIZE
    n_used = DEC_BATCH * n_pages
    n_phys = n_used + max(1, n_used // 4)

    def nrm(k, shape, scale):
        return jax.random.normal(k, shape, f32) * scale

    dt = jnp.exp(jax.random.uniform(ks[13], (DEPTH, DN_HEADS), f32, math.log(1e-3), math.log(1e-1)))
    return {
        "x_prompt": nrm(ks[0], (BATCH, SEQ, D_MODEL), 1.0),
        "x_sample": nrm(ks[1], (DEC_BATCH, DEC_SEQ, D_MODEL), 1.0),
        "cache_sb_k": nrm(ks[2], (n_phys, PAGE_SIZE, DEPTH, SB_HEADS, SB_HEAD_DIM), 1.0),
        "cache_sb_v": nrm(ks[3], (n_phys, PAGE_SIZE, DEPTH, SB_HEADS, SB_HEAD_DIM), 1.0),
        "page_table": jax.random.permutation(ks[4], n_phys)[:n_used].reshape(DEC_BATCH, n_pages).astype(jnp.int32),
        "state_delta": nrm(ks[5], (DEPTH, DEC_BATCH, DN_HEADS, DN_K_DIM, DN_V_DIM), 0.1),
        "state_conv": nrm(ks[6], (DEPTH, DEC_BATCH, CONV_W - 1, QKV_COLS), 1.0),
        "norms": 1.0 + nrm(ks[7], (DEPTH, 6, D_MODEL), 0.02),
        "ffn1_w_gate_up": nrm(ks[8], (DEPTH, D_MODEL, 2 * D_FF), D_MODEL ** -0.5),
        "ffn1_w_down": nrm(ks[9], (DEPTH, D_FF, D_MODEL), D_FF ** -0.5),
        "w_in": nrm(ks[10], (DEPTH, D_MODEL, IN_COLS), D_MODEL ** -0.5),
        "conv_w": nrm(ks[11], (DEPTH, CONV_W, QKV_COLS), CONV_W ** -0.5),
        "a_log": jnp.log(jax.random.uniform(ks[12], (DEPTH, DN_HEADS), f32, 1.0, 16.0)),
        "dt_bias": dt + jnp.log(-jnp.expm1(-dt)),
        "dn_out_norm": 1.0 + nrm(ks[14], (DEPTH, DN_V_DIM), 0.02),
        "sb_logit_bias": SB_BIAS_INIT + nrm(ks[19], (DEPTH, SB_HEADS), 0.1),
        "sb_out_norm": 1.0 + nrm(ks[15], (DEPTH, SB_HEAD_DIM), 0.02),
        "w_o": nrm(ks[16], (DEPTH, MIX_DIM, D_MODEL), MIX_DIM ** -0.5),
        "ffn2_w_gate_up": nrm(ks[17], (DEPTH, D_MODEL, 2 * D_FF), D_MODEL ** -0.5),
        "ffn2_w_down": nrm(ks[18], (DEPTH, D_FF, D_MODEL), D_FF ** -0.5),
    }

def reference(x_prompt, x_sample, cache_sb_k, cache_sb_v, page_table, state_delta, state_conv, norms,
              ffn1_w_gate_up, ffn1_w_down, w_in, conv_w, a_log, dt_bias, dn_out_norm, sb_logit_bias, sb_out_norm,
              w_o, ffn2_w_gate_up, ffn2_w_down):
    bp = x_prompt.shape[0]
    zero_conv = jnp.zeros((DEPTH, bp, CONV_W - 1, QKV_COLS), x_prompt.dtype)
    zero_delta = jnp.zeros((DEPTH, bp, DN_HEADS, DN_K_DIM, DN_V_DIM), jnp.float32)
    empty = jnp.zeros((bp, 0, SB_HEADS, SB_HEAD_DIM), x_prompt.dtype)
    y_prompt, k_rows_prompt, v_rows_prompt, delta_prompt, conv_prompt = run_group(
        x_prompt, zero_conv, zero_delta, lambda l: empty, lambda l: empty, norms, ffn1_w_gate_up, ffn1_w_down,
        w_in, conv_w, a_log, dt_bias, dn_out_norm, sb_logit_bias, sb_out_norm, w_o, ffn2_w_gate_up, ffn2_w_down)

    def gather_past(cache, l):
        rows = cache[:, :, l][page_table]
        return rows.reshape(rows.shape[0], rows.shape[1] * rows.shape[2], SB_HEADS, SB_HEAD_DIM)

    y_sample, k_rows_sample, v_rows_sample, delta_sample, conv_sample = run_group(
        x_sample, state_conv, state_delta, lambda l: gather_past(cache_sb_k, l), lambda l: gather_past(cache_sb_v, l),
        norms, ffn1_w_gate_up, ffn1_w_down, w_in, conv_w, a_log, dt_bias, dn_out_norm, sb_logit_bias, sb_out_norm,
        w_o, ffn2_w_gate_up, ffn2_w_down)

    return (y_prompt, y_sample, k_rows_prompt, v_rows_prompt, k_rows_sample, v_rows_sample,
            delta_prompt, delta_sample, conv_prompt, conv_sample)


_drawn_inputs = setup_inputs


def setup_inputs(seed=0):
    import zlib

    import numpy as np

    out = dict(_drawn_inputs(seed))
    spreads = {}
    factors = {}
    for name, (base, spread) in spreads.items():
        noise = np.random.default_rng([zlib.crc32(name.encode()), seed]).standard_normal(out[name].shape)
        drawn = base * np.exp(spread * noise) if base else spread * noise
        out[name] = __import__('jax').numpy.asarray(drawn.astype(out[name].dtype))
    for name, factor in factors.items():
        out[name] = (out[name] * factor).astype(out[name].dtype)
    return out
```

```python
import concourse.bass as bass
from concourse import mybir
from concourse.alu_op_type import AluOpType as ALU
from contextlib import ExitStack

F32 = mybir.dt.float32
F32R = mybir.dt.float32r
I32 = mybir.dt.int32
ACT = mybir.ActivationFunctionType
AX = mybir.AxisListType

P = 128
D = 1024
T_P, N_B, L_S = 1024, 8, 4
T_S = N_B * L_S
T = T_P + T_S
KC = D // P
NT = T_P // P
TB = T // 3
F = 2816
GROUPS = F // (2 * P)
H_DN, H_SB, DH = 4, 8, 64
DN = H_DN * P
QKV = 3 * DN
SB = H_SB * DH
EPS = 1e-6
TILE0 = [P * i for i in range(NT)] + [T - P]


def rows_view(dram):
    return dram[0:T_P, :].rearrange("(i p) n -> p i n", p=P)


class Scope:

    def __init__(self, nc, ctx, tag):
        self.nc, self.ctx, self.tag = nc, ctx, tag
        self.events = {}
        self.handles = []
        ctx.callback(self.close)

    def close(self):
        if self.handles:
            self.nc.clear_and_free_semaphores(self.handles)
            self.nc.all_engine_barrier()

    def sb(self, name, shape, dt=F32):
        return self.ctx.enter_context(self.nc.sbuf_tensor(f"{self.tag}_{name}", shape, dt))

    def ps(self, name, shape):
        return self.ctx.enter_context(self.nc.psum_tensor(f"{self.tag}_{name}", shape, F32))

    def sem(self, name):
        self.handles.append(self.nc.alloc_semaphore(f"{self.tag}_{name}"))
        return self.handles[-1]

    def event(self, name):
        if name not in self.events:
            self.events[name] = self.sem(name)
        return self.events[name]

    def sems(self, names):
        return [self.sem(n) for n in names.split()]


def at_least(engine, sem, value):
    if not isinstance(value, int) or value > 0:
        engine.wait_ge(sem, value)


def seam(nc, tag, y, residual, post_gain, post_scale, h_out, pre_gain, uh, ul, ident):
    with ExitStack() as ctx:
        s = Scope(nc, ctx, tag)
        post, pre = post_gain is not None, pre_gain is not None
        g_post = s.sb("g_post", [P, D]) if post else None
        g_pre = s.sb("g_pre", [P, D]) if pre else None
        res = s.sb("res", [P, NT + 1, D]) if post else y
        junk = s.sb("junk", [P, 2, D])
        stat = s.sb("stat", [P, 4, NT + 1])
        hn = s.sb("hn", [P, 2, D]) if pre else None
        pt = [s.ps(f"pt{n}", [P, KC, P]) for n in range(2)] if pre else None
        (loaded, gains, scaled_gain, sq1, var1, root1, rstd1, normed, summed, sq2, var2, root2, rstd2,
         hn_ready, transposed, hi_done, lo_done, stored) = s.sems(
            "loaded gains scaled_gain sq1 var1 root1 rstd1 normed summed sq2 var2 root2 rstd2 "
            "hn_ready transposed hi_done lo_done stored")
        block = ctx.enter_context(nc.Block())

        @block.sync
        def _(sp):
            sp.dma_start(res[:, 0:NT, :], rows_view(residual)).then_inc(loaded, 16)
            sp.dma_start(res[:, NT, :], residual[T - P:T, :]).then_inc(loaded, 16)
            if post:
                sp.dma_start(g_post[:], post_gain.partition_broadcast(P)).then_inc(gains, 16)
            if pre:
                sp.dma_start(g_pre[:], pre_gain.partition_broadcast(P)).then_inc(gains, 16)
            if h_out is not None:
                with sp.Fori(0, NT) as i:
                    sp.wait_ge(summed, i + 1)
                    sp.dma_start(rows_view(h_out)[:, bass.ds(i, 1), :], y[:, bass.ds(i, 1), :]).then_inc(stored, 16)
                sp.wait_ge(summed, NT + 1)
                sp.dma_start(h_out[T_P:T, :], y[P - T_S:P, NT, :]).then_inc(stored, 16)
                sp.wait_ge(stored, 16 * (NT + 1))

        @block.scalar
        def _(act):
            if post:
                with act.Fori(0, NT + 1) as i:
                    nc.scalar.activation(junk[:, 0, :], y[:, bass.ds(i, 1), :], ACT.Square,
                                         accum_out=stat[:, 0, bass.ds(i, 1)]).then_inc(sq1, 1)
                    act.wait_ge(sq1, i + 1)
                act.wait_ge(var1, 1)
                nc.scalar.activation(stat[:, 1, :], stat[:, 0, :], ACT.Sqrt).then_inc(root1, 1)
            else:
                act.wait_ge(loaded, 32)
            if pre:
                with act.Fori(0, NT + 1) as i:
                    if post:
                        act.wait_ge(summed, i + 1)
                    nc.scalar.activation(junk[:, 0, :], y[:, bass.ds(i, 1), :], ACT.Square,
                                         accum_out=stat[:, 2, bass.ds(i, 1)]).then_inc(sq2, 1)
                    act.wait_ge(sq2, i + 1)
                act.wait_ge(var2, 1)
                nc.scalar.activation(stat[:, 3, :], stat[:, 2, :], ACT.Sqrt).then_inc(root2, 1)

                def hi_part(i, n, width):
                    act.wait_ge(transposed, i + 1)
                    nc.scalar.activation(uh[:, :, width], pt[n][:, :, P - width_of(width):P], ACT.Copy).then_inc(hi_done, 1)

                with act.Fori(0, NT // 2) as i2:
                    for n in range(2):
                        hi_part(2 * i2 + n, n, bass.ds((2 * i2 + n) * P, P))
                hi_part(NT, 0, slice(T_P, T))

        @block.vector
        def _(dve):
            if post:
                dve.wait_ge(gains, 32 if pre else 16)
                nc.vector.tensor_scalar(g_post[:], g_post[:], post_scale, None, ALU.mult).then_inc(scaled_gain, 1)
                dve.wait_ge(sq1, NT + 1)
                nc.vector.tensor_scalar(stat[:, 0, :], stat[:, 0, :], 1.0 / D, EPS, ALU.mult, ALU.add).then_inc(var1, 1)
                dve.wait_ge(root1, 1)
                nc.vector.reciprocal(stat[:, 1, :], stat[:, 1, :]).then_inc(rstd1, 1)
                dve.wait_ge(rstd1, 1)
                dve.wait_ge(scaled_gain, 1)
                with dve.Fori(0, NT + 1) as i:
                    nc.vector.scalar_tensor_tensor(y[:, bass.ds(i, 1), :], y[:, bass.ds(i, 1), :], stat[:, 1, bass.ds(i, 1)],
                                                   g_post[:], ALU.mult, ALU.mult).then_inc(normed, 1)
            if pre:
                if not post:
                    dve.wait_ge(gains, 16)
                dve.wait_ge(sq2, NT + 1)
                nc.vector.tensor_scalar(stat[:, 2, :], stat[:, 2, :], 1.0 / D, EPS, ALU.mult, ALU.add).then_inc(var2, 1)
                dve.wait_ge(root2, 1)
                nc.vector.reciprocal(stat[:, 3, :], stat[:, 3, :]).then_inc(rstd2, 1)
                dve.wait_ge(rstd2, 1)

                def normalize(i, n, k):
                    nc.vector.scalar_tensor_tensor(hn[:, n, :], y[:, k, :], stat[:, 3, k], g_pre[:],
                                                   ALU.mult, ALU.mult).then_inc(hn_ready, 1)

                def lo_part(i, n, width):
                    dve.wait_ge(hi_done, i + 1)
                    nc.vector.tensor_tensor(ul[:, :, width], pt[n][:, :, P - width_of(width):P],
                                            uh[:, :, width].bitcast(F32), ALU.subtract).then_inc(lo_done, 1)

                with dve.Fori(0, NT // 2) as i2:
                    for n in range(2):
                        i = 2 * i2 + n
                        normalize(i, n, bass.ds(i, 1))
                        lo_part(i, n, bass.ds(i * P, P))
                normalize(NT, 0, slice(NT, NT + 1))
                lo_part(NT, 0, slice(T_P, T))

        @block.gpsimd
        def _(pool):
            if post:
                pool.wait_ge(loaded, 32)
                with pool.Fori(0, NT + 1) as i:
                    pool.wait_ge(normed, i + 1)
                    nc.gpsimd.tensor_tensor(y[:, bass.ds(i, 1), :], y[:, bass.ds(i, 1), :], res[:, bass.ds(i, 1), :],
                                            ALU.add).then_inc(summed, 1)

        @block.tensor
        def _(pe):
            if pre:
                def transposes(i, n):
                    pe.wait_ge(hn_ready, i + 1)
                    for k in range(KC):
                        last = nc.tensor.transpose(pt[n][:, k, :], hn[:, n, k * P:(k + 1) * P], ident[:])
                    last.then_inc(transposed, 1)

                with pe.Fori(0, NT // 2) as i2:
                    for n in range(2):
                        transposes(2 * i2 + n, n)
                transposes(NT, 0)


def width_of(span):
    return T_S if isinstance(span, slice) else P


def ffn(nc, tag, uh, ul, w_gate_up, w_down, y):
    with ExitStack() as ctx:
        s = Scope(nc, ctx, tag)
        raw = {k: s.sb(f"raw_{k}", [P, 2 * D]) for k in "gud"}
        w_hi = {k: s.sb(f"hi_{k}", [P, 2, D], F32R) for k in "gud"}
        w_lo = {k: s.sb(f"lo_{k}", [P, 2, D], F32R) for k in "gud"}
        silu = s.sb("silu", [P, 3, TB])
        hid = s.sb("hid", [P, 3, TB])
        hid_hi = s.sb("hid_hi", [P, 2, T], F32R)
        hid_lo = s.sb("hid_lo", [P, 2, T], F32R)
        pg = [s.ps(f"pg{t}", [P, 512]) for t in range(3)]
        pu = [s.ps(f"pu{t}", [P, 512]) for t in range(3)]
        pd = [s.ps(f"pd{n}", [P, 512]) for n in range(2)]
        ld = {k: s.sem(f"loaded_{k}") for k in "gud"}
        hi = {k: s.sem(f"hi_{k}") for k in "gud"}
        lo = {k: s.sem(f"lo_{k}") for k in "gud"}
        gate_mm, up_mm, down_mm, silu_done, hid_done, hid_hi_done, hid_lo_done, added, zeroed = s.sems(
            "gate_mm up_mm down_mm silu_done hid_done hid_hi_done hid_lo_done added zeroed")
        block = ctx.enter_context(nc.Block())

        gate_view = w_gate_up[:, 0:F].rearrange("(k p) (g c) -> g p k c", p=P, c=2 * P)
        up_view = w_gate_up[:, F:2 * F].rearrange("(k p) (g c) -> g p k c", p=P, c=2 * P)
        down_view = w_down.rearrange("(g e p) n -> g p e n", p=P, e=2)
        view = {"g": gate_view, "u": up_view, "d": down_view}

        def raw_half(k, e):
            if k == "d":
                return raw[k][:, e * D:(e + 1) * D]
            return raw[k][:].rearrange("p (k e c) -> p e k c", e=2, c=P)[:, e]

        def tiled(w, k, e):
            return w[k][:, e, :] if k == "d" else w[k][:, e, :].rearrange("p (k c) -> p k c", c=P)

        @block.sync
        def _(sp):
            def load(k, g):
                dst = raw[k][:].rearrange("p (a c) -> p a c", c=D if k == "d" else 2 * P)
                src = view[k][g] if isinstance(g, int) else view[k][bass.ds(g, 1)].rearrange("g p a c -> p (g a) c")
                sp.dma_start(dst, src).then_inc(ld[k], 16)

            for k in "gud":
                load(k, 0)
            with sp.Fori(1, GROUPS) as g:
                for k in "gud":
                    sp.wait_ge(lo[k], 2 * g)
                    load(k, g)

        @block.gpsimd
        def _(pool):
            nc.gpsimd.memset(y[:], 0.0).then_inc(zeroed, 1)

        @block.tensor
        def _(pe):
            def project(k, e, g, banks, done, freed):
                pe.wait_ge(lo[k], 2 * g + e + 1)
                if not (isinstance(g, int) and 2 * g + e == 0):
                    pe.wait_ge(freed, 2 * g + e)
                for t in range(3):
                    cols = slice(t * TB, (t + 1) * TB)
                    for c in range(KC):
                        wh, wl = (w[k][:, e, c * P:(c + 1) * P] for w in (w_hi, w_lo))
                        nc.tensor.matmul(banks[t][:, 0:TB], wh, uh[:, c, cols], start=(c == 0), stop=False)
                        nc.tensor.matmul(banks[t][:, 0:TB], wh, ul[:, c, cols], start=False, stop=False)
                        last = nc.tensor.matmul(banks[t][:, 0:TB], wl, uh[:, c, cols], start=False, stop=(c == KC - 1))
                    last.then_inc(done, 1)

            def down(g):
                pe.wait_ge(hid_lo_done, 2 * g + 2)
                pe.wait_ge(lo["d"], 2 * g + 2)
                for n in range(2 * (NT + 1)):
                    i, half = n // 2, n % 2
                    if n >= 2 or not isinstance(g, int):
                        pe.wait_ge(added, 2 * (NT + 1) * g + n - 1)
                    for e in range(2):
                        hh, hl = (x[:, e, TILE0[i]:TILE0[i] + P] for x in (hid_hi, hid_lo))
                        wh, wl = (w["d"][:, e, half * 512:half * 512 + 512] for w in (w_hi, w_lo))
                        nc.tensor.matmul(pd[n % 2][:], hh, wh, start=(e == 0), stop=False)
                        nc.tensor.matmul(pd[n % 2][:], hl, wh, start=False, stop=False)
                        last = nc.tensor.matmul(pd[n % 2][:], hh, wl, start=False, stop=(e == 1))
                    last.then_inc(down_mm, 1)

            def group(g, first):
                project("g", 0, g, pg, gate_mm, silu_done)
                if not first:
                    down(g - 1)
                project("u", 0, g, pu, up_mm, hid_done)
                project("g", 1, g, pg, gate_mm, silu_done)
                project("u", 1, g, pu, up_mm, hid_done)

            group(0, True)
            group(1, False)
            with pe.Fori(2, GROUPS) as g:
                group(g, False)
            down(GROUPS - 1)

        @block.scalar
        def _(act):
            def round_half(k, g, e, used):
                act.wait_ge(ld[k], 16 * g + 16)
                if used is not None:
                    act.wait_ge(*used)
                nc.scalar.activation(tiled(w_hi, k, e), raw_half(k, e), ACT.Copy).then_inc(hi[k], 1)

            def gate(g, e):
                if not (isinstance(g, int) and 2 * g + e == 0):
                    act.wait_ge(hid_done, 2 * g + e)
                for t in range(3):
                    act.wait_ge(gate_mm, 6 * g + 3 * e + t + 1)
                    last = nc.scalar.activation(silu[:, t, :], pg[t][:, 0:TB], ACT.Silu)
                last.then_inc(silu_done, 1)

            def hidden(g, e):
                act.wait_ge(hid_done, 2 * g + e + 1)
                nc.scalar.activation(hid_hi[:, e, :], hid[:].rearrange("p t n -> p (t n)"), ACT.Copy).then_inc(hid_hi_done, 1)

            def group(g, first, last):
                gate(g, 0)
                if not last:
                    round_half("g", g + 1, 0, (gate_mm, 6 * g + 3))
                hidden(g, 0)
                if not last:
                    round_half("u", g + 1, 0, (up_mm, 6 * g + 3))
                for e in range(2):
                    round_half("d", g, e, None if first else (down_mm, 2 * (NT + 1) * g))
                gate(g, 1)
                if not last:
                    round_half("g", g + 1, 1, (gate_mm, 6 * g + 6))
                hidden(g, 1)
                if not last:
                    round_half("u", g + 1, 1, (up_mm, 6 * g + 6))

            for e in range(2):
                round_half("g", 0, e, None)
                round_half("u", 0, e, None)
            group(0, True, False)
            with act.Fori(1, GROUPS - 1) as g:
                group(g, False, False)
            group(GROUPS - 1, False, True)

        @block.vector
        def _(dve):
            def rest_half(k, g, e):
                dve.wait_ge(hi[k], 2 * g + e + 1)
                nc.vector.tensor_tensor(tiled(w_lo, k, e), raw_half(k, e), tiled(w_hi, k, e).bitcast(F32),
                                        ALU.subtract).then_inc(lo[k], 1)

            def hidden(g, e):
                if not (isinstance(g, int) and 2 * g + e == 0):
                    dve.wait_ge(hid_lo_done, 2 * g + e)
                dve.wait_ge(silu_done, 2 * g + e + 1)
                for t in range(3):
                    dve.wait_ge(up_mm, 6 * g + 3 * e + t + 1)
                    last = nc.vector.tensor_tensor(hid[:, t, :], silu[:, t, :], pu[t][:, 0:TB], ALU.mult)
                last.then_inc(hid_done, 1)
                dve.wait_ge(hid_hi_done, 2 * g + e + 1)
                nc.vector.tensor_tensor(hid_lo[:, e, :], hid[:].rearrange("p t n -> p (t n)"),
                                        hid_hi[:, e, :].bitcast(F32), ALU.subtract).then_inc(hid_lo_done, 1)

            def add_down(g):
                for n in range(2 * (NT + 1)):
                    i, half = n // 2, n % 2
                    dve.wait_ge(down_mm, 2 * (NT + 1) * g + n + 1)
                    part = y[:, i, half * 512:half * 512 + 512]
                    nc.vector.tensor_tensor(part, part, pd[n % 2][:], ALU.add).then_inc(added, 1)

            def group(g, first, last):
                if not last:
                    rest_half("g", g + 1, 0)
                if not first:
                    add_down(g - 1)
                hidden(g, 0)
                if not last:
                    rest_half("u", g + 1, 0)
                for e in range(2):
                    rest_half("d", g, e)
                if not last:
                    rest_half("g", g + 1, 1)
                hidden(g, 1)
                if not last:
                    rest_half("u", g + 1, 1)

            for e in range(2):
                rest_half("g", 0, e)
                rest_half("u", 0, e)
            dve.wait_ge(zeroed, 1)
            group(0, True, False)
            with dve.Fori(1, GROUPS - 1) as g:
                group(g, False, False)
            group(GROUPS - 1, False, True)
            add_down(GROUPS - 1)


def make_ident(nc, ident):
    with ExitStack() as ctx:
        s = Scope(nc, ctx, "id")
        ones = s.sb("ones", [P, P])
        filled = s.sem("filled")
        block = ctx.enter_context(nc.Block())

        @block.gpsimd
        def _(pool):
            nc.gpsimd.memset(ones[:], 1.0).then_inc(filled, 1)
            pool.wait_ge(filled, 1)
            nc.gpsimd.affine_select(out=ident[:], in_=ones[:], compare_op=ALU.is_equal, fill=0.0, base=0,
                                    pattern=[[-1, P]], channel_multiplier=1).then_inc(filled, 1)
            pool.wait_ge(filled, 2)


PAIRS = 14
KIND = ["conv"] * 6 + ["gate"] * 2 + ["query"] * 2 + ["key"] * 2 + ["value"] * 2
AB0 = QKV + DN
XP = T_P + 3 + N_B * (L_S + 3)
TAIL = 3 * (1 + N_B)


def projections(nc, uh, ul, w_in, conv_w, state_conv, qt, kt, ab, qkv_nat, gate_nat, k_rows, v_rows, conv_rows, ident):
    with ExitStack() as ctx:
        s = Scope(nc, ctx, "pr")
        raw = s.sb("raw", [P, 2, KC, 2 * P])
        w_hi, w_lo = s.sb("w_hi", [P, 2, D], F32R), s.sb("w_lo", [P, 2, D], F32R)
        ab_raw = s.sb("ab_raw", [P, KC, 8])
        ab_hi, ab_lo = s.sb("ab_hi", [P, KC, 8], F32R), s.sb("ab_lo", [P, KC, 8], F32R)
        xp = s.sb("xp", [P, 2, XP])
        acc = s.sb("acc", [P, T])
        post = s.sb("post", [P, 2, T])
        nat = s.sb("nat", [P, 2, NT + 1, P])
        taps = s.sb("taps", [P, 12, 4])
        taps_nat = s.sb("taps_nat", [4, QKV])
        hist_nat = s.sb("hist_nat", [3 * N_B, QKV])
        hist = s.sb("hist", [P, 12, 3 * N_B])
        tail = s.sb("tail", [P, 12, TAIL])
        tail_nat = s.sb("tail_nat", [TAIL, QKV])
        pm = [[s.ps(f"pm{e}{t}", [P, 512]) for t in range(3)] for e in range(2)]
        pn = [s.ps(f"pn{n}", [P, 512]) for n in range(2)]
        loaded = s.sems("loaded0 loaded1")
        (small, rounded, rest, ab_hi_done, ab_split, mm, ab_mm, ab_done, padded, hist_tr, hist_done, filled,
         tapped, convolved, ready, natural, evacuated, tail_taken, tail_tr, tail_done, tail_out) = s.sems(
            "small rounded rest ab_hi_done ab_split mm ab_mm ab_done padded hist_tr hist_done filled "
            "tapped convolved ready natural evacuated tail_taken tail_tr tail_done tail_out")
        stored = s.sems("stored0 stored1")
        block = ctx.enter_context(nc.Block())

        def sample(x, lo):
            return x[:, T_P + 3:XP].rearrange("p (b l) -> p b l", l=L_S + 3)[:, :, lo:lo + L_S]

        def pair_columns(j):
            return 2 * P * j + (8 if j >= 8 else 0)

        has_rows = [k != "query" for k in KIND for _ in range(2)]
        row_units = [sum(has_rows[:n]) for n in range(2 * PAIRS + 1)]

        @block.sync
        def _(sp):
            for j in range(2):
                sp.dma_start(raw[:, j], w_in[:, 2 * P * j:2 * P * (j + 1)].rearrange("(k p) c -> p k c", p=P)).then_inc(loaded[j], 16)
            sp.dma_start(ab_raw[:], w_in[:, AB0:AB0 + 8].rearrange("(k p) c -> p k c", p=P)).then_inc(small, 16)
            sp.dma_start(hist_nat[:], state_conv).then_inc(small, 16)
            sp.dma_start(taps_nat[:], conv_w).then_inc(small, 16)
            for j in range(2, PAIRS):
                sp.wait_ge(rest, 2 * j - 2)
                c = pair_columns(j)
                sp.dma_start(raw[:, j % 2], w_in[:, c:c + 2 * P].rearrange("(k p) c -> p k c", p=P)).then_inc(loaded[j % 2], 16)

        @block.gpsimd
        def _(pool):
            nc.gpsimd.memset(xp[:, :, 0:3], 0.0).then_inc(padded, 1)
            target = ([(qkv_nat, u * P) for u in range(12)] + [(gate_nat, u * P) for u in range(4)] + [None] * 4
                      + [(k_rows, u * P) for u in range(4)] + [(v_rows, u * P) for u in range(4)])
            for n in range(2 * PAIRS):
                if not has_rows[n]:
                    continue
                r = row_units[n]
                dram, c = target[n]
                pool.wait_ge(evacuated, 3 * (r + 1))
                pool.dma_start(rows_view(dram)[:, :, c:c + P], nat[:, r % 2, 0:NT, :]).then_inc(stored[r % 2], 16)
                pool.dma_start(dram[T_P:T, c:c + P], nat[0:T_S, r % 2, NT, :]).then_inc(stored[r % 2], 16)
            pool.wait_ge(tail_done, 3)
            pool.dma_start(conv_rows, tail_nat[:]).then_inc(tail_out, 16)
            pool.wait_ge(tail_out, 16)
            for b in range(2):
                pool.wait_ge(stored[b], 16 * row_units[2 * PAIRS])

        @block.tensor
        def _(pe):
            def project(n):
                e = n % 2
                pe.wait_ge(rest, n + 1)
                if n >= 2:
                    pe.wait_ge(filled, n - 1)
                for t in range(3):
                    cols = slice(t * TB, (t + 1) * TB)
                    for c in range(KC):
                        wh, wl = (x[:, e, c * P:(c + 1) * P] for x in (w_hi, w_lo))
                        nc.tensor.matmul(pm[e][t][:, 0:TB], wh, uh[:, c, cols], start=(c == 0), stop=False)
                        nc.tensor.matmul(pm[e][t][:, 0:TB], wh, ul[:, c, cols], start=False, stop=False)
                        last = nc.tensor.matmul(pm[e][t][:, 0:TB], wl, uh[:, c, cols], start=False, stop=(c == KC - 1))
                last.then_inc(mm, 1)

            def to_rows(n):
                if not has_rows[n]:
                    return
                r = row_units[n]
                src = kt[:, n - 20, :] if KIND[n // 2] == "key" else post[:, n % 2, :]
                pe.wait_ge(ready, n + 1)
                for b in range(3):
                    if 3 * r + b >= 2:
                        pe.wait_ge(evacuated, 3 * r + b - 1)
                    for i in range(4 * b, min(4 * b + 4, NT + 1)):
                        rows = P if i < NT else T_S
                        last = nc.tensor.transpose(pn[(3 * r + b) % 2][0:rows, (i % 4) * P:(i % 4) * P + P],
                                                   src[:, i * P:i * P + rows], ident[:])
                    last.then_inc(natural, 1)

            pe.wait_ge(small, 48)
            for u in range(12):
                nc.tensor.transpose(pm[1][1][:, u * 4:u * 4 + 4], taps_nat[:, u * P:(u + 1) * P], ident[0:4, 0:4])
                last = nc.tensor.transpose(pm[1][0][:, u * 24:u * 24 + 24], hist_nat[:, u * P:(u + 1) * P], ident[0:24, 0:24])
            last.then_inc(hist_tr, 1)
            pe.wait_ge(hist_done, 1)
            for n in range(2 * PAIRS):
                project(n)
                if n >= 1:
                    to_rows(n - 1)
            to_rows(2 * PAIRS - 1)
            pe.wait_ge(ab_split, 1)
            pe.wait_ge(filled, 2 * PAIRS)
            for i in range(NT + 1):
                for c in range(KC):
                    out, rows = pm[0][0][:, 8 * i:8 * i + 8], slice(TILE0[i], TILE0[i] + P)
                    nc.tensor.matmul(out, uh[:, c, rows], ab_hi[:, c, :], start=(c == 0), stop=False)
                    nc.tensor.matmul(out, ul[:, c, rows], ab_hi[:, c, :], start=False, stop=False)
                    last = nc.tensor.matmul(out, uh[:, c, rows], ab_lo[:, c, :], start=False, stop=(c == KC - 1))
            last.then_inc(ab_mm, 1)
            pe.wait_ge(tail_taken, 12)
            for u in range(12):
                last = nc.tensor.transpose(pm[1][u // 4][0:TAIL, (u % 4) * P:(u % 4) * P + P], tail[:, u, :], ident[:])
                if u % 4 == 3:
                    last.then_inc(tail_tr, 1)

        @block.scalar
        def _(act):
            def round_half(n):
                e = n % 2
                act.wait_ge(loaded[n // 2 % 2], 16 * (n // 4) + 16)
                if n >= 2:
                    act.wait_ge(mm, n - 1)
                nc.scalar.activation(w_hi[:, e, :].rearrange("p (k c) -> p k c", c=P), raw[:, n // 2 % 2, :, e * P:(e + 1) * P],
                                     ACT.Copy).then_inc(rounded, 1)

            round_half(0)
            round_half(1)
            act.wait_ge(small, 48)
            nc.scalar.activation(ab_hi[:], ab_raw[:], ACT.Copy).then_inc(ab_hi_done, 1)
            act.wait_ge(hist_tr, 1)
            nc.scalar.activation(taps[:].rearrange("p u c -> p (u c)"), pm[1][1][:, 0:48], ACT.Copy)
            nc.scalar.activation(hist[:].rearrange("p u c -> p (u c)"), pm[1][0][:, 0:288], ACT.Copy).then_inc(hist_done, 1)

            def rows_out(n):
                if not has_rows[n]:
                    return
                r = row_units[n]
                if r >= 2:
                    act.wait_ge(stored[r % 2], 32 * (r // 2))
                for b in range(3):
                    act.wait_ge(natural, 3 * r + b + 1)
                    rows, count = (P, 4) if b < 2 else (T_S, 1)
                    nc.scalar.activation(nat[0:rows, r % 2, 4 * b:4 * b + count, :].rearrange("p i c -> p (i c)"),
                                         pn[(3 * r + b) % 2][0:rows, 0:count * P], ACT.Copy).then_inc(evacuated, 1)

            for n in range(2 * PAIRS):
                e, kind = n % 2, KIND[n // 2]
                act.wait_ge(mm, n + 1)
                banks = pm[e]
                if kind == "conv":
                    if n == 0:
                        act.wait_ge(padded, 1)
                        act.wait_ge(hist_done, 1)
                    if n >= 2:
                        act.wait_ge(tail_taken, n - 1)
                    for t in range(3):
                        end = min(T_P, (t + 1) * TB) - t * TB
                        nc.scalar.activation(xp[:, e, 3 + t * TB:3 + t * TB + end], banks[t][:, 0:end], ACT.Copy)
                    nc.scalar.activation(sample(xp[:, e], 3), banks[2][:, TB - T_S:TB].rearrange("p (b l) -> p b l", l=L_S), ACT.Copy)
                    nc.scalar.activation(sample(xp[:, e], 0)[:, :, 0:3], hist[:, n, :].rearrange("p (b l) -> p b l", l=3),
                                         ACT.Copy).then_inc(filled, 1)
                    if n + 2 < 2 * PAIRS:
                        round_half(n + 2)
                    if n >= 1:
                        rows_out(n - 1)
                    act.wait_ge(convolved, n + 1)
                    if n >= 2:
                        act.wait_ge(natural, 3 * row_units[n - 1])
                    nc.scalar.activation(post[:, e, :], acc[:], ACT.Silu).then_inc(ready, 1)
                else:
                    if kind in ("gate", "value"):
                        act.wait_ge(natural, 3 * row_units[n - 1])
                    for t in range(3):
                        cols = slice(t * TB, (t + 1) * TB)
                        if kind == "query":
                            last = nc.scalar.activation(qt[:, n - 16, cols], banks[t][:, 0:TB], ACT.Copy, scale=DH ** -0.5)
                        elif kind == "key":
                            last = nc.scalar.activation(kt[:, n - 20, cols], banks[t][:, 0:TB], ACT.Copy)
                        else:
                            last = nc.scalar.activation(post[:, e, cols], banks[t][:, 0:TB],
                                                        ACT.Silu if kind == "gate" else ACT.Copy)
                    last.then_inc(filled, 1)
                    act.wait_ge(filled, n + 1)
                    act.sem_inc(ready, 1)
                    if n + 2 < 2 * PAIRS:
                        round_half(n + 2)
                    rows_out(n - 1)
            rows_out(2 * PAIRS - 1)
            act.wait_ge(ab_mm, 1)
            nc.scalar.activation(ab[:].rearrange("p i c -> p (i c)"), pm[0][0][:, 0:8 * (NT + 1)], ACT.Copy).then_inc(ab_done, 1)
            for b in range(3):
                act.wait_ge(tail_tr, b + 1)
                nc.scalar.activation(tail_nat[:, b * 512:b * 512 + 512], pm[1][b][0:TAIL, :], ACT.Copy).then_inc(tail_done, 1)

        @block.vector
        def _(dve):
            def rest_half(n):
                e = n % 2
                dve.wait_ge(rounded, n + 1)
                nc.vector.tensor_tensor(w_lo[:, e, :].rearrange("p (k c) -> p k c", c=P), raw[:, n // 2 % 2, :, e * P:(e + 1) * P],
                                        w_hi[:, e, :].bitcast(F32).rearrange("p (k c) -> p k c", c=P),
                                        ALU.subtract).then_inc(rest, 1)

            rest_half(0)
            rest_half(1)
            dve.wait_ge(ab_hi_done, 1)
            nc.vector.tensor_tensor(ab_lo[:], ab_raw[:], ab_hi[:].bitcast(F32), ALU.subtract).then_inc(ab_split, 1)
            for n in range(2 * PAIRS):
                e = n % 2
                if n < 12:
                    dve.wait_ge(filled, n + 1)
                    if n >= 1:
                        dve.wait_ge(ready, n)
                    prompt_acc = acc[:, 0:T_P]
                    sample_acc = acc[:, T_P:T].rearrange("p (b l) -> p b l", l=L_S)
                    for j in range(4):
                        tap = taps[:, n, j:j + 1]
                        for out, src in ((prompt_acc, xp[:, e, j:j + T_P]), (sample_acc, sample(xp[:, e], j))):
                            if j == 0:
                                step = nc.vector.tensor_scalar(out, src, tap, None, ALU.mult)
                            else:
                                step = nc.vector.scalar_tensor_tensor(out, src, tap, out, ALU.mult, ALU.add)
                            step.then_inc(tapped, 1)
                            if j < 3:
                                dve.wait_ge(tapped, 8 * n + 2 * j + (1 if out is prompt_acc else 2))
                    dve.wait_ge(tapped, 8 * n + 8)
                    nc.vector.tensor_copy(tail[:, n, 0:3], xp[:, e, T_P:T_P + 3]).then_inc(convolved, 1)
                    nc.vector.tensor_copy(tail[:, n, 3:TAIL].rearrange("p (b l) -> p b l", l=3),
                                          xp[:, e, T_P + 3:XP].rearrange("p (b l) -> p b l", l=L_S + 3)[:, :, L_S:L_S + 3]
                                          ).then_inc(tail_taken, 1)
                if n + 2 < 2 * PAIRS:
                    rest_half(n + 2)


BIG = 2.0 ** 40


def prompt_attention(nc, qt, kt, v_rows, bias_row, o_all, ident):
    UNITS = [(i, e) for i in reversed(range(NT)) for e in range(2)]
    N = len(UNITS)
    LONG = sum(i >= 4 for i, _ in UNITS)
    with ExitStack() as ctx:
        s = Scope(nc, ctx, "pa")
        v = s.sb("v", [P, NT, SB])
        bias = s.sb("bias", [P, H_SB])
        pair_bias = s.sb("pair_bias", [P, 2])
        mask = s.sb("mask", [P, P])
        ones = s.sb("ones", [P, P])
        zeros = s.sb("zeros", [P, T_P])
        qz = s.sb("qz", [P, 2, T_P])
        ex = s.sb("ex", [P, 4, T_P])
        run = s.sb("run", [P, 2, T_P])
        wt = s.sb("wt", [P, 2, T_P])
        pz = [s.ps(f"pz{n}", [P, T_P]) for n in range(2)]
        pa = [s.ps(f"pa{n}", [P, 512]) for n in range(2)]
        po = [s.ps(f"po{n}", [P, 512]) for n in range(2)]
        (loaded, constants, q_zero, q_ready, z_mm, exped, held, logged, summed, decayed, weighted, turned_a, turned_b,
         copied_a, copied_b, o_mm, o_done) = s.sems(
            "loaded constants q_zero q_ready z_mm exped held logged summed decayed weighted turned_a turned_b "
            "copied_a copied_b o_mm o_done")
        block = ctx.enter_context(nc.Block())

        @block.sync
        def _(sp):
            sp.dma_start(v[:], rows_view(v_rows)).then_inc(loaded, 16)
            sp.dma_start(bias[:], bias_row.partition_broadcast(P)).then_inc(loaded, 16)

        @block.gpsimd
        def _(pool):
            nc.gpsimd.memset(ones[:], 1.0).then_inc(constants, 1)
            nc.gpsimd.memset(zeros[:], 0.0).then_inc(constants, 1)
            pool.wait_ge(constants, 2)
            nc.gpsimd.affine_select(out=mask[:], in_=ones[:], compare_op=ALU.is_gt, fill=0.0, base=0,
                                    pattern=[[-1, P]], channel_multiplier=1).then_inc(constants, 1)
            nc.gpsimd.memset(qz[:], 0.0).then_inc(q_zero, 1)

        @block.tensor
        def _(pe):
            def scores(hp, u):
                i, e = UNITS[u]
                pe.wait_ge(exped, N * hp + u - 1) if not isinstance(hp, int) or N * hp + u >= 2 else None
                for c in range(0, (i + 1) * P, 512):
                    cols = slice(c, min(c + 512, (i + 1) * P))
                    last = nc.tensor.matmul(pz[u % 2][:, cols], qz[:, e, i * P:(i + 1) * P],
                                            kt[:, bass.ds(hp, 1), cols], start=True, stop=True)
                last.then_inc(z_mm, 1)

            def turn_and_sum(hp, u, first):
                i, e = UNITS[u]
                pe.wait_ge(weighted, N * hp + u + 1)
                for c in range(2 if i >= 4 else 1):
                    if not (first and u == 0):
                        pe.wait_ge((copied_a, copied_b)[c], (N * hp + u) if c == 0 else (LONG * hp + u))
                    for j in range(4 * c, min(4 * c + 4, i + 1)):
                        last = nc.tensor.transpose(pa[c][:, (j % 4) * P:(j % 4) * P + P], ex[:, u % 4, j * P:(j + 1) * P], ident[:])
                    last.then_inc((turned_a, turned_b)[c], 1)
                if not (first and u < 2):
                    pe.wait_ge(o_done, N * hp + u - 1)
                for j in range(i + 1):
                    if j == 0:
                        pe.wait_ge(copied_a, N * hp + u + 1)
                    if j == 4:
                        pe.wait_ge(copied_b, LONG * hp + u + 1)
                    last = nc.tensor.matmul(po[u % 2][:, 0:DH], wt[:, u % 2, j * P:(j + 1) * P],
                                            v[:, j, bass.ds((2 * hp + e) * DH, DH)], start=(j == 0), stop=(j == i))
                last.then_inc(o_mm, 1)

            def pair(hp, first):
                pe.wait_ge(q_ready, 3 * hp + 3)
                for k in range(N + 3):
                    if k < N:
                        scores(hp, k)
                    if k >= 3:
                        turn_and_sum(hp, k - 3, first)

            pe.wait_ge(loaded, 32)
            pair(0, True)
            with pe.Fori(1, 4) as hp:
                pair(hp, False)

        @block.scalar
        def _(act):
            def step(hp, k, first):
                n = N * hp
                if k < N:
                    i, e = UNITS[k]
                    w = (i + 1) * P
                    act.wait_ge(z_mm, n + k + 1)
                    if not (first and k < 4):
                        act.wait_ge(o_mm, n + k - 3)
                    nc.scalar.activation(ex[:, k % 4, 0:w], pz[k % 2][:, 0:w], ACT.Exp,
                                         bias=pair_bias[:, e:e + 1]).then_inc(exped, 1)
                if 1 <= k <= N:
                    u = k - 1
                    w = (UNITS[u][0] + 1) * P
                    act.wait_ge(held, n + u + 1)
                    if not (first and u < 2):
                        act.wait_ge(weighted, n + u - 1)
                    nc.scalar.activation(run[:, u % 2, 0:w], ex[:, u % 4, 0:w], ACT.Ln, bias=1.0).then_inc(logged, 1)
                if 2 <= k <= N + 1:
                    u = k - 2
                    w = (UNITS[u][0] + 1) * P
                    act.wait_ge(summed, n + u + 1)
                    nc.scalar.activation(run[:, u % 2, 0:w], run[:, u % 2, 0:w], ACT.Exp, scale=-1.0).then_inc(decayed, 1)
                if k >= 3:
                    u = k - 3
                    w = min(512, (UNITS[u][0] + 1) * P)
                    act.wait_ge(turned_a, n + u + 1)
                    if not (first and u < 2):
                        act.wait_ge(o_mm, n + u - 1)
                    nc.scalar.activation(wt[:, u % 2, 0:w], pa[0][:, 0:w], ACT.Copy).then_inc(copied_a, 1)

            nc.scalar.preload_act_table_set("natural_log_exp_and_others")
            for k in range(N + 3):
                step(0, k, True)
            with act.Fori(1, 4) as hp:
                for k in range(N + 3):
                    step(hp, k, False)

        @block.vector
        def _(dve):
            def step(hp, k, first):
                n = N * hp
                if k < N:
                    i, e = UNITS[k]
                    w = (i + 1) * P
                    dve.wait_ge(exped, n + k + 1)
                    x = ex[:, k % 4]
                    if i > 0:
                        nc.vector.tensor_scalar(x[:, 0:w - P], x[:, 0:w - P], BIG, None, ALU.min)
                    nc.vector.scalar_tensor_tensor(x[:, w - P:w], x[:, w - P:w], BIG, mask[:], ALU.min, ALU.mult).then_inc(held, 1)
                if 1 <= k <= N:
                    u = k - 1
                    w = (UNITS[u][0] + 1) * P
                    dve.wait_ge(logged, n + u + 1)
                    back = run[:, u % 2, 0:w][:, ::-1]
                    nc.vector.tensor_tensor_scan(back, back, zeros[:, 0:w], 0.0, ALU.add, ALU.add).then_inc(summed, 1)
                if 2 <= k <= N + 1:
                    u = k - 2
                    w = (UNITS[u][0] + 1) * P
                    dve.wait_ge(decayed, n + u + 1)
                    nc.vector.tensor_tensor(ex[:, u % 4, 0:w], ex[:, u % 4, 0:w], run[:, u % 2, 0:w], ALU.mult).then_inc(weighted, 1)
                if k >= 3:
                    u = k - 3
                    i, e = UNITS[u]
                    if i >= 4:
                        w = (i + 1) * P
                        dve.wait_ge(turned_b, LONG * hp + u + 1)
                        if not (first and u < 2):
                            dve.wait_ge(o_mm, n + u - 1)
                        nc.vector.tensor_copy(wt[:, u % 2, 512:w], pa[1][:, 0:w - 512]).then_inc(copied_b, 1)
                    dve.wait_ge(o_mm, n + u + 1)
                    nc.vector.tensor_copy(o_all[:, i, bass.ds((2 * hp + e) * DH, DH)], po[u % 2][:, 0:DH]).then_inc(o_done, 1)

            def stage_queries(hp):
                nc.vector.tensor_copy(pair_bias[:], bias[:, bass.ds(2 * hp, 2)]).then_inc(q_ready, 1)
                for e in range(2):
                    rows = slice(e * DH, (e + 1) * DH)
                    nc.vector.tensor_copy(qz[rows, e, :], qt[rows, bass.ds(hp, 1), 0:T_P]).then_inc(q_ready, 1)

            dve.wait_ge(q_zero, 1)
            dve.wait_ge(loaded, 32)
            dve.wait_ge(constants, 3)
            stage_queries(0)
            for k in range(N + 3):
                step(0, k, True)
            with dve.Fori(1, 4) as hp:
                stage_queries(hp)
                for k in range(N + 3):
                    step(hp, k, False)


LEVELS = 7
FACTORS = "rq rqg rk rkb rkbg rkd beta".split()


def delta_masks(nc, masks, tri_s, same_s, level_s, spread_s, ones):
    with ExitStack() as ctx:
        s = Scope(nc, ctx, "dm")
        made = s.sem("made")
        block = ctx.enter_context(nc.Block())

        @block.gpsimd
        def _(pool):
            count = 0

            def select(out, pattern, base, mult, op=ALU.is_ge):
                nonlocal count
                nc.gpsimd.affine_select(out=out, in_=out, compare_op=op, fill=0.0, base=base, pattern=pattern,
                                        channel_multiplier=mult).then_inc(made, 1)
                count += 1
                pool.wait_ge(made, count)

            def fill(out):
                nonlocal count
                nc.gpsimd.memset(out, 1.0).then_inc(made, 1)
                count += 1
                pool.wait_ge(made, count)

            fill(ones[:])
            fill(masks[:])
            select(masks[:, 0, :], [[1, P]], 0, -1)
            for n in range(LEVELS):
                b = 1 << n
                view = masks[:, 1 + n, :].rearrange("p (m two c) -> p m two c", two=2, c=b)
                select(view[:, :, 1, :], [[-2 * b, P // (2 * b)], [0, b]], 0, 1)
                select(view[:, :, 1, :], [[2 * b, P // (2 * b)], [0, b]], b - 1, -1)
                nc.gpsimd.memset(view[:, :, 0, :], 0.0).then_inc(made, 1)
                count += 1
                pool.wait_ge(made, count)
            for m in (tri_s, same_s, spread_s):
                fill(m[:])
            select(spread_s[:], [[-L_S, N_B]], 0, 1)
            select(spread_s[:], [[L_S, N_B]], L_S - 1, -1)
            for m in (tri_s, same_s):
                v = m[:].rearrange("p (b l) -> p b l", l=L_S)
                select(v, [[-L_S, N_B], [0, L_S]], 0, 1)
                select(v, [[L_S, N_B], [0, L_S]], L_S - 1, -1)
            select(tri_s[:], [[1, T_S]], 0, -1)
            for n in range(2):
                nc.gpsimd.tensor_copy(level_s[:, n, :], masks[0:T_S, 1 + n, 0:T_S]).then_inc(made, 1)
                count += 1
            pool.wait_ge(made, count)


def delta_gates(nc, ab, qkv_nat, dt_row, a_log_row, masks, tri_s, same_s, spread_s, ones, qkv, g, big_g, last_decay,
                last_decay_s, fac):
    with ExitStack() as ctx:
        s = Scope(nc, ctx, "dg")
        E = s.event
        abx = s.sb("abx", [P, NT + 1, 8])
        dt, a_log = s.sb("dt", [P, 4]), s.sb("a_log", [P, 4])
        x, e, w, wi, l = (s.sb(n, [P, NT + 1, 4]) for n in "x e w wi l".split())
        last = s.sb("last", [P, NT + 1, 4])
        sq = s.sb("sq", [P, D])
        norm = s.sb("norm", [P, NT + 1, 8])
        gm = s.sb("gm", [T_S, N_B, 4])
        pg, pl = s.ps("pg", [P, 512]), s.ps("pl", [P, 512])
        ps_, pls = s.ps("ps", [P, 512]), s.ps("pls", [P, 512])
        pb = s.ps("pb", [P, 512])
        block = ctx.enter_context(nc.Block())

        @block.sync
        def _(sp):
            sp.dma_start(qkv[:, 0:NT, :], rows_view(qkv_nat)).then_inc(E("rows_in"), 16)
            sp.dma_start(qkv[0:T_S, NT, :], qkv_nat[T_P:T, :]).then_inc(E("rows_in"), 16)
            sp.dma_start(dt[:], dt_row.partition_broadcast(P)).then_inc(E("small_in"), 16)
            sp.dma_start(a_log[:], a_log_row.partition_broadcast(P)).then_inc(E("small_in"), 16)
            sp.wait_ge(E("abx_zero"), 1)
            sp.dma_start(abx[0:T_S, NT, :], ab[P - T_S:P, NT, :]).then_inc(E("small_in"), 16)

        @block.gpsimd
        def _(pool):
            nc.gpsimd.memset(qkv[T_S:2 * T_S, NT, :], 0.0)
            nc.gpsimd.memset(qkv[2 * T_S:P, NT, :], 0.0).then_inc(E("rows_zero"), 1)

        @block.vector
        def _(dve):
            n = 0

            def then(step):
                nonlocal n
                n += 1
                step.then_inc(E("dve_step"), 1)
                dve.wait_ge(E("dve_step"), n)

            nc.vector.memset(abx[:, NT, :], 0.0).then_inc(E("abx_zero"), 1)
            then(nc.vector.tensor_copy(abx[:, 0:NT, :], ab[:, 0:NT, :]))
            dve.wait_ge(E("small_in"), 48)
            then(nc.vector.tensor_tensor(x[:], abx[:, :, 0:4], dt[:].rearrange("p (o h) -> p o h", o=1).broadcast_to([P, NT + 1, 4]), ALU.add))
            nc.vector.tensor_scalar(e[:], x[:], 40.0, None, ALU.min).then_inc(E("x_held"), 1)
            dve.wait_ge(E("exp_x"), 1)
            then(nc.vector.tensor_scalar(w[:], e[:], 1.0, None, ALU.add))
            nc.vector.reciprocal(wi[:], w[:]).then_inc(E("one_plus"), 1)
            then(nc.vector.scalar_tensor_tensor(w[:], w[:], -1.0, e[:], ALU.add, ALU.subtract))
            dve.wait_ge(E("one_plus"), 1)
            then(nc.vector.tensor_tensor(w[:], w[:], wi[:], ALU.mult))
            dve.wait_ge(E("ln_w"), 1)
            then(nc.vector.tensor_tensor(l[:], l[:], w[:], ALU.subtract))
            then(nc.vector.tensor_tensor(l[:], l[:], x[:], ALU.max))
            dve.wait_ge(E("exp_a"), 1)
            nc.vector.scalar_tensor_tensor(g[:], l[:], -1.0, a_log[:].rearrange("p (o h) -> p o h", o=1).broadcast_to([P, NT + 1, 4]), ALU.mult, ALU.mult).then_inc(E("g_ready"), 1)
            dve.wait_ge(E("exp_b"), 1)
            then(nc.vector.tensor_scalar(fac["beta"][:], fac["beta"][:], 1.0, None, ALU.add))
            then(nc.vector.reciprocal(fac["beta"][:], fac["beta"][:]))
            dve.wait_ge(E("g_ready"), 1)
            nc.vector.tensor_tensor(gm[:], g[0:T_S, NT:NT + 1, :].broadcast_to([T_S, N_B, 4]),
                                    spread_s[:].rearrange("p (b o) -> p b o", o=1).broadcast_to([T_S, N_B, 4]), ALU.mult).then_inc(E("gm_ready"), 1)
            dve.wait_ge(E("rows_in"), 32)
            dve.wait_ge(E("rows_zero"), 1)
            with dve.Fori(0, NT + 1) as i:
                nc.vector.tensor_tensor(sq[:].rearrange("p (o n) -> p o n", o=1), qkv[:, bass.ds(i, 1), 0:D], qkv[:, bass.ds(i, 1), 0:D], ALU.mult).then_inc(E("squared"), 1)
                dve.wait_ge(E("squared"), i + 1)
                nc.vector.tensor_reduce(norm[:, bass.ds(i, 1), :], sq[:].rearrange("p (h c) -> p h c", c=P), AX.X, ALU.add).then_inc(E("reduced"), 1)
                dve.wait_ge(E("reduced"), i + 1)
            nc.vector.tensor_scalar(norm[:], norm[:], EPS, None, ALU.add).then_inc(E("norm_sum"), 1)
            dve.wait_ge(E("norm_root"), 1)
            then(nc.vector.reciprocal(norm[:], norm[:]))
            then(nc.vector.tensor_scalar(fac["rq"][:], norm[:, :, 0:4], float(P) ** -0.5, None, ALU.mult))
            then(nc.vector.tensor_copy(fac["rk"][:], norm[:, :, 4:8]))
            dve.wait_ge(E("sums"), 1)
            nc.vector.tensor_copy(big_g[:, 0:NT, :].rearrange("p i h -> p (i h)"), pg[:, 0:32])
            nc.vector.memset(last[:, NT, :], 0.0)
            nc.vector.memset(big_g[:, NT, :], 0.0)
            then(nc.vector.tensor_copy(last[:, 0:NT, :].rearrange("p i h -> p (i h)"), pl[:, 0:32]))
            then(nc.vector.tensor_copy(big_g[0:T_S, NT, :], ps_[0:T_S, 0:4]))
            then(nc.vector.tensor_copy(last[0:T_S, NT, :], pls[0:T_S, 0:4]))
            then(nc.vector.tensor_tensor(wi[:], last[:], big_g[:], ALU.subtract))
            nc.vector.tensor_copy(last_decay_s[:], pb[:, 0:32].rearrange("p (b h) -> p b h", h=4)).then_inc(E("to_exp"), 1)
            dve.wait_ge(E("exps"), 1)
            then(nc.vector.tensor_tensor(fac["rkb"][:], fac["rk"][:], fac["beta"][:], ALU.mult))
            then(nc.vector.tensor_tensor(fac["rqg"][:], fac["rq"][:], x[:], ALU.mult))
            then(nc.vector.tensor_tensor(fac["rkbg"][:], fac["rkb"][:], x[:], ALU.mult))
            then(nc.vector.tensor_tensor(fac["rkd"][:], fac["rk"][:], wi[:], ALU.mult))

        @block.scalar
        def _(act):
            nc.scalar.preload_act_table_set("natural_log_exp_and_others")
            act.wait_ge(E("x_held"), 1)
            nc.scalar.activation(e[:], e[:], ACT.Exp).then_inc(E("exp_x"), 1)
            nc.scalar.activation(a_log[:], a_log[:], ACT.Exp).then_inc(E("exp_a"), 1)
            nc.scalar.activation(fac["beta"][:], abx[:, :, 4:8], ACT.Exp, scale=-1.0).then_inc(E("exp_b"), 1)
            act.wait_ge(E("exp_x"), 1)
            nc.scalar.activation(l[:], e[:], ACT.Ln, bias=1.0).then_inc(E("ln_w"), 1)
            act.wait_ge(E("norm_sum"), 1)
            nc.scalar.activation(norm[:], norm[:], ACT.Sqrt).then_inc(E("norm_root"), 1)
            act.wait_ge(E("to_exp"), 1)
            nc.scalar.activation(x[:], big_g[:], ACT.Exp).then_inc(E("act_exp"), 1)
            nc.scalar.activation(last_decay[:], last[:], ACT.Exp).then_inc(E("act_exp"), 1)
            nc.scalar.activation(last_decay_s[:], last_decay_s[:], ACT.Exp).then_inc(E("act_exp"), 1)
            nc.scalar.activation(wi[:], wi[:], ACT.Exp).then_inc(E("exps"), 1)

        @block.tensor
        def _(pe):
            pe.wait_ge(E("g_ready"), 1)
            pe.wait_ge(E("gm_ready"), 1)
            flat = g[:, 0:NT, :].rearrange("p i h -> p (i h)")
            nc.tensor.matmul(pg[:, 0:32], masks[:, 0, :], flat, start=True, stop=True)
            nc.tensor.matmul(pl[:, 0:32], ones[:], flat, start=True, stop=True)
            nc.tensor.matmul(ps_[0:T_S, 0:4], tri_s[:], g[0:T_S, NT, :], start=True, stop=True)
            nc.tensor.matmul(pls[0:T_S, 0:4], same_s[:], g[0:T_S, NT, :], start=True, stop=True)
            nc.tensor.matmul(pb[:, 0:32], ones[0:T_S, :], gm[:].rearrange("p b h -> p (b h)"), start=True, stop=True).then_inc(E("sums"), 1)


def delta_prompt(nc, g, big_g, last_decay, fac, qkv, masks, ident, mixed, state_out):
    with ExitStack() as ctx:
        s = Scope(nc, ctx, "dp")
        E = s.event
        H = H_DN
        two = range(2)
        scaled = {n: [s.sb(f"{n}{z}", [P, H, P]) for z in two] for n in "kn kb qn qe kbg kd vb".split()}
        turned = {n: [s.sb(f"{n}t{z}", [P, H, P]) for z in two] for n in "kn kb qn qe".split()}
        dec = [s.sb(f"dec{z}", [P, H, P]) for z in two]
        mt = [s.sb(f"mt{z}", [P, H, P]) for z in two]
        at = [s.sb(f"at{z}", [P, H, P]) for z in two]
        lt = [s.sb(f"lt{z}", [P, LEVELS, H, P]) for z in two]
        x = [s.sb(f"x{z}", [P, H, P]) for z in two]
        xt = [s.sb(f"xt{z}", [P, H, P]) for z in two]
        p1 = [s.sb(f"p1{z}", [P, H, P]) for z in two]
        nwt = [s.sb(f"nwt{z}", [P, H, P]) for z in two]
        u = s.sb("u", [P, H, P])
        one_h = s.sb("one_h", [P, H, P])
        state = [s.sb(f"state{z}", [P, H, P]) for z in two]
        bank = [s.ps(f"b{n}", [P, H, P]) for n in range(8)]
        block = ctx.enter_context(nc.Block())
        SOURCE = {"kn": (DN, "rk"), "kb": (DN, "rkb"), "qn": (0, "rq"), "qe": (0, "rqg"), "kbg": (DN, "rkbg"),
                  "kd": (DN, "rkd"), "vb": (2 * DN, "beta")}
        TURN = "kn kb qn qe".split()
        A, B, C = [0, 3], [1, 4], [2, 5]
        STEPS = LEVELS - 1

        @block.gpsimd
        def _(pool):
            nc.gpsimd.memset(state[0][:], 0.0).then_inc(E("state_zero"), 1)

            def pair(i2):
                for z in two:
                    i = 2 * i2 + z
                    pool.wait_ge(E("m_ready"), i + 1)
                    for n in range(LEVELS):
                        m = masks[:, 1 + n:2 + n, :].broadcast_to([P, H, P])
                        nc.gpsimd.tensor_tensor(lt[z][:, n], mt[z][:], m, ALU.mult).then_inc(E("level_ready"), 1)

            pair(0)
            with pool.Fori(1, NT // 2) as i2:
                pair(i2)

        @block.tensor
        def _(pe):
            def chunk(i, z):
                for n, name in enumerate(TURN):
                    pe.wait_ge(E("scaled"), 5 * i + n + 1)
                    if z == 1:
                        pe.wait_ge(E("turned"), 4 * i - 4 + n + 1)
                    for h in range(H):
                        last = nc.tensor.transpose(bank[n][:, h], scaled[name][z][:, h], ident[:])
                    last.then_inc(E("turn_mm"), 1)
                pe.wait_ge(E("scaled"), 5 * i + 5)
                at_least(pe, E("held") if z else E("state_done"), i if z else 4 * i)
                for h in range(H):
                    last = nc.tensor.matmul(bank[4][:, h], dec[z][:, h], masks[:, 0, :], start=True, stop=True)
                last.then_inc(E("g_mm"), 1)
                pe.wait_ge(E("turned"), 4 * i + 4)
                at_least(pe, E("m_ready") if z else E("o_out"), i)
                for h in range(H):
                    last = nc.tensor.matmul(bank[5][:, h], turned["kn"][z][:, h], turned["kb"][z][:, h], start=True, stop=True)
                last.then_inc(E("gram_mm"), 1)
                at_least(pe, E("at_ready"), i)
                for h in range(H):
                    last = nc.tensor.matmul(bank[6][:, h], turned["kn"][z][:, h], turned["qn"][z][:, h], start=True, stop=True)
                last.then_inc(E("qk_mm"), 1)

            def invert(i2):
                for z in two:
                    pe.wait_ge(E("xt0"), 2 * i2 + z + 1)
                    for h in range(H):
                        last = nc.tensor.transpose(bank[A[z]][:, h], xt[z][:, h], ident[:])
                    last.then_inc(E("x0_mm"), 1)
                for n in range(STEPS):
                    count = 2 * (STEPS * i2 + n)
                    for z in two:
                        if n == 0:
                            pe.wait_ge(E("x0"), 2 * i2 + z + 1)
                        else:
                            pe.wait_ge(E("joined"), count + z - 1)
                        pe.wait_ge(E("level_ready"), LEVELS * (2 * i2 + z) + n + 2)
                        for h in range(H):
                            last = nc.tensor.matmul(bank[A[z]][:, h], lt[z][:, n + 1, h], x[z][:, h], start=True, stop=True)
                        last.then_inc(E("p1_mm"), 1)
                    for z in two:
                        pe.wait_ge(E("p1"), count + z + 1)
                        for h in range(H):
                            last = nc.tensor.matmul(bank[C[z]][:, h], p1[z][:, h], xt[z][:, h], start=True, stop=True)
                        if n < STEPS - 1:
                            for h in range(H):
                                last = nc.tensor.matmul(bank[B[z]][:, h], xt[z][:, h], p1[z][:, h], start=True, stop=True)
                        last.then_inc(E("join_mm"), 1)

            def advance(i, z, i2):
                pe.wait_ge(E("joined"), 2 * STEPS * (i2 + 1))
                pe.wait_ge(E("rest_scaled"), 3 * i + 3)
                pe.wait_ge(E("at_ready"), 2 * i2 + 2)
                for h in range(H):
                    last = nc.tensor.matmul(bank[6][:, h], scaled["kbg"][z][:, h], xt[z][:, h], start=True, stop=True)
                last.then_inc(E("w_mm"), 1)
                pe.wait_ge(E("nwt"), i + 1)
                at_least(pe, E("state_done"), 4 * i)
                if isinstance(i, int) and i == 0:
                    pe.wait_ge(E("state_zero"), 1)
                for h in range(H):
                    nc.tensor.matmul(bank[7][:, h], xt[z][:, h], scaled["vb"][z][:, h], start=True, stop=False)
                    last = nc.tensor.matmul(bank[7][:, h], nwt[z][:, h], state[z][:, h], start=False, stop=True)
                last.then_inc(E("u_mm"), 1)
                pe.wait_ge(E("u"), i + 1)
                for h in range(H):
                    last = nc.tensor.matmul(bank[4][:, h], scaled["kd"][z][:, h], u[:, h], start=True, stop=True)
                last.then_inc(E("ds_mm"), 1)
                at_least(pe, E("o_out"), i)
                for h in range(H):
                    nc.tensor.matmul(bank[5][:, h], turned["qe"][z][:, h], state[z][:, h], start=True, stop=False)
                    last = nc.tensor.matmul(bank[5][:, h], at[z][:, h], u[:, h], start=False, stop=True)
                last.then_inc(E("o_mm"), 1)

            def pair(i2):
                for z in two:
                    chunk(2 * i2 + z, z)
                invert(i2)
                for z in two:
                    advance(2 * i2 + z, z, i2)

            pair(0)
            with pe.Fori(1, NT // 2) as i2:
                pair(i2)

        @block.scalar
        def _(act):
            nc.scalar.preload_act_table_set("natural_log_exp_and_others")

            def pair(i2):
                for z in two:
                    i = 2 * i2 + z
                    for n, name in enumerate(TURN):
                        act.wait_ge(E("turn_mm"), 4 * i + n + 1)
                        nc.scalar.activation(turned[name][z][:], bank[n][:], ACT.Copy).then_inc(E("turned"), 1)
                    act.wait_ge(E("held"), i + 1)
                    nc.scalar.activation(dec[z][:], dec[z][:], ACT.Exp).then_inc(E("dec_exp"), 1)
                for z in two:
                    act.wait_ge(E("x0_mm"), 2 * i2 + z + 1)
                    nc.scalar.activation(x[z][:], bank[A[z]][:], ACT.Copy).then_inc(E("x0"), 1)
                for n in range(STEPS):
                    for z in two:
                        act.wait_ge(E("p1_mm"), 2 * (STEPS * i2 + n) + z + 1)
                        nc.scalar.activation(p1[z][:], bank[A[z]][:], ACT.Copy).then_inc(E("p1"), 1)
                for z in two:
                    i = 2 * i2 + z
                    act.wait_ge(E("w_mm"), i + 1)
                    nc.scalar.activation(nwt[z][:], bank[6][:], ACT.Copy, scale=-1.0).then_inc(E("nwt"), 1)
                    act.wait_ge(E("u_mm"), i + 1)
                    at_least(act, E("o_mm"), i)
                    nc.scalar.activation(u[:], bank[7][:], ACT.Copy).then_inc(E("u"), 1)

            pair(0)
            with act.Fori(1, NT // 2) as i2:
                pair(i2)

        @block.vector
        def _(dve):
            def rows(i, name):
                at, factor = SOURCE[name]
                r = qkv[:, bass.ds(i, 1), at:at + DN].rearrange("p o (h c) -> p (o h) c", c=P)
                return r, fac[factor][:, bass.ds(i, 1), :].rearrange("p o h -> p h o").broadcast_to([P, H, P])

            def pair(i2):
                for z in two:
                    i = 2 * i2 + z
                    for name in TURN:
                        nc.vector.tensor_tensor(scaled[name][z][:], *rows(i, name), ALU.mult).then_inc(E("scaled"), 1)
                    nc.vector.tensor_tensor(dec[z][:], one_h[:], g[:, bass.ds(i, 1), :].rearrange("p o h -> p h o").broadcast_to([P, H, P]),
                                            ALU.mult).then_inc(E("scaled"), 1)
                for z in two:
                    i = 2 * i2 + z
                    dve.wait_ge(E("g_mm"), i + 1)
                    for h in range(H):
                        last = nc.vector.tensor_scalar(dec[z][:, h], bank[4][:, h], big_g[:, bass.ds(i, 1), h], 0.0,
                                                       ALU.subtract, ALU.min)
                    last.then_inc(E("held"), 1)
                    dve.wait_ge(E("dec_exp"), i + 1)
                    nc.vector.tensor_tensor(dec[z][:], dec[z][:], masks[:, 0:1, :].broadcast_to([P, H, P]), ALU.mult).then_inc(E("dec_masked"), 1)
                    dve.wait_ge(E("dec_masked"), i + 1)
                    dve.wait_ge(E("gram_mm"), i + 1)
                    nc.vector.tensor_tensor(mt[z][:], dec[z][:], bank[5][:], ALU.mult).then_inc(E("m_ready"), 1)
                    dve.wait_ge(E("qk_mm"), i + 1)
                    nc.vector.tensor_tensor(at[z][:], dec[z][:], bank[6][:], ALU.mult).then_inc(E("at_ready"), 1)
                for z in two:
                    dve.wait_ge(E("level_ready"), LEVELS * (2 * i2 + z) + 1)
                    nc.vector.tensor_tensor(xt[z][:], ident[:].rearrange("p (o c) -> p o c", o=1).broadcast_to([P, H, P]), lt[z][:, 0],
                                            ALU.subtract).then_inc(E("xt0"), 1)
                for z in two:
                    for name in ("kbg", "kd", "vb"):
                        nc.vector.tensor_tensor(scaled[name][z][:], *rows(2 * i2 + z, name), ALU.mult).then_inc(E("rest_scaled"), 1)
                for n in range(STEPS):
                    for z in two:
                        dve.wait_ge(E("join_mm"), 2 * (STEPS * i2 + n) + z + 1)
                        if n < STEPS - 1:
                            nc.vector.tensor_tensor(x[z][:], x[z][:], bank[B[z]][:], ALU.subtract)
                        nc.vector.tensor_tensor(xt[z][:], xt[z][:], bank[C[z]][:], ALU.subtract).then_inc(E("joined"), 1)
                for z in two:
                    i = 2 * i2 + z
                    dve.wait_ge(E("ds_mm"), i + 1)
                    at_least(dve, E("o_mm"), i)
                    for h in range(H):
                        nc.vector.scalar_tensor_tensor(state[1 - z][:, h], state[z][:, h], last_decay[:, bass.ds(i, 1), h],
                                                       bank[4][:, h], ALU.mult, ALU.add).then_inc(E("state_done"), 1)
                    dve.wait_ge(E("o_mm"), i + 1)
                    nc.vector.tensor_scalar(mixed[:, bass.ds(i, 1), 0:DN], bank[5][:].rearrange("p h c -> p (h c)"), 1.0, None, ALU.mult).then_inc(E("o_out"), 1)

            nc.vector.memset(one_h[:], 1.0).then_inc(E("ones_made"), 1)
            dve.wait_ge(E("ones_made"), 1)
            pair(0)
            with dve.Fori(1, NT // 2) as i2:
                pair(i2)

        @block.sync
        def _(sp):
            sp.wait_ge(E("state_done"), 4 * NT)
            sp.dma_start(state_out.rearrange("h k v -> k h v"), state[0][:]).then_inc(E("stored"), 16)
            sp.wait_ge(E("stored"), 16)


def delta_sample(nc, g, big_g, last_decay_s, fac, qkv, tri_s, level_s, spread_s, ident, states, mixed, states_out):
    with ExitStack() as ctx:
        s = Scope(nc, ctx, "ds")
        E = s.event
        H, R = H_DN, T_S
        scaled = {n: s.sb(n, [R, H, P]) for n in "kn kb qn qe kbg kd vb".split()}
        turned = {n: s.sb(f"{n}t", [P, H, R]) for n in "kn kb qn qe".split()}
        one_r = s.sb("one_r", [R, H, R])
        gb, dec, mt, at, lt0, lt1, x, xt, p1 = (s.sb(n, [R, H, R]) for n in "gb dec mt at lt0 lt1 x xt p1".split())
        nwt, u_t, o_t = (s.sb(n, [P, H, R]) for n in "nwt u_t o_t".split())
        u = s.sb("u", [R, H, P])
        um = s.sb("um", [R, 2, N_B, P])
        old, new = s.sb("old", [P, N_B, H, P]), s.sb("new", [P, N_B, H, P])
        bank = [s.ps(f"b{n}", [P, 512]) for n in range(4)]
        ds = [s.ps(f"d{n}", [P, N_B, P]) for n in range(2)]
        block = ctx.enter_context(nc.Block())
        SOURCE = {"kn": (DN, "rk"), "kb": (DN, "rkb"), "qn": (0, "rq"), "qe": (0, "rqg"), "kbg": (DN, "rkbg"),
                  "kd": (DN, "rkd"), "vb": (2 * DN, "beta")}
        TURN = "kn kb qn qe".split()

        def cols(b, w=R):
            return bank[b][:, 0:H * w].rearrange("p (h c) -> p h c", c=w)

        def rows(b, w=R):
            return bank[b][0:R, 0:H * w].rearrange("p (h c) -> p h c", c=w)

        def by_head(m):
            return m.rearrange("p (o c) -> p o c", o=1).broadcast_to([R, H, R])

        @block.sync
        def _(sp):
            sp.dma_start(old[:], states.rearrange("b h k v -> k b h v")).then_inc(E("states_in"), 16)
            sp.wait_ge(E("new_ready"), H)
            sp.dma_start(states_out.rearrange("b h k v -> k b h v"), new[:]).then_inc(E("states_out"), 16)
            sp.wait_ge(E("states_out"), 16)

        @block.tensor
        def _(pe):
            for n, name in enumerate(TURN):
                pe.wait_ge(E("scaled"), n + 1)
                for h in range(H):
                    last = nc.tensor.transpose(cols(n)[:, h], scaled[name][:, h], ident[0:R, 0:R])
                last.then_inc(E("turn_mm"), 1)
            pe.wait_ge(E("scaled"), 5)
            pe.wait_ge(E("turned"), 4)
            for h in range(H):
                last = nc.tensor.matmul(rows(0)[:, h], gb[:, h], tri_s[:], start=True, stop=True)
            last.then_inc(E("g_mm"), 1)
            for h in range(H):
                last = nc.tensor.matmul(rows(1)[:, h], turned["kn"][:, h], turned["kb"][:, h], start=True, stop=True)
            last.then_inc(E("gram_mm"), 1)
            for h in range(H):
                last = nc.tensor.matmul(rows(2)[:, h], turned["kn"][:, h], turned["qn"][:, h], start=True, stop=True)
            last.then_inc(E("qk_mm"), 1)
            pe.wait_ge(E("xt0"), 1)
            for h in range(H):
                last = nc.tensor.transpose(rows(3)[:, h], xt[:, h], ident[0:R, 0:R])
            last.then_inc(E("x0_mm"), 1)
            pe.wait_ge(E("x0"), 1)
            for h in range(H):
                last = nc.tensor.matmul(rows(0)[:, h], lt1[:, h], x[:, h], start=True, stop=True)
            last.then_inc(E("p1_mm"), 1)
            pe.wait_ge(E("p1"), 1)
            for h in range(H):
                last = nc.tensor.matmul(rows(1)[:, h], p1[:, h], xt[:, h], start=True, stop=True)
            last.then_inc(E("join_mm"), 1)
            pe.wait_ge(E("joined"), 1)
            for h in range(H):
                last = nc.tensor.matmul(cols(2)[:, h], scaled["kbg"][:, h], xt[:, h], start=True, stop=True)
            last.then_inc(E("w_mm"), 1)
            pe.wait_ge(E("nwt"), 1)
            pe.wait_ge(E("states_in"), 16)
            for h in range(H):
                nc.tensor.matmul(cols(3)[:, h], scaled["vb"][:, h], xt[:, h], start=True, stop=False)
                for b in range(N_B):
                    c = slice(b * L_S, (b + 1) * L_S)
                    last = nc.tensor.matmul(cols(3)[:, h, c], old[:, b, h], nwt[:, h, c], start=False, stop=(b == N_B - 1))
            last.then_inc(E("u_mm"), 1)
            pe.wait_ge(E("u_t"), 1)
            for h in range(H):
                last = nc.tensor.transpose(rows(0, P)[:, h], u_t[:, h], ident[:])
            last.then_inc(E("u_turn"), 1)
            pe.wait_ge(E("u"), 1)
            for h in range(H):
                nc.tensor.matmul(cols(1)[:, h], u[:, h], at[:, h], start=True, stop=False)
                for b in range(N_B):
                    c = slice(b * L_S, (b + 1) * L_S)
                    last = nc.tensor.matmul(cols(1)[:, h, c], old[:, b, h], turned["qe"][:, h, c], start=False, stop=(b == N_B - 1))
            last.then_inc(E("o_mm"), 1)
            for h in range(H):
                pe.wait_ge(E("um"), h + 1)
                at_least(pe, E("new_ready"), h - 1)
                for half in range(2):
                    last = nc.tensor.matmul(ds[h % 2][:, 4 * half:4 * half + 4], scaled["kd"][:, h], um[:, h % 2, 4 * half:4 * half + 4],
                                            start=True, stop=True)
                last.then_inc(E("ds_mm"), 1)
            pe.wait_ge(E("o_t"), 1)
            for h in range(H):
                last = nc.tensor.transpose(rows(2, P)[:, h], o_t[:, h], ident[:])
            last.then_inc(E("o_turn"), 1)

        @block.scalar
        def _(act):
            for n, name in enumerate(TURN):
                act.wait_ge(E("turn_mm"), n + 1)
                nc.scalar.activation(turned[name][:], cols(n), ACT.Copy).then_inc(E("turned"), 1)
            act.wait_ge(E("held"), 1)
            nc.scalar.activation(dec[:], dec[:], ACT.Exp).then_inc(E("dec_exp"), 1)
            act.wait_ge(E("x0_mm"), 1)
            nc.scalar.activation(x[:], rows(3), ACT.Copy).then_inc(E("x0"), 1)
            act.wait_ge(E("p1_mm"), 1)
            nc.scalar.activation(p1[:], rows(0), ACT.Copy).then_inc(E("p1"), 1)
            act.wait_ge(E("w_mm"), 1)
            nc.scalar.activation(nwt[:], cols(2), ACT.Copy, scale=-1.0).then_inc(E("nwt"), 1)
            act.wait_ge(E("u_mm"), 1)
            nc.scalar.activation(u_t[:], cols(3), ACT.Copy).then_inc(E("u_t"), 1)
            act.wait_ge(E("u_turn"), 1)
            nc.scalar.activation(u[:], rows(0, P), ACT.Copy).then_inc(E("u"), 1)
            act.wait_ge(E("o_mm"), 1)
            nc.scalar.activation(o_t[:], cols(1), ACT.Copy).then_inc(E("o_t"), 1)
            act.wait_ge(E("o_turn"), 1)
            nc.scalar.activation(mixed[0:R, NT, 0:DN], bank[2][0:R, :], ACT.Copy).then_inc(E("o_out"), 1)

        @block.vector
        def _(dve):
            def source(name):
                at0, factor = SOURCE[name]
                r = qkv[0:R, NT, at0:at0 + DN].rearrange("p (h c) -> p h c", c=P)
                return r, fac[factor][0:R, NT:NT + 1, :].rearrange("p o h -> p h o").broadcast_to([R, H, P])

            nc.vector.memset(one_r[:], 1.0).then_inc(E("ones"), 1)
            for name in TURN:
                nc.vector.tensor_tensor(scaled[name][:], *source(name), ALU.mult).then_inc(E("scaled"), 1)
            dve.wait_ge(E("ones"), 1)
            nc.vector.tensor_tensor(gb[:], one_r[:], g[0:R, NT:NT + 1, :].rearrange("p o h -> p h o").broadcast_to([R, H, R]),
                                    ALU.mult).then_inc(E("scaled"), 1)
            for name in ("kbg", "kd", "vb"):
                nc.vector.tensor_tensor(scaled[name][:], *source(name), ALU.mult)
            dve.wait_ge(E("g_mm"), 1)
            for h in range(H):
                last = nc.vector.tensor_scalar(dec[:, h], rows(0)[:, h], big_g[0:R, NT, h:h + 1], 0.0, ALU.subtract, ALU.min)
            last.then_inc(E("held"), 1)
            dve.wait_ge(E("dec_exp"), 1)
            nc.vector.tensor_tensor(dec[:], dec[:], by_head(tri_s[:]), ALU.mult).then_inc(E("dec_masked"), 1)
            dve.wait_ge(E("dec_masked"), 1)
            dve.wait_ge(E("gram_mm"), 1)
            nc.vector.tensor_tensor(mt[:], dec[:], rows(1), ALU.mult).then_inc(E("mt"), 1)
            dve.wait_ge(E("qk_mm"), 1)
            nc.vector.tensor_tensor(at[:], dec[:], rows(2), ALU.mult).then_inc(E("at"), 1)
            dve.wait_ge(E("mt"), 1)
            nc.vector.tensor_tensor(lt0[:], mt[:], by_head(level_s[:, 0]), ALU.mult).then_inc(E("lt"), 1)
            nc.vector.tensor_tensor(lt1[:], mt[:], by_head(level_s[:, 1]), ALU.mult).then_inc(E("lt"), 1)
            dve.wait_ge(E("lt"), 2)
            nc.vector.tensor_tensor(xt[:], by_head(ident[0:R, 0:R]), lt0[:], ALU.subtract).then_inc(E("xt0"), 1)
            dve.wait_ge(E("join_mm"), 1)
            nc.vector.tensor_tensor(xt[:], xt[:], rows(1), ALU.subtract).then_inc(E("joined"), 1)
            dve.wait_ge(E("u"), 1)
            dve.wait_ge(E("states_in"), 16)
            for h in range(H):
                at_least(dve, E("ds_mm"), h - 1)
                nc.vector.tensor_tensor(um[:, h % 2], u[:, h:h + 1].broadcast_to([R, N_B, P]),
                                        spread_s[:].rearrange("p (b o) -> p b o", o=1).broadcast_to([R, N_B, P]), ALU.mult).then_inc(E("um"), 1)
                nc.vector.tensor_tensor(new[:, :, h], old[:, :, h], last_decay_s[:, :, h:h + 1].broadcast_to([P, N_B, P]), ALU.mult).then_inc(E("faded"), 1)
                dve.wait_ge(E("faded"), h + 1)
                dve.wait_ge(E("ds_mm"), h + 1)
                nc.vector.tensor_tensor(new[:, :, h], new[:, :, h], ds[h % 2][:], ALU.add).then_inc(E("new_ready"), 1)


def sample_attention(nc, qt, kt, v_rows, cache_k, cache_v, page_table, bias_row, spread_s, tri_s, ident, mixed):
    PAGES, G = 16, N_B // 4
    KEYS = PAGES * P + T_S
    NPHYS = cache_k.shape[0]
    with ExitStack() as ctx:
        s = Scope(nc, ctx, "sa")
        E = s.event
        table = s.sb("table", [1, N_B * PAGES], I32)
        k_page = s.sb("k_page", [P, 2, 4, SB])
        v_page = s.sb("v_page", [P, 2, 4, SB])
        v_new = s.sb("v_new", [T_S, SB])
        k_turned = s.sb("k_turned", [P, 4, 4, P])
        qb = s.sb("qb", [P, 4, 4, 8])
        zt = s.sb("zt", [P, P])
        bias = s.sb("bias", [P, H_SB])
        row_bias = s.sb("row_bias", [P, 1])
        bias_pick = s.sb("bias_pick", [P, H_SB])
        mask = s.sb("mask", [P, T_S])
        mask_t = s.sb("mask_t", [T_S, P])
        ex = s.sb("ex", [P, KEYS])
        run = s.sb("run", [P, KEYS])
        zeros = s.sb("zeros", [P, KEYS])
        wt = s.sb("wt", [P, P])
        oacc = s.sb("oacc", [P, P])
        o_t = s.sb("o_t", [P, 4, T_S])
        pk = [s.ps(f"pk{n}", [P, 4, P]) for n in range(2)]
        pz, pt, pw, pv, pm = (s.ps(n, [P, 512]) for n in "pz pt pw pv pm".split())
        block = ctx.enter_context(nc.Block())
        ROUNDS = PAGES + 1
        w_s = [s.sb(f"w_s{n}", [P, P]) for n in range(2)]

        @block.sync
        def _(sp):
            sp.dma_start(table[:], page_table.rearrange("b n -> (b n)").rearrange("(o n) -> o n", o=1)).then_inc(E("table_in"), 16)
            sp.dma_start(bias_pick[0:H_SB, 0:1], bias_row.rearrange("(h o) -> h o", o=1)).then_inc(E("small_in"), 16)
            sp.dma_start(v_new[:], v_rows[T_P:T, :]).then_inc(E("small_in"), 16)
            sp.wait_ge(E("table_in"), 16)

            def load(buffer, cache, gi, p, par, arrived, used):
                sem, per_round, per_group = used
                at_least(sp, sem, per_round * (per_group * gi + p - 1))
                for b in range(4):
                    page = sp.value_load(table[0:1, bass.ds((4 * gi + b) * PAGES + p, 1)], min_val=0, max_val=NPHYS - 1)
                    sp.dma_start(buffer[:, par, b:b + 1, :], cache[bass.ds(page, 1)].rearrange("g p n -> p g n")).then_inc(arrived[par], 16)

            def stream(buffer, cache, gi, arrived, used):
                for p in range(2):
                    load(buffer, cache, gi, p, p, arrived, used)
                with sp.Fori(1, PAGES // 2) as p2:
                    for par in range(2):
                        load(buffer, cache, gi, 2 * p2 + par, par, arrived, used)

            k_in, v_in = [E("k_in0"), E("k_in1")], [E("v_in0"), E("v_in1")]
            for gi in range(G):
                stream(k_page, cache_k, gi, k_in, (E("k_turned1"), 2, PAGES))
                stream(v_page, cache_v, gi, v_in, (E("v_mm"), 1, ROUNDS))

        @block.gpsimd
        def _(pool):
            n = 0

            def made(step):
                nonlocal n
                n += 1
                step.then_inc(E("made"), 1)
                pool.wait_ge(E("made"), n)

            made(nc.gpsimd.memset(zeros[:], 0.0))
            made(nc.gpsimd.memset(qb[:], 0.0))
            pick = k_turned[0:H_SB, 0, 0, :]
            made(nc.gpsimd.memset(pick, 1.0))
            made(nc.gpsimd.affine_select(out=pick, in_=pick, compare_op=ALU.is_equal, fill=0.0, base=0,
                                         pattern=[[0, 4], [1, H_SB], [0, L_S]], channel_multiplier=-1))
            pool.sem_inc(E("pick"), 1)
            for gi in range(G):
                at_least(pool, E("mask_turned"), gi)
                made(nc.gpsimd.memset(mask_t[:], 1.0))
                for base, mult, q, op in ((-4 * L_S * gi, 1, 0, ALU.is_ge), (4 * L_S * gi, -1, 1, ALU.is_gt)):
                    sign = -1 if mult == 1 else 1
                    made(nc.gpsimd.affine_select(out=mask_t[:], in_=mask_t[:], compare_op=op, fill=0.0, base=base,
                                                 pattern=[[sign * L_S, 4], [0, H_SB], [q, L_S]], channel_multiplier=mult))
                pool.sem_inc(E("mask_made"), 1)

        @block.tensor
        def _(pe):
            pe.wait_ge(E("pick"), 1)
            pe.wait_ge(E("small_in"), 32)
            nc.tensor.matmul(pm[:, 0:1], k_turned[0:H_SB, 0, 0, :], bias_pick[0:H_SB, 0:1], start=True, stop=True).then_inc(E("bias_mm"), 1)

            def keys(gi, p, par):
                r = ROUNDS * gi + p
                pe.wait_ge(E(f"k_in{par}"), 64 * (PAGES // 2 * gi + (p - par) // 2) + 64)
                for b in range(4):
                    at_least(pe, E(f"k_copied{b % 2}"), 2 * (PAGES * gi + p) + b // 2)
                    for c in range(4):
                        last = nc.tensor.transpose(pk[b % 2][:, c], k_page[:, par, b, c * P:(c + 1) * P], ident[:])
                    last.then_inc(E(f"k_turned{b % 2}"), 1)
                pe.wait_ge(E("k_copied0"), 2 * (PAGES * gi + p) + 2)
                pe.wait_ge(E("k_copied1"), 2 * (PAGES * gi + p) + 2)
                at_least(pe, E("zt_copied"), r)
                for b in range(4):
                    for c in range(4):
                        last = nc.tensor.matmul(pz[:, b * 32 + c * 8:b * 32 + c * 8 + 8], k_turned[:, b, c], qb[:, c, b, :],
                                                start=True, stop=True)
                last.then_inc(E("z_mm"), 1)
                back(r, P)

            def back(r, n):
                pe.wait_ge(E("zt_copied"), r + 1)
                at_least(pe, E("z_out"), r)
                nc.tensor.transpose(pt[:, 0:n], zt[0:n, :], ident[0:n, 0:n]).then_inc(E("z_turned"), 1)

            def own_keys(gi):
                r = ROUNDS * gi + PAGES
                pe.wait_ge(E("zt_copied"), r)
                for c in range(4):
                    out = pz[0:T_S, 0:P].rearrange("p (b c x) -> p c b x", b=4, c=4)[:, c]
                    last = nc.tensor.matmul(out, kt[:, c, T_P:T], qb[:, c], start=True, stop=True)
                last.then_inc(E("z_mm"), 1)
                back(r, T_S)

            def weights(r, par):
                pe.wait_ge(E("w_ready"), r + 1)
                at_least(pe, E("wt_copied"), r)
                nc.tensor.transpose(pw[:, 0:P], w_s[par][:], ident[:]).then_inc(E("w_turned"), 1)
                pe.wait_ge(E("wt_copied"), r + 1)
                at_least(pe, E("added"), r)

            def values(gi, p, par):
                r = ROUNDS * gi + p
                weights(r, par)
                pe.wait_ge(E(f"v_in{par}"), 64 * (PAGES // 2 * gi + (p - par) // 2) + 64)
                for b in range(4):
                    for c in range(4):
                        cols = slice(b * 32 + c * 8, b * 32 + c * 8 + 8)
                        last = nc.tensor.matmul(pv[:, cols], v_page[:, par, b, c * P:(c + 1) * P], wt[:, cols], start=True, stop=True)
                last.then_inc(E("v_mm"), 1)

            def own_values(gi):
                r = ROUNDS * gi + PAGES
                pe.wait_ge(E("w_ready"), r + 1)
                pe.wait_ge(E("wt_copied"), r)
                nc.tensor.transpose(pw[0:T_S, 0:P], w_s[0][:, 0:T_S], ident[:]).then_inc(E("w_turned"), 1)
                pe.wait_ge(E("wt_copied"), r + 1)
                pe.wait_ge(E("added"), r)
                for c in range(4):
                    pick_c = lambda m: m.rearrange("p (b c x) -> p c b x", b=4, c=4)[:, c]
                    last = nc.tensor.matmul(pick_c(pv[:, 0:P]), v_new[:, c * P:(c + 1) * P], pick_c(wt[0:T_S, :]), start=True, stop=True)
                last.then_inc(E("v_mm"), 1)

            for gi in range(G):
                pe.wait_ge(E("mask_made"), gi + 1)
                pe.wait_ge(E("bias_out"), 1)
                at_least(pe, E("mask_out"), gi)
                nc.tensor.transpose(pm[:, 8:8 + T_S], mask_t[:], ident[0:T_S, 0:T_S]).then_inc(E("mask_turned"), 1)
                pe.wait_ge(E("q_ready"), 2 * gi + 2)
                keys(gi, 0, 0)
                keys(gi, 1, 1)
                with pe.Fori(1, PAGES // 2) as p2:
                    for par in range(2):
                        keys(gi, 2 * p2 + par, par)
                own_keys(gi)
                values(gi, 0, 0)
                values(gi, 1, 1)
                with pe.Fori(1, PAGES // 2) as p2:
                    for par in range(2):
                        values(gi, 2 * p2 + par, par)
                own_values(gi)
            pe.wait_ge(E("gathered"), 2 * G)
            for c in range(4):
                last = nc.tensor.transpose(pw[0:T_S, c * P:(c + 1) * P], o_t[:, c, :], ident[:])
            last.then_inc(E("o_turned"), 1)

        @block.scalar
        def _(act):
            nc.scalar.preload_act_table_set("natural_log_exp_and_others")
            act.wait_ge(E("bias_mm"), 1)
            nc.scalar.activation(row_bias[:], pm[:, 0:1], ACT.Copy).then_inc(E("bias_out"), 1)

            def keys(gi, p):
                n = PAGES * gi + p
                for m in range(2):
                    b = 2 * m
                    act.wait_ge(E("k_turned0"), 2 * n + m + 1)
                    at_least(act, E("z_mm"), ROUNDS * gi + p)
                    nc.scalar.activation(k_turned[:, b], pk[0][:], ACT.Copy).then_inc(E("k_copied0"), 1)
                zt_copy(ROUNDS * gi + p, P)

            def zt_copy(r, n):
                act.wait_ge(E("z_mm"), r + 1)
                at_least(act, E("z_turned"), r)
                nc.scalar.activation(zt[0:n, :], pz[0:n, 0:P], ACT.Copy).then_inc(E("zt_copied"), 1)

            def wt_copy(r, n):
                act.wait_ge(E("w_turned"), r + 1)
                at_least(act, E("v_mm"), r)
                nc.scalar.activation(wt[0:n, :], pw[0:n, 0:P], ACT.Copy).then_inc(E("wt_copied"), 1)

            for gi in range(G):
                keys(gi, 0)
                with act.Fori(1, PAGES) as p:
                    keys(gi, p)
                zt_copy(ROUNDS * gi + PAGES, T_S)
                act.wait_ge(E("z_out"), ROUNDS * (gi + 1))
                nc.scalar.activation(ex[:], ex[:], ACT.Exp).then_inc(E("exped"), 1)
                act.wait_ge(E("held"), gi + 1)
                nc.scalar.activation(run[:], ex[:], ACT.Ln, bias=1.0).then_inc(E("logged"), 1)
                act.wait_ge(E("summed"), gi + 1)
                nc.scalar.activation(run[:], run[:], ACT.Exp, scale=-1.0).then_inc(E("decayed"), 1)
                wt_copy(ROUNDS * gi, P)
                with act.Fori(1, PAGES) as p:
                    wt_copy(ROUNDS * gi + p, P)
                wt_copy(ROUNDS * gi + PAGES, T_S)
            act.wait_ge(E("o_turned"), 1)
            nc.scalar.activation(mixed[0:T_S, NT, DN:D], pw[0:T_S, :], ACT.Copy).then_inc(E("o_out"), 1)

        @block.vector
        def _(dve):
            def keys(gi, p):
                n = PAGES * gi + p
                for m in range(2):
                    dve.wait_ge(E("k_turned1"), 2 * n + m + 1)
                    at_least(dve, E("z_mm"), ROUNDS * gi + p)
                    nc.vector.tensor_copy(k_turned[:, 2 * m + 1], pk[1][:]).then_inc(E("k_copied1"), 1)
                dve.wait_ge(E("z_turned"), ROUNDS * gi + p + 1)
                nc.vector.tensor_scalar(ex[:, bass.ds(p * P, P)], pt[:, 0:P], row_bias[:], None, ALU.add).then_inc(E("z_out"), 1)

            def weigh(gi, p, par):
                r = ROUNDS * gi + p
                at_least(dve, E("w_turned"), r - 1)
                c = bass.ds(p * P, P)
                nc.vector.tensor_tensor(w_s[par][:], ex[:, c], run[:, c], ALU.mult).then_inc(E("w_ready"), 1)

            def add(r):
                dve.wait_ge(E("v_mm"), r + 1)
                nc.vector.tensor_tensor(oacc[:], oacc[:], pv[:, 0:P], ALU.add).then_inc(E("added"), 1)
                dve.wait_ge(E("added"), r + 1)

            for gi in range(G):
                first = ROUNDS * gi
                at_least(dve, E("z_mm"), first)
                if gi == 0:
                    dve.wait_ge(E("pick"), 1)
                    dve.wait_ge(E("bias_out"), 1)
                for e in range(2):
                    rows = slice(e * DH, (e + 1) * DH)
                    src = qt[rows, :, T_P + 16 * gi:T_P + 16 * gi + 16].rearrange("p c (b q) -> p c b q", q=L_S)
                    nc.vector.tensor_copy(qb[rows, :, :, 4 * e:4 * e + 4], src).then_inc(E("q_ready"), 1)
                dve.wait_ge(E("mask_turned"), gi + 1)
                nc.vector.tensor_copy(mask[:], pm[:, 8:8 + T_S]).then_inc(E("mask_out"), 1)
                nc.vector.memset(oacc[:], 0.0).then_inc(E("oacc_zero"), 1)
                keys(gi, 0)
                with dve.Fori(1, PAGES) as p:
                    keys(gi, p)
                dve.wait_ge(E("z_turned"), first + ROUNDS)
                nc.vector.tensor_scalar(ex[:, PAGES * P:KEYS], pt[:, 0:T_S], row_bias[:], None, ALU.add).then_inc(E("z_out"), 1)
                dve.wait_ge(E("exped"), gi + 1)
                nc.vector.tensor_scalar(ex[:, 0:PAGES * P], ex[:, 0:PAGES * P], BIG, None, ALU.min)
                dve.wait_ge(E("mask_out"), gi + 1)
                nc.vector.scalar_tensor_tensor(ex[:, PAGES * P:KEYS], ex[:, PAGES * P:KEYS], BIG, mask[:], ALU.min, ALU.mult).then_inc(E("held"), 1)
                dve.wait_ge(E("logged"), gi + 1)
                nc.vector.tensor_tensor_scan(run[:, ::-1], run[:, ::-1], zeros[:], 0.0, ALU.add, ALU.add).then_inc(E("summed"), 1)
                dve.wait_ge(E("decayed"), gi + 1)
                dve.wait_ge(E("oacc_zero"), gi + 1)
                weigh(gi, 0, 0)
                weigh(gi, 1, 1)
                add(first)
                with dve.Fori(1, PAGES // 2) as p2:
                    for par in range(2):
                        weigh(gi, 2 * p2 + par, par)
                        add(first + 2 * p2 + par - 1)
                at_least(dve, E("w_turned"), first + PAGES - 1)
                nc.vector.tensor_tensor(w_s[0][:, 0:T_S], ex[:, PAGES * P:KEYS], run[:, PAGES * P:KEYS], ALU.mult).then_inc(E("w_ready"), 1)
                add(first + PAGES - 1)
                add(first + PAGES)
                for e in range(2):
                    rows = slice(e * DH, (e + 1) * DH)
                    src = oacc[rows, :].rearrange("p (b c e q) -> p c b e q", b=4, c=4, e=2)[:, :, :, e, :]
                    dst = o_t[rows, :, 16 * gi:16 * gi + 16].rearrange("p c (b q) -> p c b q", q=L_S)
                    nc.vector.tensor_copy(dst, src).then_inc(E("gathered"), 1)
                dve.wait_ge(E("gathered"), 2 * gi + 2)


def finish_mix(nc, mixed, gate_nat, dn_gain_row, sb_gain_row):
    with ExitStack() as ctx:
        s = Scope(nc, ctx, "fm")
        E = s.event
        N = NT + 1
        gate = s.sb("gate", [P, N, DN])
        g_dn, g_sb = s.sb("g_dn", [P, P]), s.sb("g_sb", [P, DH])
        sq = s.sb("sq", [P, 2, D])
        stat = s.sb("stat", [P, N, H_DN + H_SB])
        block = ctx.enter_context(nc.Block())

        @block.sync
        def _(sp):
            sp.dma_start(gate[:, 0:NT, :], rows_view(gate_nat)).then_inc(E("loaded"), 16)
            sp.dma_start(gate[0:T_S, NT, :], gate_nat[T_P:T, :]).then_inc(E("loaded"), 16)
            sp.dma_start(g_dn[:], dn_gain_row.partition_broadcast(P)).then_inc(E("loaded"), 16)
            sp.dma_start(g_sb[:], sb_gain_row.partition_broadcast(P)).then_inc(E("loaded"), 16)

        @block.scalar
        def _(act):
            for i in range(N):
                rows = slice(0, P if i < NT else T_S)
                at_least(act, E("reduced"), 2 * (i - 1))
                nc.scalar.activation(sq[rows, i % 2], mixed[rows, i, :], ACT.Square).then_inc(E("squared"), 1)
            act.wait_ge(E("var"), 1)
            nc.scalar.activation(stat[:], stat[:], ACT.Sqrt).then_inc(E("root"), 1)

        @block.gpsimd
        def _(pool):
            pool.wait_ge(E("loaded"), 64)
            for i in range(N):
                rows = slice(0, P if i < NT else T_S)
                n = rows.stop
                v = gate[rows, i, :].rearrange("p (h c) -> p h c", c=P)
                nc.gpsimd.tensor_tensor(v, v, g_dn[rows, :].rearrange("p (o c) -> p o c", o=1).broadcast_to([n, H_DN, P]),
                                        ALU.mult).then_inc(E("gate_ready"), 1)

        @block.vector
        def _(dve):
            nc.vector.memset(stat[:], 1.0).then_inc(E("stat_set"), 1)
            dve.wait_ge(E("stat_set"), 1)
            for i in range(N):
                rows = slice(0, P if i < NT else T_S)
                dve.wait_ge(E("squared"), i + 1)
                for at, w, h0, h1 in ((0, P, 0, H_DN), (DN, DH, H_DN, H_DN + H_SB)):
                    nc.vector.tensor_reduce(stat[rows, i, h0:h1], sq[rows, i % 2, at:at + DN].rearrange("p (h c) -> p h c", c=w),
                                            AX.X, ALU.add).then_inc(E("reduced"), 1)
            dve.wait_ge(E("reduced"), 2 * N)
            nc.vector.tensor_scalar(stat[:, :, 0:H_DN], stat[:, :, 0:H_DN], 1.0 / P, EPS, ALU.mult, ALU.add)
            nc.vector.tensor_scalar(stat[:, :, H_DN:], stat[:, :, H_DN:], 1.0 / DH, EPS, ALU.mult, ALU.add).then_inc(E("var"), 1)
            dve.wait_ge(E("root"), 1)
            nc.vector.reciprocal(stat[:], stat[:]).then_inc(E("rstd"), 1)
            dve.wait_ge(E("rstd"), 1)
            for i in range(N):
                rows = slice(0, P if i < NT else T_S)
                n = rows.stop
                a = mixed[rows, i, 0:DN].rearrange("p (h c) -> p h c", c=P)
                b = mixed[rows, i, DN:D].rearrange("p (h c) -> p h c", c=DH)
                r = stat[rows, i, :].rearrange("p (h o) -> p h o", o=1)
                nc.vector.tensor_tensor(a, a, r[:, 0:H_DN].broadcast_to([n, H_DN, P]), ALU.mult)
                nc.vector.tensor_tensor(b, b, r[:, H_DN:].broadcast_to([n, H_SB, DH]), ALU.mult).then_inc(E("scaled"), 1)
                dve.wait_ge(E("scaled"), i + 1)
                dve.wait_ge(E("gate_ready"), i + 1)
                nc.vector.tensor_tensor(mixed[rows, i, 0:DN], mixed[rows, i, 0:DN], gate[rows, i, :], ALU.mult)
                nc.vector.tensor_tensor(b, b, g_sb[rows, :].rearrange("p (o c) -> p o c", o=1).broadcast_to([n, H_SB, DH]), ALU.mult)


def mix_out(nc, mixed, w_o, y, ident):
    with ExitStack() as ctx:
        s = Scope(nc, ctx, "mo")
        E = s.event
        N = NT + 1
        w_raw = s.sb("w_raw", [P, KC, D])
        w_hi, w_lo = s.sb("w_hi", [P, KC, D], F32R), s.sb("w_lo", [P, KC, D], F32R)
        m_hi, m_lo = s.sb("m_hi", [P, 2, KC, P], F32R), s.sb("m_lo", [P, 2, KC, P], F32R)
        pt = [s.ps(f"pt{n}", [P, KC, P]) for n in range(2)]
        po = [s.ps(f"po{n}", [P, 512]) for n in range(4)]
        block = ctx.enter_context(nc.Block())

        def span(i):
            return slice(0, P) if i < NT else slice(P - T_S, P)

        @block.sync
        def _(sp):
            view = w_o.rearrange("(k p) n -> p k n", p=P)
            for k in range(KC):
                sp.dma_start(w_raw[:, k, :], view[:, k, :]).then_inc(E(f"w_in{k}"), 16)

        @block.tensor
        def _(pe):
            def turn(i):
                rows = P if i < NT else T_S
                at_least(pe, E("m_lo"), i - 1)
                for k in range(KC):
                    last = nc.tensor.transpose(pt[i % 2][:, k, 0:rows], mixed[0:rows, i, k * P:(k + 1) * P], ident[0:rows, 0:rows])
                last.then_inc(E("turned"), 1)

            turn(0)
            turn(1)
            for i in range(N):
                pe.wait_ge(E("m_lo"), i + 1)
                for half in range(2):
                    n = 2 * i + half
                    at_least(pe, E("y_out"), n - 3)
                    for k in range(KC):
                        if i == 0 and half == 0:
                            pe.wait_ge(E("w_lo"), k + 1)
                        cols = slice(half * 512, half * 512 + 512)
                        out = po[n % 4][:]
                        nc.tensor.matmul(out, m_hi[:, i % 2, k], w_hi[:, k, cols], start=(k == 0), stop=False)
                        nc.tensor.matmul(out, m_lo[:, i % 2, k], w_hi[:, k, cols], start=False, stop=False)
                        last = nc.tensor.matmul(out, m_hi[:, i % 2, k], w_lo[:, k, cols], start=False, stop=(k == KC - 1))
                    last.then_inc(E("y_mm"), 1)
                if i + 2 < N:
                    turn(i + 2)

        @block.scalar
        def _(act):
            def hi(i):
                act.wait_ge(E("turned"), i + 1)
                at_least(act, E("y_mm"), 2 * (i - 1))
                rows = P if i < NT else T_S
                if i == NT:
                    act.wait_ge(E("cleared"), 2)
                nc.scalar.activation(m_hi[:, i % 2, :, span(i)], pt[i % 2][:, :, 0:rows], ACT.Copy).then_inc(E("m_hi"), 1)

            hi(0)
            hi(1)
            for k in range(KC):
                act.wait_ge(E(f"w_in{k}"), 16)
                nc.scalar.activation(w_hi[:, k, :], w_raw[:, k, :], ACT.Copy).then_inc(E("w_hi"), 1)
            for i in range(N):
                for half in range(2):
                    n = 2 * i + half
                    act.wait_ge(E("y_mm"), n + 1)
                    nc.scalar.activation(y[:, i, half * 512:half * 512 + 512], po[n % 4][:], ACT.Copy).then_inc(E("y_out"), 1)
                if i + 2 < N:
                    hi(i + 2)

        @block.vector
        def _(dve):
            def lo(i):
                dve.wait_ge(E("m_hi"), i + 1)
                rows = P if i < NT else T_S
                nc.vector.tensor_tensor(m_lo[:, i % 2, :, span(i)], pt[i % 2][:, :, 0:rows],
                                        m_hi[:, i % 2, :, span(i)].bitcast(F32), ALU.subtract).then_inc(E("m_lo"), 1)

            lo(0)
            lo(1)
            for k in range(KC):
                dve.wait_ge(E("w_hi"), k + 1)
                nc.vector.tensor_tensor(w_lo[:, k, :], w_raw[:, k, :], w_hi[:, k, :].bitcast(F32), ALU.subtract).then_inc(E("w_lo"), 1)
            for i in range(2, N):
                if i == NT:
                    dve.wait_ge(E("y_mm"), 2 * (NT - 1))
                    for m in (m_hi, m_lo):
                        nc.vector.memset(m[:, i % 2, :, 0:P - T_S].bitcast(F32), 0.0).then_inc(E("cleared"), 1)
                    dve.wait_ge(E("cleared"), 2)
                lo(i)


def hymba_step(nc, x, cache_k, cache_v, page_table, state_delta, state_conv, norms, ffn1_gu, ffn1_d, w_in, conv_w,
               a_log, dt_bias, dn_norm, sb_bias, sb_norm, w_o, ffn2_gu, ffn2_d, y_out, k_rows, v_rows, delta_p, delta_s, conv_rows):
    qkv_nat = nc.dram_tensor("qkv_rows", (T, QKV), F32, kind="Internal").ap()
    gate_nat = nc.dram_tensor("gate_rows", (T, DN), F32, kind="Internal").ap()
    h1 = nc.dram_tensor("h1", (T, D), F32, kind="Internal").ap()
    h2 = nc.dram_tensor("h2", (T, D), F32, kind="Internal").ap()
    with ExitStack() as ctx:
        whole = Scope(nc, ctx, "w")
        ident = whole.sb("ident", [P, P])
        make_ident(nc, ident)

        with ExitStack() as mix_ctx:
            m = Scope(nc, mix_ctx, "m")
            ab = m.sb("ab", [P, NT + 1, 8])
            with ExitStack() as c:
                s = Scope(nc, c, "u")
                uh, ul = s.sb("uh", [P, KC, T], F32R), s.sb("ul", [P, KC, T], F32R)
                with ExitStack() as c2:
                    y = Scope(nc, c2, "y1").sb("y", [P, NT + 1, D])
                    seam(nc, "n1", y, x, None, None, None, norms[0], uh, ul, ident)
                    ffn(nc, "f1", uh, ul, ffn1_gu, ffn1_d, y)
                    seam(nc, "n2", y, x, norms[1], 0.5, h1, norms[2], uh, ul, ident)
                with ExitStack() as c2:
                    t = Scope(nc, c2, "t")
                    qt, kt = t.sb("qt", [P, 4, T]), t.sb("kt", [P, 4, T])
                    projections(nc, uh, ul, w_in, conv_w, state_conv, qt, kt, ab, qkv_nat, gate_nat, k_rows, v_rows, conv_rows, ident)
                    qk_store = nc.dram_tensor("qk_store", (2, P, 4, T), F32, kind="Internal").ap()
                    move(nc, "qs", [(qk_store[0], qt[:]), (qk_store[1], kt[:])])
            mixed = m.sb("mixed", [P, NT + 1, D])
            with ExitStack() as c:
                s = Scope(nc, c, "sm")
                masks = s.sb("masks", [P, 1 + LEVELS, P])
                tri_s, same_s = s.sb("tri_s", [T_S, T_S]), s.sb("same_s", [T_S, T_S])
                level_s, spread_s = s.sb("level_s", [T_S, 2, T_S]), s.sb("spread_s", [T_S, N_B])
                ones = s.sb("ones", [P, P])
                delta_masks(nc, masks, tri_s, same_s, level_s, spread_s, ones)
                with ExitStack() as c2:
                    d = Scope(nc, c2, "d")
                    g, big_g, last_decay = (d.sb(n, [P, NT + 1, 4]) for n in ("g", "big_g", "last_decay"))
                    last_decay_s = d.sb("last_decay_s", [P, N_B, 4])
                    fac = {n: d.sb(n, [P, NT + 1, 4]) for n in FACTORS}
                    qkv = d.sb("qkv", [P, NT + 1, QKV])
                    delta_gates(nc, ab, qkv_nat, dt_bias, a_log, masks, tri_s, same_s, spread_s, ones, qkv, g, big_g,
                                last_decay, last_decay_s, fac)
                    delta_prompt(nc, g, big_g, last_decay, fac, qkv, masks, ident, mixed, delta_p)
                    delta_sample(nc, g, big_g, last_decay_s, fac, qkv, tri_s, level_s, spread_s, ident, state_delta, mixed, delta_s)
                with ExitStack() as c2:
                    t = Scope(nc, c2, "t2")
                    qt, kt = t.sb("qt", [P, 4, T]), t.sb("kt", [P, 4, T])
                    move(nc, "ql", [(qt[:], qk_store[0]), (kt[:], qk_store[1])])
                    prompt_attention(nc, qt, kt, v_rows, sb_bias, mixed[:, 0:NT, DN:D], ident)
                    sample_attention(nc, qt, kt, v_rows, cache_k, cache_v, page_table, sb_bias, spread_s, tri_s, ident, mixed)
            finish_mix(nc, mixed, gate_nat, dn_norm, sb_norm)
            with ExitStack() as c:
                y = Scope(nc, c, "y2").sb("y", [P, NT + 1, D])
                mix_out(nc, mixed, w_o, y, ident)
                y_store = nc.dram_tensor("y_store", (P, NT + 1, D), F32, kind="Internal").ap()
                move(nc, "ys", [(y_store, y[:])])
        uh, ul = whole.sb("uh", [P, KC, T], F32R), whole.sb("ul", [P, KC, T], F32R)
        y = whole.sb("y", [P, NT + 1, D])
        move(nc, "yl", [(y[:], y_store)])
        seam(nc, "n3", y, h1, norms[3], 1.0, h2, norms[4], uh, ul, ident)
        ffn(nc, "f2", uh, ul, ffn2_gu, ffn2_d, y)
        seam(nc, "n4", y, h2, norms[5], 0.5, y_out, None, None, None, ident)


def move(nc, tag, pairs):
    with ExitStack() as ctx:
        moved = Scope(nc, ctx, tag).sem("moved")
        block = ctx.enter_context(nc.Block())

        @block.sync
        def _(sp):
            for out, in_ in pairs:
                sp.dma_start(out, in_).then_inc(moved, 16)
            sp.wait_ge(moved, 16 * len(pairs))


def kernel(x_prompt, x_sample, cache_sb_k, cache_sb_v, page_table, state_delta, state_conv, norms, ffn1_w_gate_up,
           ffn1_w_down, w_in, conv_w, a_log, dt_bias, dn_out_norm, sb_logit_bias, sb_out_norm, w_o, ffn2_w_gate_up,
           ffn2_w_down):
    import numpy as np
    import concourse.bacc as bacc
    from concourse.bass_utils import run_bass_kernel_spmd

    n_phys, page = cache_sb_k.shape[:2]
    arrays = {
        "x": np.concatenate([np.asarray(x_prompt).reshape(T_P, D), np.asarray(x_sample).reshape(T_S, D)]),
        "cache_k": np.asarray(cache_sb_k).reshape(n_phys, page, SB),
        "cache_v": np.asarray(cache_sb_v).reshape(n_phys, page, SB),
        "page_table": np.asarray(page_table),
        "state_delta": np.asarray(state_delta)[0],
        "state_conv": np.asarray(state_conv).reshape(3 * N_B, QKV),
        "norms": np.asarray(norms)[0],
        "ffn1_gu": np.asarray(ffn1_w_gate_up)[0],
        "ffn1_d": np.asarray(ffn1_w_down)[0],
        "w_in": np.asarray(w_in)[0],
        "conv_w": np.asarray(conv_w)[0],
        "a_log": np.asarray(a_log)[0],
        "dt_bias": np.asarray(dt_bias)[0],
        "dn_norm": np.asarray(dn_out_norm)[0],
        "sb_bias": np.asarray(sb_logit_bias)[0],
        "sb_norm": np.asarray(sb_out_norm)[0],
        "w_o": np.asarray(w_o)[0],
        "ffn2_gu": np.asarray(ffn2_w_gate_up)[0],
        "ffn2_d": np.asarray(ffn2_w_down)[0],
    }
    outs = {
        "y_out": (T, D),
        "k_rows": (T, SB),
        "v_rows": (T, SB),
        "delta_p": (H_DN, P, P),
        "delta_s": (N_B, H_DN, P, P),
        "conv_rows": (TAIL, QKV),
    }
    nc = bacc.Bacc("TRN2", target_bir_lowering=False, num_devices=1)
    in_maps, args = {}, []
    for name, a in arrays.items():
        in_maps[f"in_{name}"] = np.ascontiguousarray(a)
        args.append(nc.dram_tensor(f"in_{name}", a.shape, mybir.dt.from_np(a.dtype), kind="ExternalInput").ap())
    for name, shape in outs.items():
        args.append(nc.dram_tensor(f"out_{name}", shape, F32, kind="ExternalOutput").ap())
    hymba_step(nc, *args)
    got = run_bass_kernel_spmd(nc, [in_maps], core_ids=[0]).results[0]
    y, k, v = (got[f"out_{n}"] for n in ("y_out", "k_rows", "v_rows"))
    conv = got["out_conv_rows"]
    heads = lambda r, b, n: r.reshape(b, n, 1, H_SB, DH)
    return (y[:T_P].reshape(1, T_P, D), y[T_P:].reshape(N_B, L_S, D),
            heads(k[:T_P], 1, T_P), heads(v[:T_P], 1, T_P), heads(k[T_P:], N_B, L_S), heads(v[T_P:], N_B, L_S),
            got["out_delta_p"].reshape(1, 1, H_DN, P, P), got["out_delta_s"].reshape(1, N_B, H_DN, P, P),
            conv[:3].reshape(1, 1, 3, QKV), conv[3:].reshape(1, N_B, 3, QKV))
```

```python
import concourse.bass as bass
from concourse import mybir
from concourse.alu_op_type import AluOpType as ALU
from contextlib import ExitStack

F32 = mybir.dt.float32
F32R = mybir.dt.float32r
I32 = mybir.dt.int32
ACT = mybir.ActivationFunctionType
AX = mybir.AxisListType

P = 128
D = 1024
T_P, N_B, L_S = 1024, 8, 4
T_S = N_B * L_S
T = T_P + T_S
KC = D // P
NT = T_P // P
TB = T // 3
F = 2816
GROUPS = F // (2 * P)
H_DN, H_SB, DH = 4, 8, 64
DN = H_DN * P
QKV = 3 * DN
SB = H_SB * DH
EPS = 1e-6
TILE0 = [P * i for i in range(NT)] + [T - P]


def rows_view(dram):
    return dram[0:T_P, :].rearrange("(i p) n -> p i n", p=P)


class Scope:

    def __init__(self, nc, ctx, tag):
        self.nc, self.ctx, self.tag = nc, ctx, tag
        self.events = {}
        self.handles = []
        ctx.callback(self.close)

    def close(self):
        if self.handles:
            self.nc.clear_and_free_semaphores(self.handles)
            self.nc.all_engine_barrier()

    def sb(self, name, shape, dt=F32, side=None):
        return self.ctx.enter_context(self.nc.sbuf_tensor(f"{self.tag}_{name}", shape, dt, side=side))

    def ps(self, name, shape):
        return self.ctx.enter_context(self.nc.psum_tensor(f"{self.tag}_{name}", shape, F32))

    def sem(self, name):
        self.handles.append(self.nc.alloc_semaphore(f"{self.tag}_{name}"))
        return self.handles[-1]

    def event(self, name):
        if name not in self.events:
            self.events[name] = self.sem(name)
        return self.events[name]

    def sems(self, names):
        return [self.sem(n) for n in names.split()]


def at_least(engine, sem, value):
    if not isinstance(value, int) or value > 0:
        engine.wait_ge(sem, value)


def seam(nc, tag, y, residual, post_gain, post_scale, h_out, pre_gain, uh, ul, ident):
    N = NT + 1
    with ExitStack() as ctx:
        s = Scope(nc, ctx, tag)
        E = s.event
        post, pre = post_gain is not None, pre_gain is not None
        g_post = s.sb("g_post", [P, D]) if post else None
        g_pre = s.sb("g_pre", [P, D]) if pre else None
        res = s.sb("res", [P, N, D]) if post else y
        squares = s.sb("squares", [P, D])
        stat = s.sb("stat", [P, 2, 3, N])
        eps = s.sb("eps", [P, 1])
        hn = s.sb("hn", [P, 2, D]) if pre else None
        pt = [s.ps(f"pt{n}", [P, KC, P]) for n in range(2)] if pre else None
        block = ctx.enter_context(nc.Block())

        def new_cols(i):
            return (slice(i * P, (i + 1) * P), slice(0, P)) if i < NT else (slice(T_P, T), slice(P - T_S, P))

        def on_pool(i):
            return pre or i % 2 == 0

        @block.sync
        def _(sp):
            def load(i):
                sp.dma_start(res[:, i, :], residual[TILE0[i]:TILE0[i] + P, :]).then_inc(E(f"res_in{i}"), 16)

            load(0)
            if post:
                sp.dma_start(g_post[:], post_gain.partition_broadcast(P)).then_inc(E("post_gain_in"), 16)
            if pre:
                sp.dma_start(g_pre[:], pre_gain.partition_broadcast(P)).then_inc(E("pre_gain_in"), 16)
            for i in range(1, N):
                load(i)
            if h_out is not None:
                for i in range(N):
                    rows = new_cols(i)[1]
                    if on_pool(i):
                        sp.wait_ge(E("h_ready"), sum(map(on_pool, range(i + 1))))
                    else:
                        sp.wait_ge(E("h_ready_dve"), i + 1 - sum(map(on_pool, range(i + 1))))
                    sp.dma_start(h_out[new_cols(i)[0], :], y[rows, i, :]).then_inc(E("stored"), 16)
                sp.wait_ge(E("stored"), 16 * N)

        @block.scalar
        def _(act):
            def root_mean_square(norm, i):
                nc.scalar.activation(squares[:], y[:, i, :], ACT.Square, accum_out=stat[:, norm, 0, i:i + 1]).then_inc(E(f"squared{norm}"), 1)
                act.wait_ge(E(f"squared{norm}"), i + 1)
                nc.scalar.activation(stat[:, norm, 1, i:i + 1], stat[:, norm, 0, i:i + 1], ACT.Sqrt, bias=eps[:],
                                     scale=1.0 / D).then_inc(E(f"root{norm}"), 1)

            act.wait_ge(E("eps_set"), 1)
            for k in range(N + 2):
                if post and k < N:
                    root_mean_square(0, k)
                if pre and 1 <= k <= N:
                    i = k - 1
                    act.wait_ge(E("h_ready") if post else E(f"res_in{i}"), i + 1 if post else 16)
                    root_mean_square(1, i)
                if pre and k >= 2:
                    i = k - 2
                    cols, rows = new_cols(i)
                    act.wait_ge(E("transposed"), i + 1)
                    nc.scalar.activation(uh[:, :, cols], pt[i % 2][:, :, rows], ACT.Copy).then_inc(E("hi_done"), 1)

        @block.vector
        def _(dve):
            def inverse(norm, i):
                dve.wait_ge(E(f"root{norm}"), i + 1)
                nc.vector.reciprocal(stat[:, norm, 2, i:i + 1], stat[:, norm, 1, i:i + 1]).then_inc(E(f"rstd{norm}"), 1)
                dve.wait_ge(E(f"rstd{norm}"), i + 1)
                return stat[:, norm, 2, i:i + 1]

            nc.vector.memset(eps[:], EPS).then_inc(E("eps_set"), 1)
            if post:
                dve.wait_ge(E("post_gain_in"), 16)
                nc.vector.tensor_scalar(g_post[:], g_post[:], post_scale, None, ALU.mult).then_inc(E("gain_scaled"), 1)
                dve.wait_ge(E("gain_scaled"), 1)
            for k in range(N + 2):
                if post and k < N:
                    nc.vector.scalar_tensor_tensor(y[:, k, :], y[:, k, :], inverse(0, k), g_post[:], ALU.mult, ALU.mult).then_inc(E("normed"), 1)
                    if not on_pool(k):
                        dve.wait_ge(E("normed"), k + 1)
                        dve.wait_ge(E(f"res_in{k}"), 16)
                        nc.vector.tensor_tensor(y[:, k, :], y[:, k, :], res[:, k, :], ALU.add).then_inc(E("h_ready_dve"), 1)
                if pre and 1 <= k <= N:
                    i = k - 1
                    rstd = inverse(1, i)
                    if i == 0:
                        dve.wait_ge(E("pre_gain_in"), 16)
                    at_least(dve, E("transposed"), i - 1)
                    nc.vector.scalar_tensor_tensor(hn[:, i % 2, :], y[:, i, :], rstd, g_pre[:], ALU.mult, ALU.mult).then_inc(E("hn_ready"), 1)
                if pre and k >= 2:
                    i = k - 2
                    cols, rows = new_cols(i)
                    dve.wait_ge(E("hi_done"), i + 1)
                    nc.vector.tensor_tensor(ul[:, :, cols], pt[i % 2][:, :, rows], uh[:, :, cols].bitcast(F32), ALU.subtract).then_inc(E("lo_done"), 1)

        @block.gpsimd
        def _(pool):
            if post:
                for i in filter(on_pool, range(N)):
                    pool.wait_ge(E(f"res_in{i}"), 16)
                    pool.wait_ge(E("normed"), i + 1)
                    nc.gpsimd.tensor_tensor(y[:, i, :], y[:, i, :], res[:, i, :], ALU.add).then_inc(E("h_ready"), 1)

        @block.tensor
        def _(pe):
            if pre:
                for i in range(N):
                    pe.wait_ge(E("hn_ready"), i + 1)
                    at_least(pe, E("lo_done"), i - 1)
                    for c in range(KC):
                        last = nc.tensor.transpose(pt[i % 2][:, c, :], hn[:, i % 2, c * P:(c + 1) * P], ident[:])
                    last.then_inc(E("transposed"), 1)


def ffn(nc, tag, uh, ul, w_gate_up, w_down, y):
    with ExitStack() as ctx:
        s = Scope(nc, ctx, tag)
        raw = {k: s.sb(f"raw_{k}", [P, 2 * D]) for k in "gud"}
        w_hi = {k: s.sb(f"hi_{k}", [P, 2, D], F32R) for k in "gud"}
        w_lo = {k: s.sb(f"lo_{k}", [P, 2, D], F32R) for k in "gud"}
        silu = s.sb("silu", [P, 3, TB])
        hid = s.sb("hid", [P, 3, TB])
        hid_hi = s.sb("hid_hi", [P, 2, T], F32R)
        hid_lo = s.sb("hid_lo", [P, 2, T], F32R)
        pg = [s.ps(f"pg{t}", [P, 512]) for t in range(3)]
        pu = [s.ps(f"pu{t}", [P, 512]) for t in range(3)]
        pd = [s.ps(f"pd{n}", [P, 512]) for n in range(2)]
        ld = {k: s.sem(f"loaded_{k}") for k in "gud"}
        hi = {k: s.sem(f"hi_{k}") for k in "gud"}
        lo = {k: s.sem(f"lo_{k}") for k in "gud"}
        gate_mm, up_mm, down_mm, silu_done, hid_done, hid_hi_done, hid_lo_done, added, zeroed = s.sems(
            "gate_mm up_mm down_mm silu_done hid_done hid_hi_done hid_lo_done added zeroed")
        block = ctx.enter_context(nc.Block())

        gate_view = w_gate_up[:, 0:F].rearrange("(k p) (g c) -> g p k c", p=P, c=2 * P)
        up_view = w_gate_up[:, F:2 * F].rearrange("(k p) (g c) -> g p k c", p=P, c=2 * P)
        down_view = w_down.rearrange("(g e p) n -> g p e n", p=P, e=2)
        view = {"g": gate_view, "u": up_view, "d": down_view}

        def raw_half(k, e):
            if k == "d":
                return raw[k][:, e * D:(e + 1) * D]
            return raw[k][:].rearrange("p (k e c) -> p e k c", e=2, c=P)[:, e]

        def tiled(w, k, e):
            return w[k][:, e, :] if k == "d" else w[k][:, e, :].rearrange("p (k c) -> p k c", c=P)

        @block.sync
        def _(sp):
            def load(k, g):
                dst = raw[k][:].rearrange("p (a c) -> p a c", c=D if k == "d" else 2 * P)
                src = view[k][g] if isinstance(g, int) else view[k][bass.ds(g, 1)].rearrange("g p a c -> p (g a) c")
                sp.dma_start(dst, src).then_inc(ld[k], 16)

            for k in "gud":
                load(k, 0)
            with sp.Fori(1, GROUPS) as g:
                for k in "gud":
                    sp.wait_ge(lo[k], 2 * g)
                    load(k, g)

        @block.gpsimd
        def _(pool):
            nc.gpsimd.memset(y[:], 0.0).then_inc(zeroed, 1)

        @block.tensor
        def _(pe):
            def project(k, e, g, banks, done, freed):
                pe.wait_ge(lo[k], 2 * g + e + 1)
                if not (isinstance(g, int) and 2 * g + e == 0):
                    pe.wait_ge(freed, 2 * g + e)
                for t in range(3):
                    cols = slice(t * TB, (t + 1) * TB)
                    for c in range(KC):
                        wh, wl = (w[k][:, e, c * P:(c + 1) * P] for w in (w_hi, w_lo))
                        nc.tensor.matmul(banks[t][:, 0:TB], wh, uh[:, c, cols], start=(c == 0), stop=False)
                        nc.tensor.matmul(banks[t][:, 0:TB], wh, ul[:, c, cols], start=False, stop=False)
                        last = nc.tensor.matmul(banks[t][:, 0:TB], wl, uh[:, c, cols], start=False, stop=(c == KC - 1))
                    last.then_inc(done, 1)

            def down(g):
                pe.wait_ge(hid_lo_done, 2 * g + 2)
                pe.wait_ge(lo["d"], 2 * g + 2)
                for n in range(2 * (NT + 1)):
                    i, half = n // 2, n % 2
                    if n >= 2 or not isinstance(g, int):
                        pe.wait_ge(added, 2 * (NT + 1) * g + n - 1)
                    for e in range(2):
                        hh, hl = (x[:, e, TILE0[i]:TILE0[i] + P] for x in (hid_hi, hid_lo))
                        wh, wl = (w["d"][:, e, half * 512:half * 512 + 512] for w in (w_hi, w_lo))
                        nc.tensor.matmul(pd[n % 2][:], hh, wh, start=(e == 0), stop=False)
                        nc.tensor.matmul(pd[n % 2][:], hl, wh, start=False, stop=False)
                        last = nc.tensor.matmul(pd[n % 2][:], hh, wl, start=False, stop=(e == 1))
                    last.then_inc(down_mm, 1)

            def group(g, first):
                project("g", 0, g, pg, gate_mm, silu_done)
                if not first:
                    down(g - 1)
                project("u", 0, g, pu, up_mm, hid_done)
                project("g", 1, g, pg, gate_mm, silu_done)
                project("u", 1, g, pu, up_mm, hid_done)

            group(0, True)
            group(1, False)
            with pe.Fori(2, GROUPS) as g:
                group(g, False)
            down(GROUPS - 1)

        @block.scalar
        def _(act):
            def round_half(k, g, e, used):
                act.wait_ge(ld[k], 16 * g + 16)
                if used is not None:
                    act.wait_ge(*used)
                nc.scalar.activation(tiled(w_hi, k, e), raw_half(k, e), ACT.Copy).then_inc(hi[k], 1)

            def gate(g, e):
                if not (isinstance(g, int) and 2 * g + e == 0):
                    act.wait_ge(hid_done, 2 * g + e)
                for t in range(3):
                    act.wait_ge(gate_mm, 6 * g + 3 * e + t + 1)
                    last = nc.scalar.activation(silu[:, t, :], pg[t][:, 0:TB], ACT.Silu)
                last.then_inc(silu_done, 1)

            def hidden(g, e):
                act.wait_ge(hid_done, 2 * g + e + 1)
                nc.scalar.activation(hid_hi[:, e, :], hid[:].rearrange("p t n -> p (t n)"), ACT.Copy).then_inc(hid_hi_done, 1)

            def group(g, first, last):
                gate(g, 0)
                if not last:
                    round_half("g", g + 1, 0, (gate_mm, 6 * g + 3))
                hidden(g, 0)
                if not last:
                    round_half("u", g + 1, 0, (up_mm, 6 * g + 3))
                for e in range(2):
                    round_half("d", g, e, None if first else (down_mm, 2 * (NT + 1) * g))
                gate(g, 1)
                if not last:
                    round_half("g", g + 1, 1, (gate_mm, 6 * g + 6))
                hidden(g, 1)
                if not last:
                    round_half("u", g + 1, 1, (up_mm, 6 * g + 6))

            for e in range(2):
                round_half("g", 0, e, None)
                round_half("u", 0, e, None)
            group(0, True, False)
            with act.Fori(1, GROUPS - 1) as g:
                group(g, False, False)
            group(GROUPS - 1, False, True)

        @block.vector
        def _(dve):
            def rest_half(k, g, e):
                dve.wait_ge(hi[k], 2 * g + e + 1)
                nc.vector.tensor_tensor(tiled(w_lo, k, e), raw_half(k, e), tiled(w_hi, k, e).bitcast(F32),
                                        ALU.subtract).then_inc(lo[k], 1)

            def hidden(g, e):
                if not (isinstance(g, int) and 2 * g + e == 0):
                    dve.wait_ge(hid_lo_done, 2 * g + e)
                dve.wait_ge(silu_done, 2 * g + e + 1)
                for t in range(3):
                    dve.wait_ge(up_mm, 6 * g + 3 * e + t + 1)
                    last = nc.vector.tensor_tensor(hid[:, t, :], silu[:, t, :], pu[t][:, 0:TB], ALU.mult)
                last.then_inc(hid_done, 1)
                dve.wait_ge(hid_hi_done, 2 * g + e + 1)
                nc.vector.tensor_tensor(hid_lo[:, e, :], hid[:].rearrange("p t n -> p (t n)"),
                                        hid_hi[:, e, :].bitcast(F32), ALU.subtract).then_inc(hid_lo_done, 1)

            def add_down(g):
                for n in range(2 * (NT + 1)):
                    i, half = n // 2, n % 2
                    dve.wait_ge(down_mm, 2 * (NT + 1) * g + n + 1)
                    part = y[:, i, half * 512:half * 512 + 512]
                    nc.vector.tensor_tensor(part, part, pd[n % 2][:], ALU.add).then_inc(added, 1)

            def group(g, first, last):
                if not first:
                    add_down(g - 1)
                if not last:
                    rest_half("g", g + 1, 0)
                hidden(g, 0)
                if not last:
                    rest_half("u", g + 1, 0)
                for e in range(2):
                    rest_half("d", g, e)
                if not last:
                    rest_half("g", g + 1, 1)
                hidden(g, 1)
                if not last:
                    rest_half("u", g + 1, 1)

            for e in range(2):
                rest_half("g", 0, e)
                rest_half("u", 0, e)
            dve.wait_ge(zeroed, 1)
            group(0, True, False)
            with dve.Fori(1, GROUPS - 1) as g:
                group(g, False, False)
            group(GROUPS - 1, False, True)
            add_down(GROUPS - 1)


def make_ident(nc, ident):
    with ExitStack() as ctx:
        s = Scope(nc, ctx, "id")
        ones = s.sb("ones", [P, P])
        filled = s.sem("filled")
        block = ctx.enter_context(nc.Block())

        @block.gpsimd
        def _(pool):
            nc.gpsimd.memset(ones[:], 1.0).then_inc(filled, 1)
            pool.wait_ge(filled, 1)
            nc.gpsimd.affine_select(out=ident[:], in_=ones[:], compare_op=ALU.is_equal, fill=0.0, base=0,
                                    pattern=[[-1, P]], channel_multiplier=1).then_inc(filled, 1)
            pool.wait_ge(filled, 2)


PAIRS = 14
KIND = ["conv"] * 6 + ["gate"] * 2 + ["query"] * 2 + ["key"] * 2 + ["value"] * 2
AB0 = QKV + DN
XP = T_P + 3 + N_B * (L_S + 3)
TAIL = 3 * (1 + N_B)


def projections(nc, uh, ul, w_in, conv_w, state_conv, qt, kt, ab, qkv_nat, gate_nat, k_rows, v_rows, conv_rows, ident):
    with ExitStack() as ctx:
        s = Scope(nc, ctx, "pr")
        raw = s.sb("raw", [P, 2, KC, 2 * P])
        w_hi, w_lo = s.sb("w_hi", [P, 2, D], F32R), s.sb("w_lo", [P, 2, D], F32R)
        ab_raw = s.sb("ab_raw", [P, KC, 8])
        ab_w = s.sb("ab_w", [P, KC, P], F32R)
        ab_cols = s.sb("ab_cols", [2 * 8, T])
        ab_lo_rows = s.sb("ab_lo_rows", [P, NT + 1, 8])
        xp = s.sb("xp", [P, 2, XP])
        acc = s.sb("acc", [P, T])
        post = s.sb("post", [P, 2, T])
        nat = s.sb("nat", [P, 2, NT + 1, P])
        taps = s.sb("taps", [P, 12, 4])
        taps_nat = s.sb("taps_nat", [4, QKV])
        hist_nat = s.sb("hist_nat", [3 * N_B, QKV])
        hist = s.sb("hist", [P, 12, 3 * N_B])
        tail = s.sb("tail", [P, 12, TAIL])
        tail_nat = s.sb("tail_nat", [TAIL, QKV])
        pm = [[s.ps(f"pm{e}{t}", [P, 512]) for t in range(3)] for e in range(2)]
        pn = [s.ps(f"pn{n}", [P, 512]) for n in range(2)]
        loaded = s.sems("loaded0 loaded1")
        (small, rounded, rest, ab_hi_done, ab_split, mm, ab_mm, ab_taken, ab_turned, ab_done, padded, hist_tr, hist_done, filled,
         tapped, convolved, ready, natural, evacuated, tail_taken, tail_tr, tail_done, tail_out) = s.sems(
            "small rounded rest ab_hi_done ab_split mm ab_mm ab_taken ab_turned ab_done padded hist_tr hist_done filled "
            "tapped convolved ready natural evacuated tail_taken tail_tr tail_done tail_out")
        stored = s.sems("stored0 stored1")
        block = ctx.enter_context(nc.Block())

        def sample(x, lo):
            return x[:, T_P + 3:XP].rearrange("p (b l) -> p b l", l=L_S + 3)[:, :, lo:lo + L_S]

        def pair_columns(j):
            return 2 * P * j + (8 if j >= 8 else 0)

        has_rows = [k != "query" for k in KIND for _ in range(2)]
        row_units = [sum(has_rows[:n]) for n in range(2 * PAIRS + 1)]

        @block.sync
        def _(sp):
            for j in range(2):
                sp.dma_start(raw[:, j], w_in[:, 2 * P * j:2 * P * (j + 1)].rearrange("(k p) c -> p k c", p=P)).then_inc(loaded[j], 16)
            sp.dma_start(ab_raw[:], w_in[:, AB0:AB0 + 8].rearrange("(k p) c -> p k c", p=P)).then_inc(small, 16)
            sp.dma_start(hist_nat[:], state_conv).then_inc(small, 16)
            sp.dma_start(taps_nat[:], conv_w).then_inc(small, 16)
            for j in range(2, PAIRS):
                sp.wait_ge(rest, 2 * j - 2)
                c = pair_columns(j)
                sp.dma_start(raw[:, j % 2], w_in[:, c:c + 2 * P].rearrange("(k p) c -> p k c", p=P)).then_inc(loaded[j % 2], 16)

        @block.gpsimd
        def _(pool):
            nc.gpsimd.memset(xp[:, :, 0:3], 0.0).then_inc(padded, 1)
            nc.gpsimd.memset(ab_w[:].bitcast(F32), 0.0).then_inc(padded, 1)
            target = ([(qkv_nat, u * P) for u in range(12)] + [(gate_nat, u * P) for u in range(4)] + [None] * 4
                      + [(k_rows, u * P) for u in range(4)] + [(v_rows, u * P) for u in range(4)])
            for n in range(2 * PAIRS):
                if not has_rows[n]:
                    continue
                r = row_units[n]
                dram, c = target[n]
                pool.wait_ge(evacuated, 3 * (r + 1))
                pool.dma_start(rows_view(dram)[:, :, c:c + P], nat[:, r % 2, 0:NT, :]).then_inc(stored[r % 2], 16)
                pool.dma_start(dram[T_P:T, c:c + P], nat[0:T_S, r % 2, NT, :]).then_inc(stored[r % 2], 16)
            pool.wait_ge(tail_done, 3)
            pool.dma_start(conv_rows, tail_nat[:]).then_inc(tail_out, 16)
            pool.wait_ge(tail_out, 16)
            for b in range(2):
                pool.wait_ge(stored[b], 16 * row_units[2 * PAIRS])

        @block.tensor
        def _(pe):
            def project(n):
                e = n % 2
                pe.wait_ge(rest, n + 1)
                if n >= 2:
                    pe.wait_ge(filled, n - 1)
                for t in range(3):
                    cols = slice(t * TB, (t + 1) * TB)
                    for c in range(KC):
                        wh, wl = (x[:, e, c * P:(c + 1) * P] for x in (w_hi, w_lo))
                        nc.tensor.matmul(pm[e][t][:, 0:TB], wh, uh[:, c, cols], start=(c == 0), stop=False)
                        nc.tensor.matmul(pm[e][t][:, 0:TB], wh, ul[:, c, cols], start=False, stop=False)
                        last = nc.tensor.matmul(pm[e][t][:, 0:TB], wl, uh[:, c, cols], start=False, stop=(c == KC - 1))
                    to_rows(n - 2, ((), (0, 1), (2,))[t])
                last.then_inc(mm, 1)

            def to_rows(n, banks):
                if n < 0 or not has_rows[n]:
                    return
                r = row_units[n]
                src = kt[:, n - 20, :] if KIND[n // 2] == "key" else post[:, n % 2, :]
                pe.wait_ge(ready, n + 1)
                for b in banks:
                    if 3 * r + b >= 2:
                        pe.wait_ge(evacuated, 3 * r + b - 1)
                    for i in range(4 * b, min(4 * b + 4, NT + 1)):
                        rows = P if i < NT else T_S
                        last = nc.tensor.transpose(pn[(3 * r + b) % 2][0:rows, (i % 4) * P:(i % 4) * P + P],
                                                   src[:, i * P:i * P + rows], ident[:])
                    last.then_inc(natural, 1)

            pe.wait_ge(small, 48)
            for u in range(12):
                nc.tensor.transpose(pm[1][1][:, u * 4:u * 4 + 4], taps_nat[:, u * P:(u + 1) * P], ident[0:4, 0:4])
                last = nc.tensor.transpose(pm[1][0][:, u * 24:u * 24 + 24], hist_nat[:, u * P:(u + 1) * P], ident[0:24, 0:24])
            last.then_inc(hist_tr, 1)
            pe.wait_ge(hist_done, 1)
            for n in range(2 * PAIRS):
                project(n)
            for n in (2 * PAIRS - 2, 2 * PAIRS - 1):
                to_rows(n, range(3))
            pe.wait_ge(ab_split, 1)
            pe.wait_ge(filled, 2 * PAIRS)
            for t in range(3):
                cols = slice(t * TB, (t + 1) * TB)
                for c in range(KC):
                    nc.tensor.matmul(pm[0][t][:, 0:TB], ab_w[:, c], uh[:, c, cols], start=(c == 0), stop=False)
                    last = nc.tensor.matmul(pm[0][t][:, 0:TB], ab_w[:, c], ul[:, c, cols], start=False, stop=(c == KC - 1))
            last.then_inc(ab_mm, 1)
            pe.wait_ge(ab_taken, 1)
            for i in range(NT + 1):
                last = nc.tensor.transpose(pn[0][:, 16 * i:16 * i + 16], ab_cols[:, TILE0[i]:TILE0[i] + P], ident[0:16, 0:16])
            last.then_inc(ab_turned, 1)
            pe.wait_ge(tail_taken, 12)
            for u in range(12):
                last = nc.tensor.transpose(pm[1][u // 4][0:TAIL, (u % 4) * P:(u % 4) * P + P], tail[:, u, :], ident[:])
                if u % 4 == 3:
                    last.then_inc(tail_tr, 1)

        @block.scalar
        def _(act):
            def round_half(n):
                e = n % 2
                act.wait_ge(loaded[n // 2 % 2], 16 * (n // 4) + 16)
                if n >= 2:
                    act.wait_ge(mm, n - 1)
                nc.scalar.activation(w_hi[:, e, :].rearrange("p (k c) -> p k c", c=P), raw[:, n // 2 % 2, :, e * P:(e + 1) * P],
                                     ACT.Copy).then_inc(rounded, 1)

            round_half(0)
            round_half(1)
            act.wait_ge(small, 48)
            act.wait_ge(padded, 2)
            nc.scalar.activation(ab_w[:, :, 0:8], ab_raw[:], ACT.Copy).then_inc(ab_hi_done, 1)
            act.wait_ge(hist_tr, 1)
            nc.scalar.activation(taps[:].rearrange("p u c -> p (u c)"), pm[1][1][:, 0:48], ACT.Copy)
            nc.scalar.activation(hist[:].rearrange("p u c -> p (u c)"), pm[1][0][:, 0:288], ACT.Copy).then_inc(hist_done, 1)

            def rows_out(n):
                if n < 0 or not has_rows[n]:
                    return
                r = row_units[n]
                if r >= 2:
                    act.wait_ge(stored[r % 2], 32 * (r // 2))
                for b in range(3):
                    act.wait_ge(natural, 3 * r + b + 1)
                    rows, count = (P, 4) if b < 2 else (T_S, 1)
                    nc.scalar.activation(nat[0:rows, r % 2, 4 * b:4 * b + count, :].rearrange("p i c -> p (i c)"),
                                         pn[(3 * r + b) % 2][0:rows, 0:count * P], ACT.Copy).then_inc(evacuated, 1)

            for n in range(2 * PAIRS):
                e, kind = n % 2, KIND[n // 2]
                rows_out(n - 2)
                act.wait_ge(mm, n + 1)
                banks = pm[e]
                if kind == "conv":
                    if n == 0:
                        act.wait_ge(padded, 2)
                        act.wait_ge(hist_done, 1)
                    if n >= 2:
                        act.wait_ge(tail_taken, n - 1)
                    for t in range(3):
                        end = min(T_P, (t + 1) * TB) - t * TB
                        nc.scalar.activation(xp[:, e, 3 + t * TB:3 + t * TB + end], banks[t][:, 0:end], ACT.Copy)
                    nc.scalar.activation(sample(xp[:, e], 3), banks[2][:, TB - T_S:TB].rearrange("p (b l) -> p b l", l=L_S), ACT.Copy)
                    nc.scalar.activation(sample(xp[:, e], 0)[:, :, 0:3], hist[:, n, :].rearrange("p (b l) -> p b l", l=3),
                                         ACT.Copy).then_inc(filled, 1)
                    if n + 2 < 2 * PAIRS:
                        round_half(n + 2)
                    act.wait_ge(convolved, n + 1)
                    if n >= 2:
                        act.wait_ge(natural, 3 * row_units[n - 1])
                    nc.scalar.activation(post[:, e, :], acc[:], ACT.Silu).then_inc(ready, 1)
                else:
                    if kind in ("gate", "value"):
                        act.wait_ge(natural, 3 * row_units[n - 1])
                    for t in range(3):
                        cols = slice(t * TB, (t + 1) * TB)
                        if kind == "query":
                            last = nc.scalar.activation(qt[:, n - 16, cols], banks[t][:, 0:TB], ACT.Copy, scale=DH ** -0.5)
                        elif kind == "key":
                            last = nc.scalar.activation(kt[:, n - 20, cols], banks[t][:, 0:TB], ACT.Copy)
                        else:
                            last = nc.scalar.activation(post[:, e, cols], banks[t][:, 0:TB],
                                                        ACT.Silu if kind == "gate" else ACT.Copy)
                    last.then_inc(filled, 1)
                    act.wait_ge(filled, n + 1)
                    act.sem_inc(ready, 1)
                    if n + 2 < 2 * PAIRS:
                        round_half(n + 2)
            for n in (2 * PAIRS - 2, 2 * PAIRS - 1):
                rows_out(n)
            act.wait_ge(ab_mm, 1)
            for t in range(3):
                last = nc.scalar.activation(ab_cols[:, t * TB:(t + 1) * TB], pm[0][t][0:16, 0:TB], ACT.Copy)
            last.then_inc(ab_taken, 1)
            act.wait_ge(ab_turned, 1)
            rows = pn[0][:, 0:16 * (NT + 1)].rearrange("p (i c) -> p i c", c=16)
            nc.scalar.activation(ab_lo_rows[:], rows[:, :, 8:16], ACT.Copy).then_inc(ab_done, 1)
            for b in range(3):
                act.wait_ge(tail_tr, b + 1)
                nc.scalar.activation(tail_nat[:, b * 512:b * 512 + 512], pm[1][b][0:TAIL, :], ACT.Copy).then_inc(tail_done, 1)

        @block.vector
        def _(dve):
            def rest_half(n):
                e = n % 2
                dve.wait_ge(rounded, n + 1)
                nc.vector.tensor_tensor(w_lo[:, e, :].rearrange("p (k c) -> p k c", c=P), raw[:, n // 2 % 2, :, e * P:(e + 1) * P],
                                        w_hi[:, e, :].bitcast(F32).rearrange("p (k c) -> p k c", c=P),
                                        ALU.subtract).then_inc(rest, 1)

            rest_half(0)
            rest_half(1)
            dve.wait_ge(ab_hi_done, 1)
            nc.vector.tensor_tensor(ab_w[:, :, 8:16], ab_raw[:], ab_w[:, :, 0:8].bitcast(F32), ALU.subtract).then_inc(ab_split, 1)
            for n in range(2 * PAIRS):
                e = n % 2
                if n < 12:
                    dve.wait_ge(filled, n + 1)
                    if n >= 1:
                        dve.wait_ge(ready, n)
                    prompt_acc = acc[:, 0:T_P]
                    sample_acc = acc[:, T_P:T].rearrange("p (b l) -> p b l", l=L_S)
                    for j in range(4):
                        tap = taps[:, n, j:j + 1]
                        for out, src in ((prompt_acc, xp[:, e, j:j + T_P]), (sample_acc, sample(xp[:, e], j))):
                            if j == 0:
                                step = nc.vector.tensor_scalar(out, src, tap, None, ALU.mult)
                            else:
                                step = nc.vector.scalar_tensor_tensor(out, src, tap, out, ALU.mult, ALU.add)
                            step.then_inc(tapped, 1)
                            if j < 3:
                                dve.wait_ge(tapped, 8 * n + 2 * j + (1 if out is prompt_acc else 2))
                    dve.wait_ge(tapped, 8 * n + 8)
                    nc.vector.tensor_copy(tail[:, n, 0:3], xp[:, e, T_P:T_P + 3]).then_inc(convolved, 1)
                    nc.vector.tensor_copy(tail[:, n, 3:TAIL].rearrange("p (b l) -> p b l", l=3),
                                          xp[:, e, T_P + 3:XP].rearrange("p (b l) -> p b l", l=L_S + 3)[:, :, L_S:L_S + 3]
                                          ).then_inc(tail_taken, 1)
                if n + 2 < 2 * PAIRS:
                    rest_half(n + 2)
            dve.wait_ge(ab_done, 1)
            rows = pn[0][:, 0:16 * (NT + 1)].rearrange("p (i c) -> p i c", c=16)
            nc.vector.tensor_tensor(ab[:], ab_lo_rows[:], rows[:, :, 0:8], ALU.add)


BIG = 2.0 ** 40


def prompt_attention(nc, qt, kt, v_rows, bias_row, o_all, ident):
    TILES = list(reversed(range(NT)))
    LONG = [i >= 4 for i in TILES]
    TURNS = [sum(2 if x else 1 for x in LONG[:k]) for k in range(NT + 1)]
    PAIRS = H_SB // 2
    with ExitStack() as ctx:
        s = Scope(nc, ctx, "pa")
        E = s.event
        v = s.sb("v", [P, NT, SB])
        bias = s.sb("bias", [P, H_SB])
        pair_bias = s.sb("pair_bias", [P, 2])
        mask = s.sb("mask", [P, P])
        ones = s.sb("ones", [P, P])
        zeros = s.sb("zeros", [P, 1])
        q_pair, k_pair = s.sb("q_pair", [P, T_P]), s.sb("k_pair", [P, T_P])
        v_pair = s.sb("v_pair", [P, NT, P])
        ex = s.sb("ex", [P, 4, 2, T_P])
        run = s.sb("run", [P, 2, 2, T_P])
        wt = s.sb("wt", [P, 2, 2, T_P])
        ot = s.sb("ot", [P, 2, P])
        pz = [s.ps(f"pz{e}", [P, T_P]) for e in range(2)]
        pa = [s.ps(f"pa{n}", [P, 512]) for n in range(2)]
        po, pb = s.ps("po", [P, 512]), s.ps("pb", [P, 512])
        block = ctx.enter_context(nc.Block())

        class Unit:

            def __init__(self, hp, k, d):
                self.n = NT * hp + (k - d)
                self.place = (k - d) % NT
                self.i = TILES[self.place]
                self.keys = (self.i + 1) * P
                self.long = LONG[self.place]
                self.turns = TURNS[NT] * (hp - (k < d)) + TURNS[self.place]
                self.pieces = [(e, c, min(c + 512, self.keys)) for e in range(2) for c in range(0, self.keys, 512)]

        def sweep(engine, step):
            for k in range(NT):
                step(0, k, lambda d: k >= d)
            with engine.Fori(1, PAIRS) as hp:
                for k in range(NT):
                    step(hp, k, lambda d: True)
            for k in range(5):
                step(PAIRS, k, lambda d: k < d)

        @block.sync
        def _(sp):
            sp.dma_start(v[:], rows_view(v_rows)).then_inc(E("loaded"), 16)
            sp.dma_start(bias[:], bias_row.partition_broadcast(P)).then_inc(E("loaded"), 16)

        @block.gpsimd
        def _(pool):
            nc.gpsimd.memset(ones[:], 1.0).then_inc(E("constants"), 1)
            nc.gpsimd.memset(zeros[:], 0.0).then_inc(E("constants"), 1)
            pool.wait_ge(E("constants"), 2)
            nc.gpsimd.affine_select(out=mask[:], in_=ones[:], compare_op=ALU.is_gt, fill=0.0, base=0,
                                    pattern=[[-1, P]], channel_multiplier=1).then_inc(E("constants"), 1)

            def step(hp, k, active):
                if active(2):
                    u = Unit(hp, k, 2)
                    x = ex[:, u.place % 4, :, 0:u.keys]
                    pool.wait_ge(E("decayed"), u.n + 1)
                    nc.gpsimd.tensor_tensor(x, x, run[:, u.place % 2, :, 0:u.keys], ALU.mult).then_inc(E("weighted"), 1)

            sweep(pool, step)

        @block.tensor
        def _(pe):
            def scores(u, hp):
                if u.place == 0:
                    pe.wait_ge(E("q_staged"), hp + 1)
                at_least(pe, E("exped"), 2 * u.n)
                for c in range(0, u.keys, 512):
                    cols = slice(c, min(c + 512, u.keys))
                    for e in range(2):
                        rows = slice(e * DH, (e + 1) * DH)
                        last = nc.tensor.matmul(pz[e][:, cols], q_pair[rows, u.i * P:(u.i + 1) * P],
                                                k_pair[rows, cols], start=True, stop=True)
                last.then_inc(E("z_mm"), 1)

            def turn(u):
                pe.wait_ge(E("weighted"), u.n + 1)
                for m, (e, c0, c1) in enumerate(u.pieces):
                    at_least(pe, E(f"copied{m % 2}"), u.turns + m // 2)
                    for j in range(c0, c1, P):
                        last = nc.tensor.transpose(pa[m % 2][:, j - c0:j - c0 + P], ex[:, u.place % 4, e, j:j + P], ident[:])
                    last.then_inc(E(f"turned{m % 2}"), 1)

            def sums(u, hp):
                if u.place == 0:
                    pe.wait_ge(E("v_staged"), hp + 1)
                for m in range(2):
                    pe.wait_ge(E(f"copied{m}"), u.turns + len(u.pieces) // 2)
                at_least(pe, E("ot_copied"), u.n)
                for j in range(u.i + 1):
                    for e in range(2):
                        rows = slice(e * DH, (e + 1) * DH)
                        last = nc.tensor.matmul(po[rows, 0:P], v_pair[:, j, rows], wt[:, u.place % 2, e, j * P:(j + 1) * P],
                                                start=(j == 0), stop=(j == u.i))
                last.then_inc(E("o_mm"), 1)

            def back(u):
                pe.wait_ge(E("ot_copied"), u.n + 1)
                at_least(pe, E("o_done"), u.n)
                nc.tensor.transpose(pb[:, 0:P], ot[:, u.place % 2], ident[:]).then_inc(E("o_turned"), 1)

            def step(hp, k, active):
                if active(0):
                    scores(Unit(hp, k, 0), hp)
                if active(3):
                    turn(Unit(hp, k, 3))
                if active(4):
                    sums(Unit(hp, k, 4), hp)
                if active(5):
                    back(Unit(hp, k, 5))

            pe.wait_ge(E("loaded"), 32)
            sweep(pe, step)

        @block.scalar
        def _(act):
            def copy(u, half):
                if half == 0:
                    at_least(act, E("o_mm"), u.n - 1)
                for m, (e, c0, c1) in list(enumerate(u.pieces))[2 * half:2 * half + 1]:
                    act.wait_ge(E("turned0"), u.turns + half + 1)
                    nc.scalar.activation(wt[:, u.place % 2, e, c0:c1], pa[0][:, 0:c1 - c0], ACT.Copy).then_inc(E("copied0"), 1)

            def step(hp, k, active):
                if active(2):
                    u = Unit(hp, k, 2)
                    r = run[:, u.place % 2, :, 0:u.keys]
                    act.wait_ge(E("summed"), 2 * u.n + 2)
                    nc.scalar.activation(r, r, ACT.Exp, scale=-1.0).then_inc(E("decayed"), 1)
                if active(0):
                    u = Unit(hp, k, 0)
                    act.wait_ge(E("z_mm"), u.n + 1)
                    before = Unit(hp, k, 4)
                    for m in range(2):
                        at_least(act, E(f"turned{m}"), before.turns + len(before.pieces) // 2 if not isinstance(hp, int) or k >= 4 else 0)
                    for e in range(2):
                        nc.scalar.activation(ex[:, u.place % 4, e, 0:u.keys], pz[e][:, 0:u.keys], ACT.Exp,
                                             bias=pair_bias[:, e:e + 1]).then_inc(E("exped"), 1)
                if active(3):
                    copy(Unit(hp, k, 3), 0)
                if active(1):
                    u = Unit(hp, k, 1)
                    act.wait_ge(E("held"), u.n + 1)
                    at_least(act, E("weighted"), u.n - 1)
                    nc.scalar.activation(run[:, u.place % 2, :, 0:u.keys], ex[:, u.place % 4, :, 0:u.keys], ACT.Ln,
                                         bias=1.0).then_inc(E("logged"), 1)
                if active(3):
                    copy(Unit(hp, k, 3), 1)
                if active(4):
                    u = Unit(hp, k, 4)
                    act.wait_ge(E("o_mm"), u.n + 1)
                    at_least(act, E("o_turned"), u.n - 1)
                    nc.scalar.activation(ot[:, u.place % 2], po[:, 0:P], ACT.Copy).then_inc(E("ot_copied"), 1)

            nc.scalar.preload_act_table_set("natural_log_exp_and_others")
            sweep(act, step)

        @block.vector
        def _(dve):
            def copy(u, half):
                if half == 0:
                    at_least(dve, E("o_mm"), u.n - 1)
                for m, (e, c0, c1) in list(enumerate(u.pieces))[2 * half + 1:2 * half + 2]:
                    dve.wait_ge(E("turned1"), u.turns + half + 1)
                    nc.vector.tensor_copy(wt[:, u.place % 2, e, c0:c1], pa[1][:, 0:c1 - c0]).then_inc(E("copied1"), 1)

            def step(hp, k, active):
                if active(0):
                    if k == 0:
                        at_least(dve, E("z_mm"), NT * hp)
                        nc.vector.tensor_scalar(pair_bias[:], bias[:, bass.ds(2 * hp, 2)], 1.0, None, ALU.mult)
                        nc.vector.tensor_scalar(k_pair[:], kt[:, bass.ds(hp, 1), 0:T_P], 1.0, None, ALU.mult)
                        nc.vector.tensor_scalar(q_pair[:], qt[:, bass.ds(hp, 1), 0:T_P], 1.0, None, ALU.mult).then_inc(E("q_staged"), 1)
                    u = Unit(hp, k, 0)
                    dve.wait_ge(E("exped"), 2 * u.n + 2)
                    if u.i > 0:
                        x = ex[:, u.place % 4, :, 0:u.keys - P]
                        nc.vector.tensor_scalar(x, x, BIG, None, ALU.min)
                    x = ex[:, u.place % 4, :, u.keys - P:u.keys]
                    nc.vector.scalar_tensor_tensor(x, x, BIG, mask[:].rearrange("p (o n) -> p o n", o=1).broadcast_to([P, 2, P]),
                                                   ALU.min, ALU.mult).then_inc(E("held"), 1)
                if active(4) and k == 4:
                    at_least(dve, E("o_mm"), NT * hp)
                    nc.vector.tensor_scalar(v_pair[:], v[:, :, bass.ds(P * hp, P)], 1.0, None, ALU.mult).then_inc(E("v_staged"), 1)
                if active(3):
                    copy(Unit(hp, k, 3), 0)
                if active(1):
                    u = Unit(hp, k, 1)
                    dve.wait_ge(E("logged"), u.n + 1)
                    for e in range(2):
                        r = run[:, u.place % 2, e, 0:u.keys][:, ::-1]
                        nc.vector.tensor_tensor_scan(r, r, zeros[:].broadcast_to([P, u.keys]), 0.0, ALU.add, ALU.add).then_inc(E("summed"), 1)
                if active(3):
                    copy(Unit(hp, k, 3), 1)
                if active(5):
                    u = Unit(hp, k, 5)
                    dve.wait_ge(E("o_turned"), u.n + 1)
                    at = P * (hp - (k < 5))
                    nc.vector.tensor_scalar(o_all[:, u.i, bass.ds(at, P)], pb[:, 0:P], 1.0, None, ALU.mult).then_inc(E("o_done"), 1)

            dve.wait_ge(E("loaded"), 32)
            dve.wait_ge(E("constants"), 3)
            sweep(dve, step)


LEVELS = 7
FACTORS = "rq rqg rk rkb rkbg rkd beta".split()


def delta_masks(nc, pool, made, masks, tri_s, same_s, level_s, spread_s, ones):
    count = 0

    def select(out, pattern, base, mult, op=ALU.is_ge):
        nonlocal count
        nc.gpsimd.affine_select(out=out, in_=out, compare_op=op, fill=0.0, base=base, pattern=pattern,
                                channel_multiplier=mult).then_inc(made, 1)
        count += 1
        pool.wait_ge(made, count)

    def fill(out):
        nonlocal count
        nc.gpsimd.memset(out, 1.0).then_inc(made, 1)
        count += 1
        pool.wait_ge(made, count)

    fill(ones[:])
    fill(masks[:])
    select(masks[:, 0, :], [[1, P]], 0, -1)
    for n in range(LEVELS):
        b = 1 << n
        view = masks[:, 1 + n, :].rearrange("p (m two c) -> p m two c", two=2, c=b)
        select(view[:, :, 1, :], [[-2 * b, P // (2 * b)], [0, b]], 0, 1)
        select(view[:, :, 1, :], [[2 * b, P // (2 * b)], [0, b]], b - 1, -1)
        nc.gpsimd.memset(view[:, :, 0, :], 0.0).then_inc(made, 1)
        count += 1
        pool.wait_ge(made, count)
    for m in (tri_s, same_s, spread_s):
        fill(m[:])
    select(spread_s[:], [[-L_S, N_B]], 0, 1)
    select(spread_s[:], [[L_S, N_B]], L_S - 1, -1)
    for m in (tri_s, same_s):
        v = m[:].rearrange("p (b l) -> p b l", l=L_S)
        select(v, [[-L_S, N_B], [0, L_S]], 0, 1)
        select(v, [[L_S, N_B], [0, L_S]], L_S - 1, -1)
    select(tri_s[:], [[1, T_S]], 0, -1)
    for n in range(2):
        nc.gpsimd.tensor_copy(level_s[:, n, :], masks[0:T_S, 1 + n, 0:T_S]).then_inc(made, 1)
        count += 1
    pool.wait_ge(made, count)


def delta_gates(nc, ab, qkv_nat, dt_row, a_log_row, masks, tri_s, same_s, spread_s, ones, qkv, g, big_g, last_decay,
                last_decay_s, fac):
    with ExitStack() as ctx:
        s = Scope(nc, ctx, "dg")
        E = s.event
        abx = s.sb("abx", [P, NT + 1, 8])
        dt, a_log = s.sb("dt", [P, 4]), s.sb("a_log", [P, 4])
        x, e, w, wi, l = (s.sb(n, [P, NT + 1, 4]) for n in "x e w wi l".split())
        last = s.sb("last", [P, NT + 1, 4])
        sq = s.sb("sq", [P, 2, D])
        norm = s.sb("norm", [P, NT + 1, 8])
        gm = s.sb("gm", [T_S, N_B, 4])
        pg, pl = s.ps("pg", [P, 512]), s.ps("pl", [P, 512])
        ps_, pls = s.ps("ps", [P, 512]), s.ps("pls", [P, 512])
        pb = s.ps("pb", [P, 512])
        block = ctx.enter_context(nc.Block())

        @block.sync
        def _(sp):
            sp.dma_start(dt[:], dt_row.partition_broadcast(P)).then_inc(E("small_in"), 16)
            sp.dma_start(a_log[:], a_log_row.partition_broadcast(P)).then_inc(E("small_in"), 16)
            sp.wait_ge(E("abx_zero"), 1)
            sp.dma_start(abx[0:T_S, NT, :], ab[P - T_S:P, NT, :]).then_inc(E("small_in"), 16)
            for i in range(NT):
                sp.dma_start(qkv[:, i, :], qkv_nat[i * P:(i + 1) * P, :]).then_inc(E(f"rows_in{i}"), 16)
            sp.dma_start(qkv[0:T_S, NT, :], qkv_nat[T_P:T, :]).then_inc(E(f"rows_in{NT}"), 16)

        @block.gpsimd
        def _(pool):
            nc.gpsimd.memset(qkv[T_S:2 * T_S, NT, :], 0.0)
            nc.gpsimd.memset(qkv[2 * T_S:P, NT, :], 0.0).then_inc(E("rows_zero"), 1)

        @block.vector
        def _(dve):
            n = 0

            def then(step):
                nonlocal n
                n += 1
                step.then_inc(E("dve_step"), 1)
                dve.wait_ge(E("dve_step"), n)

            nc.vector.memset(abx[:, NT, :], 0.0).then_inc(E("abx_zero"), 1)
            then(nc.vector.tensor_copy(abx[:, 0:NT, :], ab[:, 0:NT, :]))
            dve.wait_ge(E("small_in"), 48)
            then(nc.vector.tensor_tensor(x[:], abx[:, :, 0:4], dt[:].rearrange("p (o h) -> p o h", o=1).broadcast_to([P, NT + 1, 4]), ALU.add))
            nc.vector.tensor_scalar(e[:], x[:], 40.0, None, ALU.min).then_inc(E("x_held"), 1)
            dve.wait_ge(E("exp_x"), 1)
            then(nc.vector.tensor_scalar(w[:], e[:], 1.0, None, ALU.add))
            nc.vector.reciprocal(wi[:], w[:]).then_inc(E("one_plus"), 1)
            then(nc.vector.scalar_tensor_tensor(w[:], w[:], -1.0, e[:], ALU.add, ALU.subtract))
            dve.wait_ge(E("one_plus"), 1)
            then(nc.vector.tensor_tensor(w[:], w[:], wi[:], ALU.mult))
            dve.wait_ge(E("ln_w"), 1)
            then(nc.vector.tensor_tensor(l[:], l[:], w[:], ALU.subtract))
            then(nc.vector.tensor_tensor(l[:], l[:], x[:], ALU.max))
            dve.wait_ge(E("exp_a"), 1)
            nc.vector.scalar_tensor_tensor(g[:], l[:], -1.0, a_log[:].rearrange("p (o h) -> p o h", o=1).broadcast_to([P, NT + 1, 4]), ALU.mult, ALU.mult).then_inc(E("g_ready"), 1)
            dve.wait_ge(E("exp_b"), 1)
            then(nc.vector.tensor_scalar(fac["beta"][:], fac["beta"][:], 1.0, None, ALU.add))
            then(nc.vector.reciprocal(fac["beta"][:], fac["beta"][:]))
            dve.wait_ge(E("g_ready"), 1)
            nc.vector.tensor_tensor(gm[:], g[0:T_S, NT:NT + 1, :].broadcast_to([T_S, N_B, 4]),
                                    spread_s[:].rearrange("p (b o) -> p b o", o=1).broadcast_to([T_S, N_B, 4]), ALU.mult).then_inc(E("gm_ready"), 1)
            for i in range(NT + 1):
                dve.wait_ge(E("squared"), i + 1)
                nc.vector.tensor_reduce(norm[:, i, :], sq[:, i % 2].rearrange("p (h c) -> p h c", c=P), AX.X, ALU.add).then_inc(E("reduced"), 1)
            dve.wait_ge(E("reduced"), NT + 1)
            nc.vector.tensor_scalar(norm[:], norm[:], EPS, None, ALU.add).then_inc(E("norm_sum"), 1)
            dve.wait_ge(E("norm_root"), 1)
            then(nc.vector.reciprocal(norm[:], norm[:]))
            then(nc.vector.tensor_scalar(fac["rq"][:], norm[:, :, 0:4], float(P) ** -0.5, None, ALU.mult))
            then(nc.vector.tensor_copy(fac["rk"][:], norm[:, :, 4:8]))
            dve.wait_ge(E("sums"), 1)
            nc.vector.tensor_copy(big_g[:, 0:NT, :].rearrange("p i h -> p (i h)"), pg[:, 0:32])
            nc.vector.memset(last[:, NT, :], 0.0)
            nc.vector.memset(big_g[:, NT, :], 0.0)
            then(nc.vector.tensor_copy(last[:, 0:NT, :].rearrange("p i h -> p (i h)"), pl[:, 0:32]))
            then(nc.vector.tensor_copy(big_g[0:T_S, NT, :], ps_[0:T_S, 0:4]))
            then(nc.vector.tensor_copy(last[0:T_S, NT, :], pls[0:T_S, 0:4]))
            then(nc.vector.tensor_tensor(wi[:], last[:], big_g[:], ALU.subtract))
            nc.vector.tensor_copy(last_decay_s[:], pb[:, 0:32].rearrange("p (b h) -> p b h", h=4)).then_inc(E("to_exp"), 1)
            dve.wait_ge(E("exps"), 1)
            then(nc.vector.tensor_tensor(fac["rkb"][:], fac["rk"][:], fac["beta"][:], ALU.mult))
            then(nc.vector.tensor_tensor(fac["rqg"][:], fac["rq"][:], x[:], ALU.mult))
            then(nc.vector.tensor_tensor(fac["rkbg"][:], fac["rkb"][:], x[:], ALU.mult))
            then(nc.vector.tensor_tensor(fac["rkd"][:], fac["rk"][:], wi[:], ALU.mult))

        @block.scalar
        def _(act):
            nc.scalar.preload_act_table_set("natural_log_exp_and_others")
            act.wait_ge(E("x_held"), 1)
            nc.scalar.activation(e[:], e[:], ACT.Exp).then_inc(E("exp_x"), 1)
            nc.scalar.activation(a_log[:], a_log[:], ACT.Exp).then_inc(E("exp_a"), 1)
            nc.scalar.activation(fac["beta"][:], abx[:, :, 4:8], ACT.Exp, scale=-1.0).then_inc(E("exp_b"), 1)
            act.wait_ge(E("exp_x"), 1)
            nc.scalar.activation(l[:], e[:], ACT.Ln, bias=1.0).then_inc(E("ln_w"), 1)
            for i in range(NT + 1):
                act.wait_ge(E(f"rows_in{i}"), 16)
                if i == NT:
                    act.wait_ge(E("rows_zero"), 1)
                at_least(act, E("reduced"), i - 1)
                nc.scalar.activation(sq[:, i % 2], qkv[:, i, 0:D], ACT.Square).then_inc(E("squared"), 1)
            act.wait_ge(E("norm_sum"), 1)
            nc.scalar.activation(norm[:], norm[:], ACT.Sqrt).then_inc(E("norm_root"), 1)
            act.wait_ge(E("to_exp"), 1)
            nc.scalar.activation(x[:], big_g[:], ACT.Exp).then_inc(E("act_exp"), 1)
            nc.scalar.activation(last_decay[:], last[:], ACT.Exp).then_inc(E("act_exp"), 1)
            nc.scalar.activation(last_decay_s[:], last_decay_s[:], ACT.Exp).then_inc(E("act_exp"), 1)
            nc.scalar.activation(wi[:], wi[:], ACT.Exp).then_inc(E("exps"), 1)

        @block.tensor
        def _(pe):
            pe.wait_ge(E("g_ready"), 1)
            pe.wait_ge(E("gm_ready"), 1)
            flat = g[:, 0:NT, :].rearrange("p i h -> p (i h)")
            nc.tensor.matmul(pg[:, 0:32], masks[:, 0, :], flat, start=True, stop=True)
            nc.tensor.matmul(pl[:, 0:32], ones[:], flat, start=True, stop=True)
            nc.tensor.matmul(ps_[0:T_S, 0:4], tri_s[:], g[0:T_S, NT, :], start=True, stop=True)
            nc.tensor.matmul(pls[0:T_S, 0:4], same_s[:], g[0:T_S, NT, :], start=True, stop=True)
            nc.tensor.matmul(pb[:, 0:32], ones[0:T_S, :], gm[:].rearrange("p b h -> p (b h)"), start=True, stop=True).then_inc(E("sums"), 1)


def delta_prompt(nc, g, big_g, last_decay, fac, qkv, masks, ident, mixed, state_out):
    with ExitStack() as ctx:
        s = Scope(nc, ctx, "dp")
        E = s.event
        H = H_DN
        two = range(2)
        scaled = {n: [s.sb(f"{n}{z}", [P, H, P]) for z in two] for n in "kn kb qn qe kbg kd vb".split()}
        turned = {n: [s.sb(f"{n}t{z}", [P, H, P]) for z in two] for n in "kn kb qn qe".split()}
        dec = [s.sb(f"dec{z}", [P, H, P]) for z in two]
        mt = [s.sb(f"mt{z}", [P, H, P]) for z in two]
        at = [s.sb(f"at{z}", [P, H, P]) for z in two]
        lt = [s.sb(f"lt{z}", [P, LEVELS, H, P]) for z in two]
        x = [s.sb(f"x{z}", [P, H, P]) for z in two]
        xt = [s.sb(f"xt{z}", [P, H, P]) for z in two]
        p1 = [s.sb(f"p1{z}", [P, H, P]) for z in two]
        nwt = [s.sb(f"nwt{z}", [P, H, P]) for z in two]
        u = s.sb("u", [P, H, P])
        one_h = s.sb("one_h", [P, H, P])
        state = [s.sb(f"state{z}", [P, H, P]) for z in two]
        bank = [s.ps(f"b{n}", [P, H, P]) for n in range(8)]
        block = ctx.enter_context(nc.Block())
        SOURCE = {"kn": (DN, "rk"), "kb": (DN, "rkb"), "qn": (0, "rq"), "qe": (0, "rqg"), "kbg": (DN, "rkbg"),
                  "kd": (DN, "rkd"), "vb": (2 * DN, "beta")}
        TURN = "kn kb qn qe".split()
        A, B, C = [0, 3], [1, 4], [2, 5]
        W = [6, 3]
        STEPS = LEVELS - 1

        @block.gpsimd
        def _(pool):
            nc.gpsimd.memset(state[0][:], 0.0).then_inc(E("state_zero"), 1)

            def pair(i2):
                for n in range(LEVELS):
                    for z in two:
                        if n == 0:
                            pool.wait_ge(E("m_ready"), 2 * i2 + z + 1)
                        m = masks[:, 1 + n:2 + n, :].broadcast_to([P, H, P])
                        nc.gpsimd.tensor_tensor(lt[z][:, n], mt[z][:], m, ALU.mult).then_inc(E(f"level_ready{z}"), 1)

            pair(0)
            with pool.Fori(1, NT // 2) as i2:
                pair(i2)

        @block.tensor
        def _(pe):
            def chunk(i, z):
                for n, name in enumerate(TURN):
                    pe.wait_ge(E("scaled"), 5 * i + n + 1)
                    if z == 1:
                        pe.wait_ge(E("turned"), 4 * i - 4 + n + 1)
                    for h in range(H):
                        last = nc.tensor.transpose(bank[n][:, h], scaled[name][z][:, h], ident[:])
                    last.then_inc(E("turn_mm"), 1)
                pe.wait_ge(E("scaled"), 5 * i + 5)
                at_least(pe, E("held") if z else E("state_done"), i if z else 4 * i)
                for h in range(H):
                    last = nc.tensor.matmul(bank[4][:, h], dec[z][:, h], masks[:, 0, :], start=True, stop=True)
                last.then_inc(E("g_mm"), 1)
                pe.wait_ge(E("turned"), 4 * i + 4)
                at_least(pe, E("m_ready") if z else E("o_out"), i)
                for h in range(H):
                    last = nc.tensor.matmul(bank[5][:, h], turned["kn"][z][:, h], turned["kb"][z][:, h], start=True, stop=True)
                last.then_inc(E("gram_mm"), 1)
                at_least(pe, E("at_ready"), i)
                for h in range(H):
                    last = nc.tensor.matmul(bank[6][:, h], turned["kn"][z][:, h], turned["qn"][z][:, h], start=True, stop=True)
                last.then_inc(E("qk_mm"), 1)

            def invert(i2):
                for z in two:
                    pe.wait_ge(E("xt0"), 2 * i2 + z + 1)
                    for h in range(H):
                        last = nc.tensor.transpose(bank[A[z]][:, h], xt[z][:, h], ident[:])
                    last.then_inc(E("x0_mm"), 1)
                for n in range(STEPS):
                    count = 2 * (STEPS * i2 + n)
                    for z in two:
                        if n == 0:
                            pe.wait_ge(E("x0"), 2 * i2 + z + 1)
                        else:
                            pe.wait_ge(E("joined"), count + z - 1)
                        pe.wait_ge(E(f"level_ready{z}"), LEVELS * i2 + n + 2)
                        for h in range(H):
                            last = nc.tensor.matmul(bank[A[z]][:, h], lt[z][:, n + 1, h], x[z][:, h], start=True, stop=True)
                        last.then_inc(E("p1_mm"), 1)
                    for z in two:
                        pe.wait_ge(E("p1"), count + z + 1)
                        for h in range(H):
                            last = nc.tensor.matmul(bank[C[z]][:, h], p1[z][:, h], xt[z][:, h], start=True, stop=True)
                        if n < STEPS - 1:
                            for h in range(H):
                                last = nc.tensor.matmul(bank[B[z]][:, h], xt[z][:, h], p1[z][:, h], start=True, stop=True)
                        last.then_inc(E("join_mm"), 1)

            def advance(i, z, i2):
                pe.wait_ge(E("nwt"), i + 1)
                at_least(pe, E("state_done"), 4 * i)
                if isinstance(i, int) and i == 0:
                    pe.wait_ge(E("state_zero"), 1)
                for h in range(H):
                    nc.tensor.matmul(bank[7][:, h], xt[z][:, h], scaled["vb"][z][:, h], start=True, stop=False)
                    last = nc.tensor.matmul(bank[7][:, h], nwt[z][:, h], state[z][:, h], start=False, stop=True)
                last.then_inc(E("u_mm"), 1)
                pe.wait_ge(E("u"), i + 1)
                for h in range(H):
                    last = nc.tensor.matmul(bank[4][:, h], scaled["kd"][z][:, h], u[:, h], start=True, stop=True)
                last.then_inc(E("ds_mm"), 1)
                at_least(pe, E("o_out"), i)
                for h in range(H):
                    nc.tensor.matmul(bank[5][:, h], turned["qe"][z][:, h], state[z][:, h], start=True, stop=False)
                    last = nc.tensor.matmul(bank[5][:, h], at[z][:, h], u[:, h], start=False, stop=True)
                last.then_inc(E("o_mm"), 1)

            def pair(i2):
                for z in two:
                    chunk(2 * i2 + z, z)
                invert(i2)
                pe.wait_ge(E("joined"), 2 * STEPS * (i2 + 1))
                pe.wait_ge(E("rest_scaled"), 6 * i2 + 6)
                pe.wait_ge(E("at_ready"), 2 * i2 + 2)
                for z in two:
                    for h in range(H):
                        last = nc.tensor.matmul(bank[W[z]][:, h], scaled["kbg"][z][:, h], xt[z][:, h], start=True, stop=True)
                    last.then_inc(E("w_mm"), 1)
                for z in two:
                    advance(2 * i2 + z, z, i2)

            pair(0)
            with pe.Fori(1, NT // 2) as i2:
                pair(i2)

        @block.scalar
        def _(act):
            nc.scalar.preload_act_table_set("natural_log_exp_and_others")

            def pair(i2):
                for z in two:
                    i = 2 * i2 + z
                    for n, name in enumerate(TURN):
                        act.wait_ge(E("turn_mm"), 4 * i + n + 1)
                        nc.scalar.activation(turned[name][z][:], bank[n][:], ACT.Copy).then_inc(E("turned"), 1)
                    act.wait_ge(E("held"), i + 1)
                    nc.scalar.activation(dec[z][:], dec[z][:], ACT.Exp).then_inc(E("dec_exp"), 1)
                for z in two:
                    act.wait_ge(E("x0_mm"), 2 * i2 + z + 1)
                    nc.scalar.activation(x[z][:], bank[A[z]][:], ACT.Copy).then_inc(E("x0"), 1)
                for n in range(STEPS):
                    for z in two:
                        act.wait_ge(E("p1_mm"), 2 * (STEPS * i2 + n) + z + 1)
                        nc.scalar.activation(p1[z][:], bank[A[z]][:], ACT.Copy).then_inc(E("p1"), 1)
                for z in two:
                    act.wait_ge(E("w_mm"), 2 * i2 + z + 1)
                    nc.scalar.activation(nwt[z][:], bank[W[z]][:], ACT.Copy, scale=-1.0).then_inc(E("nwt"), 1)
                for z in two:
                    i = 2 * i2 + z
                    act.wait_ge(E("u_mm"), i + 1)
                    at_least(act, E("o_mm"), i)
                    nc.scalar.activation(u[:], bank[7][:], ACT.Copy).then_inc(E("u"), 1)

            pair(0)
            with act.Fori(1, NT // 2) as i2:
                pair(i2)

        @block.vector
        def _(dve):
            def rows(i, name):
                at, factor = SOURCE[name]
                r = qkv[:, bass.ds(i, 1), at:at + DN].rearrange("p o (h c) -> p (o h) c", c=P)
                return r, fac[factor][:, bass.ds(i, 1), :].rearrange("p o h -> p h o").broadcast_to([P, H, P])

            def scale(i, z):
                for name in TURN:
                    nc.vector.tensor_tensor(scaled[name][z][:], *rows(i, name), ALU.mult).then_inc(E("scaled"), 1)
                nc.vector.tensor_tensor(dec[z][:], one_h[:], g[:, bass.ds(i, 1), :].rearrange("p o h -> p h o").broadcast_to([P, H, P]),
                                        ALU.mult).then_inc(E("scaled"), 1)

            def pair(i2, more=True):
                for z in two:
                    i = 2 * i2 + z
                    dve.wait_ge(E("g_mm"), i + 1)
                    for h in range(H):
                        last = nc.vector.tensor_scalar(dec[z][:, h], bank[4][:, h], big_g[:, bass.ds(i, 1), h], 0.0,
                                                       ALU.subtract, ALU.min)
                    last.then_inc(E("held"), 1)
                    dve.wait_ge(E("dec_exp"), i + 1)
                    nc.vector.tensor_tensor(dec[z][:], dec[z][:], masks[:, 0:1, :].broadcast_to([P, H, P]), ALU.mult).then_inc(E("dec_masked"), 1)
                    dve.wait_ge(E("dec_masked"), i + 1)
                    dve.wait_ge(E("gram_mm"), i + 1)
                    nc.vector.tensor_tensor(mt[z][:], dec[z][:], bank[5][:], ALU.mult).then_inc(E("m_ready"), 1)
                    dve.wait_ge(E("qk_mm"), i + 1)
                    nc.vector.tensor_tensor(at[z][:], dec[z][:], bank[6][:], ALU.mult).then_inc(E("at_ready"), 1)
                for z in two:
                    dve.wait_ge(E(f"level_ready{z}"), LEVELS * i2 + 1)
                    nc.vector.tensor_tensor(xt[z][:], ident[:].rearrange("p (o c) -> p o c", o=1).broadcast_to([P, H, P]), lt[z][:, 0],
                                            ALU.subtract).then_inc(E("xt0"), 1)
                for z in two:
                    for name in ("kbg", "kd", "vb"):
                        nc.vector.tensor_tensor(scaled[name][z][:], *rows(2 * i2 + z, name), ALU.mult).then_inc(E("rest_scaled"), 1)
                for n in range(STEPS):
                    for z in two:
                        dve.wait_ge(E("join_mm"), 2 * (STEPS * i2 + n) + z + 1)
                        if n < STEPS - 1:
                            nc.vector.tensor_tensor(x[z][:], x[z][:], bank[B[z]][:], ALU.subtract)
                        nc.vector.tensor_tensor(xt[z][:], xt[z][:], bank[C[z]][:], ALU.subtract).then_inc(E("joined"), 1)
                for z in two:
                    i = 2 * i2 + z
                    if more:
                        scale(i + 2, z)
                    dve.wait_ge(E("ds_mm"), i + 1)
                    at_least(dve, E("o_mm"), i)
                    for h in range(H):
                        nc.vector.scalar_tensor_tensor(state[1 - z][:, h], state[z][:, h], last_decay[:, bass.ds(i, 1), h],
                                                       bank[4][:, h], ALU.mult, ALU.add).then_inc(E("state_done"), 1)
                    dve.wait_ge(E("o_mm"), i + 1)
                    nc.vector.tensor_scalar(mixed[:, bass.ds(i, 1), 0:DN], bank[5][:].rearrange("p h c -> p (h c)"), 1.0, None, ALU.mult).then_inc(E("o_out"), 1)

            nc.vector.memset(one_h[:], 1.0).then_inc(E("ones_made"), 1)
            dve.wait_ge(E("ones_made"), 1)
            for z in two:
                scale(z, z)
            pair(0)
            with dve.Fori(1, NT // 2 - 1) as i2:
                pair(i2)
            pair(NT // 2 - 1, more=False)

        @block.sync
        def _(sp):
            sp.wait_ge(E("state_done"), 4 * NT)
            sp.dma_start(state_out.rearrange("h k v -> k h v"), state[0][:]).then_inc(E("stored"), 16)
            sp.wait_ge(E("stored"), 16)


def delta_sample(nc, g, big_g, last_decay_s, fac, qkv, tri_s, level_s, spread_s, ident, states, mixed, states_out):
    with ExitStack() as ctx:
        s = Scope(nc, ctx, "ds")
        E = s.event
        H, R = H_DN, T_S
        scaled = {n: s.sb(n, [R, H, P]) for n in "kn kb qn qe kbg kd vb".split()}
        turned = {n: s.sb(f"{n}t", [P, H, R]) for n in "kn kb qn".split()}
        one_r = s.sb("one_r", [R, H, R])
        gb, dec, mt, at, lt0, lt1, x, xt, p1 = (s.sb(n, [R, H, R]) for n in "gb dec mt at lt0 lt1 x xt p1".split())
        u_t, o_t = (s.sb(n, [P, H, R]) for n in "u_t o_t".split())
        nq, nq_s = s.sb("nq", [P, H, N_B, 2, L_S]), s.sb("nq_s", [P, H, N_B, 2, L_S])
        u = s.sb("u", [R, H, P])
        um = s.sb("um", [R, 2, N_B, P])
        old, new = s.sb("old", [P, N_B, H, P]), s.sb("new", [P, N_B, H, P])
        bank = [s.ps(f"b{n}", [P, 512]) for n in range(4)]
        ds = [s.ps(f"d{n}", [P, N_B, P]) for n in range(2)]
        block = ctx.enter_context(nc.Block())
        SOURCE = {"kn": (DN, "rk"), "kb": (DN, "rkb"), "qn": (0, "rq"), "qe": (0, "rqg"), "kbg": (DN, "rkbg"),
                  "kd": (DN, "rkd"), "vb": (2 * DN, "beta")}
        TURN = "kn kb qn qe".split()

        def cols(b, w=R):
            return bank[b][:, 0:H * w].rearrange("p (h c) -> p h c", c=w)

        def side_by_side(x, which):
            return x[:, :, :, which, :]

        def by_sequence(x):
            return x.rearrange("p h (b l) -> p h b l", l=L_S)

        def rows(b, w=R):
            return bank[b][0:R, 0:H * w].rearrange("p (h c) -> p h c", c=w)

        def by_head(m):
            return m.rearrange("p (o c) -> p o c", o=1).broadcast_to([R, H, R])

        @block.sync
        def _(sp):
            sp.dma_start(old[:], states.rearrange("b h k v -> k b h v")).then_inc(E("states_in"), 16)
            for h in range(H):
                sp.wait_ge(E("new_ready"), h + 1)
                sp.dma_start(states_out[:, h].rearrange("b k v -> k b v"), new[:, :, h]).then_inc(E("states_out"), 16)
            sp.wait_ge(E("states_out"), 16 * H)

        @block.gpsimd
        def _(pool):
            pool.wait_ge(E("states_in"), 16)
            for h in range(H):
                nc.gpsimd.tensor_tensor(new[:, :, h], old[:, :, h], last_decay_s[:, :, h:h + 1].broadcast_to([P, N_B, P]), ALU.mult).then_inc(E("faded"), 1)

        @block.tensor
        def _(pe):
            for n, name in enumerate(TURN):
                pe.wait_ge(E("scaled"), n + 1)
                for h in range(H):
                    last = nc.tensor.transpose(cols(n)[:, h], scaled[name][:, h], ident[0:R, 0:R])
                last.then_inc(E("turn_mm"), 1)
            pe.wait_ge(E("scaled"), 5)
            pe.wait_ge(E("turned"), 4)
            for h in range(H):
                last = nc.tensor.matmul(rows(0)[:, h], gb[:, h], tri_s[:], start=True, stop=True)
            last.then_inc(E("g_mm"), 1)
            for h in range(H):
                last = nc.tensor.matmul(rows(1)[:, h], turned["kn"][:, h], turned["kb"][:, h], start=True, stop=True)
            last.then_inc(E("gram_mm"), 1)
            for h in range(H):
                last = nc.tensor.matmul(rows(2)[:, h], turned["kn"][:, h], turned["qn"][:, h], start=True, stop=True)
            last.then_inc(E("qk_mm"), 1)
            pe.wait_ge(E("xt0"), 1)
            for h in range(H):
                last = nc.tensor.transpose(rows(3)[:, h], xt[:, h], ident[0:R, 0:R])
            last.then_inc(E("x0_mm"), 1)
            pe.wait_ge(E("x0"), 1)
            for h in range(H):
                last = nc.tensor.matmul(rows(0)[:, h], lt1[:, h], x[:, h], start=True, stop=True)
            last.then_inc(E("p1_mm"), 1)
            pe.wait_ge(E("p1"), 1)
            for h in range(H):
                last = nc.tensor.matmul(rows(1)[:, h], p1[:, h], xt[:, h], start=True, stop=True)
            last.then_inc(E("join_mm"), 1)
            pe.wait_ge(E("joined"), 1)
            for h in range(H):
                last = nc.tensor.matmul(cols(2)[:, h], scaled["kbg"][:, h], xt[:, h], start=True, stop=True)
            last.then_inc(E("w_mm"), 1)
            for h in range(H):
                last = nc.tensor.matmul(cols(0)[:, h], scaled["vb"][:, h], xt[:, h], start=True, stop=True)
            last.then_inc(E("vx_mm"), 1)
            pe.wait_ge(E("nwt"), 1)
            pe.wait_ge(E("states_in"), 16)
            for h in range(H):
                for b in range(N_B):
                    out = bank[3][:, 0:2 * H * R].rearrange("p (h b x) -> p h b x", h=H, b=N_B)[:, h, b]
                    last = nc.tensor.matmul(out, old[:, b, h], nq[:, h, b].rearrange("p s l -> p (s l)"), start=True, stop=True)
            last.then_inc(E("nq_mm"), 1)
            pe.wait_ge(E("u_t"), 1)
            for h in range(H):
                last = nc.tensor.transpose(rows(0, P)[:, h], u_t[:, h], ident[:])
            last.then_inc(E("u_turn"), 1)
            pe.wait_ge(E("u"), 1)
            for h in range(H):
                last = nc.tensor.matmul(cols(1)[:, h], u[:, h], at[:, h], start=True, stop=True)
            last.then_inc(E("o_mm"), 1)
            for h in range(H):
                pe.wait_ge(E("um"), h + 1)
                at_least(pe, E("new_ready"), h - 1)
                for half in range(2):
                    last = nc.tensor.matmul(ds[h % 2][:, 4 * half:4 * half + 4], scaled["kd"][:, h], um[:, h % 2, 4 * half:4 * half + 4],
                                            start=True, stop=True)
                last.then_inc(E("ds_mm"), 1)
            pe.wait_ge(E("o_t"), 1)
            for h in range(H):
                last = nc.tensor.transpose(rows(2, P)[:, h], o_t[:, h], ident[:])
            last.then_inc(E("o_turn"), 1)

        @block.scalar
        def _(act):
            for n, name in enumerate(TURN):
                act.wait_ge(E("turn_mm"), n + 1)
                nc.scalar.activation(turned[name][:] if name in turned else side_by_side(nq, 1), (cols(n) if name in turned else by_sequence(cols(n))), ACT.Copy).then_inc(E("turned"), 1)
            act.wait_ge(E("held"), 1)
            nc.scalar.activation(dec[:], dec[:], ACT.Exp).then_inc(E("dec_exp"), 1)
            act.wait_ge(E("x0_mm"), 1)
            nc.scalar.activation(x[:], rows(3), ACT.Copy).then_inc(E("x0"), 1)
            act.wait_ge(E("p1_mm"), 1)
            nc.scalar.activation(p1[:], rows(0), ACT.Copy).then_inc(E("p1"), 1)
            act.wait_ge(E("w_mm"), 1)
            nc.scalar.activation(side_by_side(nq, 0), by_sequence(cols(2)), ACT.Copy, scale=-1.0).then_inc(E("nwt"), 1)
            act.wait_ge(E("nq_mm"), 1)
            nc.scalar.activation(nq_s[:].rearrange("p h b s l -> p (h b s l)"), bank[3][:, 0:2 * H * R], ACT.Copy).then_inc(E("nq_s"), 1)
            act.wait_ge(E("u_turn"), 1)
            nc.scalar.activation(u[:], rows(0, P), ACT.Copy).then_inc(E("u"), 1)
            act.wait_ge(E("o_turn"), 1)
            nc.scalar.activation(mixed[0:R, NT, 0:DN], bank[2][0:R, :], ACT.Copy).then_inc(E("o_out"), 1)

        @block.vector
        def _(dve):
            def source(name):
                at0, factor = SOURCE[name]
                r = qkv[0:R, NT, at0:at0 + DN].rearrange("p (h c) -> p h c", c=P)
                return r, fac[factor][0:R, NT:NT + 1, :].rearrange("p o h -> p h o").broadcast_to([R, H, P])

            nc.vector.memset(one_r[:], 1.0).then_inc(E("ones"), 1)
            for name in TURN:
                nc.vector.tensor_tensor(scaled[name][:], *source(name), ALU.mult).then_inc(E("scaled"), 1)
            dve.wait_ge(E("ones"), 1)
            nc.vector.tensor_tensor(gb[:], one_r[:], g[0:R, NT:NT + 1, :].rearrange("p o h -> p h o").broadcast_to([R, H, R]),
                                    ALU.mult).then_inc(E("scaled"), 1)
            for name in ("kbg", "kd", "vb"):
                nc.vector.tensor_tensor(scaled[name][:], *source(name), ALU.mult)
            dve.wait_ge(E("g_mm"), 1)
            for h in range(H):
                last = nc.vector.tensor_scalar(dec[:, h], rows(0)[:, h], big_g[0:R, NT, h:h + 1], 0.0, ALU.subtract, ALU.min)
            last.then_inc(E("held"), 1)
            dve.wait_ge(E("dec_exp"), 1)
            nc.vector.tensor_tensor(dec[:], dec[:], by_head(tri_s[:]), ALU.mult).then_inc(E("dec_masked"), 1)
            dve.wait_ge(E("dec_masked"), 1)
            dve.wait_ge(E("gram_mm"), 1)
            nc.vector.tensor_tensor(mt[:], dec[:], rows(1), ALU.mult).then_inc(E("mt"), 1)
            dve.wait_ge(E("qk_mm"), 1)
            nc.vector.tensor_tensor(at[:], dec[:], rows(2), ALU.mult).then_inc(E("at"), 1)
            dve.wait_ge(E("mt"), 1)
            nc.vector.tensor_tensor(lt0[:], mt[:], by_head(level_s[:, 0]), ALU.mult).then_inc(E("lt"), 1)
            nc.vector.tensor_tensor(lt1[:], mt[:], by_head(level_s[:, 1]), ALU.mult).then_inc(E("lt"), 1)
            dve.wait_ge(E("lt"), 2)
            nc.vector.tensor_tensor(xt[:], by_head(ident[0:R, 0:R]), lt0[:], ALU.subtract).then_inc(E("xt0"), 1)
            dve.wait_ge(E("join_mm"), 1)
            nc.vector.tensor_tensor(xt[:], xt[:], rows(1), ALU.subtract).then_inc(E("joined"), 1)
            dve.wait_ge(E("nq_s"), 1)
            dve.wait_ge(E("vx_mm"), 1)
            nc.vector.tensor_tensor(by_sequence(u_t[:]), side_by_side(nq_s, 0), by_sequence(cols(0)), ALU.add).then_inc(E("u_t"), 1)
            dve.wait_ge(E("u"), 1)
            dve.wait_ge(E("o_mm"), 1)
            nc.vector.tensor_tensor(by_sequence(o_t[:]), side_by_side(nq_s, 1), by_sequence(cols(1)), ALU.add).then_inc(E("o_t"), 1)
            dve.wait_ge(E("states_in"), 16)
            for h in range(H):
                at_least(dve, E("ds_mm"), h - 1)
                nc.vector.tensor_tensor(um[:, h % 2], u[:, h:h + 1].broadcast_to([R, N_B, P]),
                                        spread_s[:].rearrange("p (b o) -> p b o", o=1).broadcast_to([R, N_B, P]), ALU.mult).then_inc(E("um"), 1)
                dve.wait_ge(E("faded"), h + 1)
                dve.wait_ge(E("ds_mm"), h + 1)
                nc.vector.tensor_tensor(new[:, :, h], new[:, :, h], ds[h % 2][:], ALU.add).then_inc(E("new_ready"), 1)


def sample_attention(nc, qt, kt, v_rows, cache_k, cache_v, page_table, bias_row, ident, mixed, pool_work):
    PAGES, G = page_table.shape[1], N_B // 4
    AHEAD = 4
    CACHED = PAGES * P
    KEYS = CACHED + T_S
    ROUNDS = PAGES + 1
    NPHYS = cache_k.shape[0]
    R = 32
    with ExitStack() as ctx:
        s = Scope(nc, ctx, "sa")
        E = s.event
        table = s.sb("table", [1, N_B * PAGES], I32)
        k_page = s.sb("k_page", [P, AHEAD, 4, SB])
        v_page = s.sb("v_page", [P, AHEAD, 4, SB])
        v_new = s.sb("v_new", [T_S, SB])
        k_turned = s.sb("k_turned", [P, 2, 4, 4, P])
        run = s.sb("run", [P, G, KEYS])
        qb = s.sb("qb", [P, G, 4, 4, R])
        bias = s.sb("bias", [H_SB, 1])
        row_bias = s.sb("row_bias", [P, 1])
        pick_t = s.sb("pick_t", [H_SB, P])
        own_t = s.sb("own_t", [T_S, G, P])
        sample_t = s.sb("sample_t", [T_S, G, P])
        pick, own, sample = s.sb("pick", [P, H_SB]), s.sb("own", [P, G, T_S]), s.sb("sample", [P, G, T_S])
        ex = s.sb("ex", [P, G, KEYS])
        zeros = s.sb("zeros", [P, 1])
        w_s, wt = s.sb("w_s", [P, 2, P]), s.sb("wt", [P, 2, P])
        o_rows = s.sb("o_rows", [P, G, SB])
        pk = [s.ps(f"pk{b}", [P, 4, P]) for b in range(4)]
        pz = [s.ps(f"pz{par}", [P, 512]) for par in range(2)]
        pw = pz
        pv, pm = s.ps("pv", [P, 512]), s.ps("pm", [P, 512])
        block = ctx.enter_context(nc.Block())

        def static(p, *values):
            return isinstance(p, int) and p in values

        def load(engine, mine, buffer, cache, gi, p, u, arrived):
            for b in mine:
                page = engine.value_load(table[0:1, bass.ds((4 * gi + b) * PAGES + p, 1)], min_val=0, max_val=NPHYS - 1)
                engine.dma_start(buffer[:, u, b:b + 1, :], cache[bass.ds(page, 1)].rearrange("g p n -> p g n")).then_inc(E(f"{arrived}{u}"), 16)

        def load_keys(engine, mine, gi, p, u):
            at_least(engine, E("k_turned1"), 2 * (PAGES * gi + p - AHEAD + 1))
            load(engine, mine, k_page, cache_k, gi, p, u, "k_in")

        def load_values(engine, mine, gi, p, u):
            r = ROUNDS * gi + p
            at_least(engine, E("v_mm"), r - AHEAD if static(p, *range(AHEAD)) else r - AHEAD + 1)
            load(engine, mine, v_page, cache_v, gi, p, u, "v_in")

        @block.sync
        def _(sp):
            sp.dma_start(table[:], page_table.rearrange("b n -> (b n)").rearrange("(o n) -> o n", o=1)).then_inc(E("table_in"), 16)
            sp.dma_start(bias[:], bias_row.rearrange("(h o) -> h o", o=1)).then_inc(E("small_in"), 16)
            sp.dma_start(v_new[:], v_rows[T_P:T, :]).then_inc(E("small_in"), 16)
            sp.wait_ge(E("table_in"), 16)

            def pages(step, gi, peeled):
                if peeled:
                    for u in range(AHEAD):
                        step(gi, u, u)
                with sp.Fori(1, PAGES // AHEAD) as p4:
                    for u in range(AHEAD):
                        step(gi, AHEAD * p4 + u, u)

            for gi in range(G):
                pages(lambda gi, p, u: load_keys(sp, (0, 1), gi, p, u), gi, True)
            for u in range(AHEAD):
                load_values(sp, range(4), 0, u, u)
            for gi in range(G):
                pages(lambda gi, p, u: load_values(sp, (0, 1), gi, p, u), gi, gi > 0)

        @block.gpsimd
        def _(pool):
            n = 0

            def made(step):
                nonlocal n
                n += 1
                step.then_inc(E("made"), 1)
                pool.wait_ge(E("made"), n)

            def select(m, base, mult, pattern, op):
                made(nc.gpsimd.affine_select(out=m, in_=m, compare_op=op, fill=0.0, base=base, pattern=pattern, channel_multiplier=mult))

            made(nc.gpsimd.memset(qb[:], 0.0))
            for m in (pick_t, own_t, sample_t):
                made(nc.gpsimd.memset(m[:], 1.0))
            select(pick_t[:], 0, -1, [[0, 4], [1, H_SB], [0, L_S]], ALU.is_equal)
            for gi in range(G):
                first = 4 * L_S * gi
                select(own_t[:, gi], -first, 1, [[-L_S, 4], [0, H_SB], [0, L_S]], ALU.is_ge)
                select(own_t[:, gi], first, -1, [[L_S, 4], [0, H_SB], [1, L_S]], ALU.is_gt)
                select(sample_t[:, gi], -first, 1, [[-L_S, 4], [0, H_SB], [-1, L_S]], ALU.is_equal)
            pool.sem_inc(E("masks_made"), 1)
            made(nc.gpsimd.memset(zeros[:], 0.0))
            pool.sem_inc(E("zeros_made"), 1)
            pool_work(pool, E("pool_work"))

        @block.tensor
        def _(pe):
            pe.wait_ge(E("masks_made"), 1)
            pe.wait_ge(E("small_in"), 32)
            nc.tensor.matmul(pm[:, 0:1], pick_t[:], bias[:], start=True, stop=True)
            nc.tensor.transpose(pm[:, 8:8 + H_SB], pick_t[:], ident[0:H_SB, 0:H_SB])
            for gi in range(G):
                nc.tensor.transpose(pm[:, 32 + 32 * gi:64 + 32 * gi], own_t[:, gi], ident[0:T_S, 0:T_S])
                last = nc.tensor.transpose(pm[:, 128 + 32 * gi:160 + 32 * gi], sample_t[:, gi], ident[0:T_S, 0:T_S])
            last.then_inc(E("masks_turned"), 1)

            def turn(gi, p, u):
                n = PAGES * gi + p
                pe.wait_ge(E(f"k_in{u}"), 64 * (PAGES // AHEAD * gi + (p - u) // AHEAD) + 64)
                for b in range(4):
                    at_least(pe, E(f"k_copied{b % 2}"), 2 * (n - 1) + b // 2 + 1)
                    for c in range(4):
                        last = nc.tensor.transpose(pk[b][:, c], k_page[:, u, b, c * P:(c + 1) * P], ident[:])
                    last.then_inc(E(f"k_turned{b % 2}"), 1)

            def products(out, gi, moving):
                for c in range(4):
                    for b in range(4):
                        last = nc.tensor.matmul(out[R * b:R * b + R, :], qb[:, gi, c, b], moving(b, c), start=(c == 0), stop=(c == 3))
                last.then_inc(E("z_mm"), 1)

            def scores(gi, p, par):
                for e in range(2):
                    pe.wait_ge(E(f"k_copied{e}"), 2 * (PAGES * gi + p) + 2)
                r = ROUNDS * gi + p
                at_least(pe, E("z_out"), r if static(p, 0) else r - 1)
                products(pz[par][:, 0:P], gi, lambda b, c: k_turned[:, par, b, c])

            def own_scores(gi):
                pe.wait_ge(E("z_out"), ROUNDS * gi + PAGES - 1)
                products(pz[0][:, 0:T_S], gi, lambda b, c: kt[:, c, T_P:T])

            def turn_weights(gi, p, par, n=P):
                r = ROUNDS * gi + p
                pe.wait_ge(E("w_ready"), r + 1)
                at_least(pe, E("wt_copied"), r if static(p, 0) else r - 1)
                nc.tensor.transpose(pw[par][0:n, 0:P], w_s[:, par, 0:n], ident[:]).then_inc(E("w_turned"), 1)

            def values(gi, p, par, moving, first, last, keys=P):
                pe.wait_ge(E("wt_copied"), ROUNDS * gi + p + 1)
                for b in range(4):
                    mm = nc.tensor.matmul(pv[R * b:R * b + R, :], wt[0:keys, par, R * b:R * b + R], moving(b), start=first, stop=last)
                mm.then_inc(E("v_mm"), 1)

            pe.wait_ge(E("q_ready"), G)
            pe.wait_ge(E("masks_out"), 1)
            for gi in range(G):
                def key_round(p, u):
                    turn(gi, p, u)
                    if not static(p, 0):
                        scores(gi, p - 1, (u - 1) % 2)

                for p in range(AHEAD):
                    key_round(p, p)
                with pe.Fori(1, PAGES // AHEAD) as p4:
                    for u in range(AHEAD):
                        key_round(AHEAD * p4 + u, u)
                scores(gi, PAGES - 1, 1)
                own_scores(gi)

            pe.wait_ge(E("z_out"), ROUNDS * G)
            for gi in range(G):
                def page_values(p, u):
                    pe.wait_ge(E(f"v_in{u}"), 64 * (PAGES // AHEAD * gi + (p - u) // AHEAD) + 64)
                    values(gi, p, u % 2, lambda b: v_page[:, u, b], static(p, 0), False)

                def value_round(p, u):
                    turn_weights(gi, p, u % 2)
                    if not static(p, 0):
                        page_values(p - 1, (u - 1) % AHEAD)

                at_least(pe, E("o_kept"), gi)
                for p in range(AHEAD):
                    value_round(p, p)
                with pe.Fori(1, PAGES // AHEAD) as p4:
                    for u in range(AHEAD):
                        value_round(AHEAD * p4 + u, u)
                turn_weights(gi, PAGES, 0, T_S)
                page_values(PAGES - 1, AHEAD - 1)
                values(gi, PAGES, 0, lambda b: v_new[:], False, True, T_S)
            for gi in range(G):
                pe.wait_ge(E("o_kept"), gi + 1)
                last = nc.tensor.matmul(pm[0:T_S, :], sample[:, gi], o_rows[:, gi], start=(gi == 0), stop=(gi == G - 1))
            last.then_inc(E("gathered"), 1)

        @block.scalar
        def _(act):
            nc.scalar.preload_act_table_set("natural_log_exp_and_others")

            def key_round(gi, p, u):
                at_least(act, E("z_mm"), ROUNDS * gi + p - 1)
                for m in range(2):
                    act.wait_ge(E("k_turned0"), 2 * (PAGES * gi + p) + m + 1)
                    nc.scalar.activation(k_turned[:, u % 2, 2 * m], pk[2 * m][:], ACT.Copy).then_inc(E("k_copied0"), 1)

            def wt_copy(gi, p, par, n=P):
                r = ROUNDS * gi + p
                act.wait_ge(E("w_turned"), r + 1)
                at_least(act, E("v_mm"), r if static(p, 0) else r - 1)
                nc.scalar.activation(wt[0:n, par, :], pw[par][0:n, 0:P], ACT.Copy).then_inc(E("wt_copied"), 1)

            def weigh_step(gi, k):
                if k == 0:
                    act.wait_ge(E("z_out"), ROUNDS * (gi + 1))
                    nc.scalar.activation(ex[:, gi], ex[:, gi], ACT.Exp).then_inc(E("exped"), 1)
                if k == 1:
                    act.wait_ge(E("held"), gi + 1)
                    nc.scalar.activation(run[:, gi], ex[:, gi], ACT.Ln, bias=1.0).then_inc(E("logged"), 1)
                if k == 2:
                    act.wait_ge(E("summed"), gi + 1)
                    nc.scalar.activation(run[:, gi], run[:, gi], ACT.Exp, scale=-1.0).then_inc(E("decayed"), 1)

            def keys(gi, weigh):
                def one_round(p, u):
                    key_round(gi, p, u % 2)
                    if isinstance(p, int) and p + AHEAD - 1 >= PAGES:
                        if gi + 1 < G:
                            load_keys(act, (2, 3), gi + 1, p + AHEAD - 1 - PAGES, (u + AHEAD - 1) % AHEAD)
                    else:
                        load_keys(act, (2, 3), gi, p + AHEAD - 1, (u + AHEAD - 1) % AHEAD)

                for p in range(AHEAD):
                    one_round(p, p)
                    if weigh is not None:
                        weigh_step(weigh, p)
                with act.Fori(1, PAGES // AHEAD - 1) as p4:
                    for u in range(AHEAD):
                        one_round(AHEAD * p4 + u, u)
                for u in range(AHEAD):
                    one_round(PAGES - AHEAD + u, u)

            def value_pages(gi, weigh):
                def value_round(p, u):
                    wt_copy(gi, p, u % 2)
                    if not static(p, 0):
                        load_values(act, (2, 3), gi, p + AHEAD - 1, (u + AHEAD - 1) % AHEAD)

                for p in range(AHEAD):
                    value_round(p, p)
                    if weigh is not None:
                        weigh_step(weigh, p)
                with act.Fori(1, PAGES // AHEAD - 1) as p4:
                    for u in range(AHEAD):
                        value_round(AHEAD * p4 + u, u)
                value_round(PAGES - AHEAD, 0)
                for p in range(PAGES - AHEAD + 1, PAGES):
                    wt_copy(gi, p, p % 2)
                wt_copy(gi, PAGES, 0, T_S)

            act.wait_ge(E("table_in"), 16)
            for u in range(AHEAD - 1):
                load_keys(act, (2, 3), 0, u, u)
            keys(0, None)
            keys(1, 0)
            value_pages(0, 1)
            for u in range(AHEAD):
                load_values(act, (2, 3), 1, u, u)
            value_pages(1, None)
            act.wait_ge(E("gathered"), 1)
            nc.scalar.activation(mixed[0:T_S, NT, DN:D], pm[0:T_S, :], ACT.Copy).then_inc(E("o_out"), 1)

        @block.vector
        def _(dve):
            def z_out(gi, p, par, cols):
                dve.wait_ge(E("z_mm"), ROUNDS * gi + p + 1)
                n = P if cols is None else T_S
                cols = bass.ds(p * P, P) if cols is None else cols
                nc.vector.tensor_scalar(ex[:, gi, cols], pz[par][:, 0:n], row_bias[:], None, ALU.add).then_inc(E("z_out"), 1)

            def key_round(gi, p, u):
                at_least(dve, E("z_mm"), ROUNDS * gi + p - 1)
                for m in range(2):
                    dve.wait_ge(E("k_turned1"), 2 * (PAGES * gi + p) + m + 1)
                    nc.vector.tensor_copy(k_turned[:, u, 2 * m + 1], pk[2 * m + 1][:]).then_inc(E("k_copied1"), 1)
                if not static(p, 0):
                    z_out(gi, p - 1, (u - 1) % 2, None)

            def weigh_step(gi, k):
                if k == 0:
                    dve.wait_ge(E("exped"), gi + 1)
                    nc.vector.tensor_scalar(ex[:, gi, 0:CACHED], ex[:, gi, 0:CACHED], BIG, None, ALU.min)
                    nc.vector.scalar_tensor_tensor(ex[:, gi, CACHED:KEYS], ex[:, gi, CACHED:KEYS], BIG, own[:, gi], ALU.min, ALU.mult).then_inc(E("held"), 1)
                if k == 1:
                    dve.wait_ge(E("logged"), gi + 1)
                    nc.vector.tensor_tensor_scan(run[:, gi, ::-1], run[:, gi, ::-1], zeros[:].broadcast_to([P, KEYS]), 0.0, ALU.add, ALU.add).then_inc(E("summed"), 1)

            def weights(gi, p, par, n=P):
                r = ROUNDS * gi + p
                if static(p, 0):
                    dve.wait_ge(E("decayed"), gi + 1)
                at_least(dve, E("w_turned"), r if static(p, 0) else r - 1)
                c = bass.ds(p * P, P) if n == P else slice(CACHED, KEYS)
                nc.vector.tensor_tensor(w_s[:, par, 0:n], ex[:, gi, c], run[:, gi, c], ALU.mult).then_inc(E("w_ready"), 1)

            dve.wait_ge(E("masks_turned"), 1)
            nc.vector.tensor_copy(row_bias[:], pm[:, 0:1])
            nc.vector.tensor_copy(pick[:], pm[:, 8:8 + H_SB])
            nc.vector.tensor_copy(own[:], pm[:, 32:96].rearrange("p (g j) -> p g j", g=G))
            nc.vector.tensor_copy(sample[:], pm[:, 128:192].rearrange("p (g j) -> p g j", g=G)).then_inc(E("masks_out"), 1)
            for gi in range(G):
                for h in range(H_SB):
                    c, e = h // 2, h % 2
                    src = qt[e * DH:(e + 1) * DH, c, T_P + 16 * gi:T_P + 16 * gi + 16].rearrange("p (b q) -> p b q", q=L_S)
                    last = nc.vector.tensor_copy(qb[e * DH:(e + 1) * DH, gi, c, :, L_S * h:L_S * h + L_S], src)
                last.then_inc(E("q_ready"), 1)
            dve.wait_ge(E("masks_out"), 1)
            dve.wait_ge(E("zeros_made"), 1)
            for gi in range(G):
                for p in range(AHEAD):
                    key_round(gi, p, p % 2)
                    if gi > 0:
                        weigh_step(gi - 1, p)
                with dve.Fori(AHEAD // 2, PAGES // 2) as p2:
                    for u in range(2):
                        key_round(gi, 2 * p2 + u, u)
                z_out(gi, PAGES - 1, 1, None)
                z_out(gi, PAGES, 0, slice(CACHED, KEYS))
            for gi in range(G):
                for p in range(AHEAD):
                    weights(gi, p, p % 2)
                    if gi == 0:
                        weigh_step(G - 1, p)
                with dve.Fori(AHEAD // 2, PAGES // 2) as p2:
                    for u in range(2):
                        weights(gi, 2 * p2 + u, u)
                weights(gi, PAGES, 0, T_S)
                dve.wait_ge(E("v_mm"), ROUNDS * (gi + 1))
                nc.vector.tensor_tensor(o_rows[:, gi].rearrange("p (h c) -> p h c", c=DH), pv[:].rearrange("p (h c) -> p h c", c=DH),
                                        pick[:].rearrange("p (h o) -> p h o", o=1).broadcast_to([P, H_SB, DH]), ALU.mult).then_inc(E("o_kept"), 1)


def mix_out(nc, mixed, gate_rows, dn_gain_row, sb_gain_row, w_o, y, ident):
    with ExitStack() as ctx:
        s = Scope(nc, ctx, "mo")
        E = s.event
        N = NT + 1
        w_raw = s.sb("w_raw", [P, KC, D])
        w_hi, w_lo = s.sb("w_hi", [P, KC, D], F32R), s.sb("w_lo", [P, KC, D], F32R)
        m_hi, m_lo = s.sb("m_hi", [P, 2, KC, P], F32R), s.sb("m_lo", [P, 2, KC, P], F32R)
        gate = s.sb("gate", [P, 2, DN])
        g_dn, g_sb = s.sb("g_dn", [P, P]), s.sb("g_sb", [P, DH])
        sq = s.sb("sq", [P, D])
        stat = s.sb("stat", [P, 3, N, H_DN + H_SB])
        pt = [s.ps(f"pt{n}", [P, KC, P]) for n in range(2)]
        po = [s.ps(f"po{n}", [P, 512]) for n in range(4)]
        block = ctx.enter_context(nc.Block())

        def span(i):
            return slice(0, P) if i < NT else slice(P - T_S, P)

        def rows_of(i):
            return P if i < NT else T_S

        @block.sync
        def _(sp):
            def load_gate(i):
                at_least(sp, E("finished"), i - 1)
                sp.dma_start(gate[0:rows_of(i), i % 2, :], gate_rows[i * P:i * P + rows_of(i), :]).then_inc(E(f"gate_in{i % 2}"), 16)

            load_gate(0)
            sp.dma_start(g_dn[:], dn_gain_row.partition_broadcast(P)).then_inc(E("gains_in"), 16)
            sp.dma_start(g_sb[:], sb_gain_row.partition_broadcast(P)).then_inc(E("gains_in"), 16)
            load_gate(1)
            view = w_o.rearrange("(k p) n -> p k n", p=P)
            for k in range(KC):
                sp.dma_start(w_raw[:, k, :], view[:, k, :]).then_inc(E(f"w_in{k}"), 16)
            for i in range(2, N):
                load_gate(i)

        @block.tensor
        def _(pe):
            def turn(i):
                n = rows_of(i)
                pe.wait_ge(E("finished"), i + 1)
                at_least(pe, E("m_lo"), i - 1)
                for k in range(KC):
                    last = nc.tensor.transpose(pt[i % 2][:, k, 0:n], mixed[0:n, i, k * P:(k + 1) * P], ident[0:n, 0:n])
                last.then_inc(E("turned"), 1)

            turn(0)
            turn(1)
            for i in range(N):
                pe.wait_ge(E("m_lo"), i + 1)
                for half in range(2):
                    n = 2 * i + half
                    at_least(pe, E("y_out"), n - 3)
                    for k in range(KC):
                        if i == 0 and half == 0:
                            pe.wait_ge(E("w_lo"), k + 1)
                        cols = slice(half * 512, half * 512 + 512)
                        out = po[n % 4][:]
                        nc.tensor.matmul(out, m_hi[:, i % 2, k], w_hi[:, k, cols], start=(k == 0), stop=False)
                        nc.tensor.matmul(out, m_lo[:, i % 2, k], w_hi[:, k, cols], start=False, stop=False)
                        last = nc.tensor.matmul(out, m_hi[:, i % 2, k], w_lo[:, k, cols], start=False, stop=(k == KC - 1))
                    last.then_inc(E("y_mm"), 1)
                if i + 2 < N:
                    turn(i + 2)

        @block.scalar
        def _(act):
            def square(i):
                n = rows_of(i)
                at_least(act, E("reduced"), 2 * i)
                nc.scalar.activation(sq[0:n], mixed[0:n, i, :], ACT.Square).then_inc(E("squared"), 1)

            def root(i):
                n = rows_of(i)
                act.wait_ge(E("mean"), i + 1)
                nc.scalar.activation(stat[0:n, 1, i], stat[0:n, 0, i], ACT.Sqrt).then_inc(E("root"), 1)

            def hi(i):
                act.wait_ge(E("turned"), i + 1)
                at_least(act, E("y_mm"), 2 * (i - 1))
                if i == NT:
                    act.wait_ge(E("cleared"), 2)
                nc.scalar.activation(m_hi[:, i % 2, :, span(i)], pt[i % 2][:, :, 0:rows_of(i)], ACT.Copy).then_inc(E("m_hi"), 1)

            def round_weights(k):
                act.wait_ge(E(f"w_in{k}"), 16)
                nc.scalar.activation(w_hi[:, k, :], w_raw[:, k, :], ACT.Copy).then_inc(E("w_hi"), 1)

            square(0)
            root(0)
            square(1)
            round_weights(0)
            hi(0)
            root(1)
            for k in range(1, KC):
                round_weights(k)
                if k == 3:
                    hi(1)
            for i in range(N):
                for half in range(2):
                    n = 2 * i + half
                    if i + 2 < N:
                        (square, root)[half](i + 2)
                    act.wait_ge(E("y_mm"), n + 1)
                    nc.scalar.activation(y[:, i, half * 512:half * 512 + 512], po[n % 4][:], ACT.Copy).then_inc(E("y_out"), 1)
                if i + 2 < N:
                    hi(i + 2)

        @block.vector
        def _(dve):
            def finish(i):
                n = rows_of(i)
                dve.wait_ge(E("squared"), i + 1)
                heads = ((0, P, 0, H_DN), (DN, DH, H_DN, H_DN + H_SB))
                for at, w, h0, h1 in heads:
                    nc.vector.tensor_reduce(stat[0:n, 0, i, h0:h1], sq[0:n, at:at + DN].rearrange("p (h c) -> p h c", c=w),
                                            AX.X, ALU.add).then_inc(E("reduced"), 1)
                dve.wait_ge(E("reduced"), 2 * i + 2)
                for at, w, h0, h1 in heads:
                    last = nc.vector.tensor_scalar(stat[0:n, 0, i, h0:h1], stat[0:n, 0, i, h0:h1], 1.0 / w, EPS, ALU.mult, ALU.add)
                last.then_inc(E("mean"), 1)
                dve.wait_ge(E(f"gate_in{i % 2}"), 16 * (i // 2) + 16)
                if i == 0:
                    dve.wait_ge(E("gains_in"), 32)
                v = gate[0:n, i % 2, :].rearrange("p (h c) -> p h c", c=P)
                nc.vector.tensor_tensor(v, v, g_dn[0:n, :].rearrange("p (o c) -> p o c", o=1).broadcast_to([n, H_DN, P]), ALU.mult)
                dve.wait_ge(E("root"), i + 1)
                nc.vector.reciprocal(stat[0:n, 2, i], stat[0:n, 1, i]).then_inc(E("rstd"), 1)
                dve.wait_ge(E("rstd"), i + 1)
                a = mixed[0:n, i, 0:DN].rearrange("p (h c) -> p h c", c=P)
                b = mixed[0:n, i, DN:D].rearrange("p (h c) -> p h c", c=DH)
                r = stat[0:n, 2, i, :].rearrange("p (h o) -> p h o", o=1)
                nc.vector.tensor_tensor(a, a, r[:, 0:H_DN].broadcast_to([n, H_DN, P]), ALU.mult)
                nc.vector.tensor_tensor(b, b, r[:, H_DN:].broadcast_to([n, H_SB, DH]), ALU.mult).then_inc(E("scaled"), 1)
                dve.wait_ge(E("scaled"), i + 1)
                nc.vector.tensor_tensor(a, a, v, ALU.mult)
                nc.vector.tensor_tensor(b, b, g_sb[0:n, :].rearrange("p (o c) -> p o c", o=1).broadcast_to([n, H_SB, DH]),
                                        ALU.mult).then_inc(E("finished"), 1)

            def lo(i):
                dve.wait_ge(E("m_hi"), i + 1)
                nc.vector.tensor_tensor(m_lo[:, i % 2, :, span(i)], pt[i % 2][:, :, 0:rows_of(i)],
                                        m_hi[:, i % 2, :, span(i)].bitcast(F32), ALU.subtract).then_inc(E("m_lo"), 1)

            def rest_weights(k):
                dve.wait_ge(E("w_hi"), k + 1)
                nc.vector.tensor_tensor(w_lo[:, k, :], w_raw[:, k, :], w_hi[:, k, :].bitcast(F32), ALU.subtract).then_inc(E("w_lo"), 1)

            finish(0)
            rest_weights(0)
            lo(0)
            finish(1)
            for k in range(1, KC):
                rest_weights(k)
                if k == 3:
                    lo(1)
            for i in range(2, N):
                finish(i)
                if i == NT:
                    dve.wait_ge(E("y_mm"), 2 * (NT - 1))
                    for m in (m_hi, m_lo):
                        nc.vector.memset(m[:, i % 2, :, 0:P - T_S].bitcast(F32), 0.0).then_inc(E("cleared"), 1)
                    dve.wait_ge(E("cleared"), 2)
                lo(i)


def hymba_step(nc, x, cache_k, cache_v, page_table, state_delta, state_conv, norms, ffn1_gu, ffn1_d, w_in, conv_w,
               a_log, dt_bias, dn_norm, sb_bias, sb_norm, w_o, ffn2_gu, ffn2_d, y_out, k_rows, v_rows, delta_p, delta_s, conv_rows):
    qkv_nat = nc.dram_tensor("qkv_rows", (T, QKV), F32, kind="Internal").ap()
    gate_nat = nc.dram_tensor("gate_rows", (T, DN), F32, kind="Internal").ap()
    h1 = nc.dram_tensor("h1", (T, D), F32, kind="Internal").ap()
    h2 = nc.dram_tensor("h2", (T, D), F32, kind="Internal").ap()
    with ExitStack() as ctx:
        whole = Scope(nc, ctx, "w")
        ident = whole.sb("ident", [P, P])
        make_ident(nc, ident)
        ab = whole.sb("ab", [P, NT + 1, 8])
        mix = ctx.enter_context(ExitStack())

        with ExitStack() as queries:
            with ExitStack() as c:
                u = Scope(nc, c, "u")
                uh, ul = u.sb("uh", [P, KC, T], F32R), u.sb("ul", [P, KC, T], F32R)
                with ExitStack() as c2:
                    y = Scope(nc, c2, "y1").sb("y", [P, NT + 1, D])
                    seam(nc, "n1", y, x, None, None, None, norms[0], uh, ul, ident)
                    ffn(nc, "f1", uh, ul, ffn1_gu, ffn1_d, y)
                    seam(nc, "n2", y, x, norms[1], 0.5, h1, norms[2], uh, ul, ident)
                t = Scope(nc, queries, "t")
                qt, kt = t.sb("qt", [P, 4, T], side="right"), t.sb("kt", [P, 4, T], side="right")
                projections(nc, uh, ul, w_in, conv_w, state_conv, qt, kt, ab, qkv_nat, gate_nat, k_rows, v_rows, conv_rows, ident)
            s = Scope(nc, mix, "m")
            mixed = s.sb("mixed", [P, NT + 1, D])
            masks = s.sb("masks", [P, 1 + LEVELS, P])
            tri_s, same_s = s.sb("tri_s", [T_S, T_S]), s.sb("same_s", [T_S, T_S])
            level_s, spread_s = s.sb("level_s", [T_S, 2, T_S]), s.sb("spread_s", [T_S, N_B])
            ones = s.sb("ones", [P, P])
            prompt_attention(nc, qt, kt, v_rows, sb_bias, mixed[:, 0:NT, DN:D], ident)
            sample_attention(nc, qt, kt, v_rows, cache_k, cache_v, page_table, sb_bias, ident, mixed,
                             lambda pool, made: delta_masks(nc, pool, made, masks, tri_s, same_s, level_s, spread_s, ones))
        with ExitStack() as c:
            s = Scope(nc, c, "d")
            g, big_g, last_decay = (s.sb(n, [P, NT + 1, 4]) for n in ("g", "big_g", "last_decay"))
            last_decay_s = s.sb("last_decay_s", [P, N_B, 4])
            fac = {n: s.sb(n, [P, NT + 1, 4]) for n in FACTORS}
            qkv = s.sb("qkv", [P, NT + 1, QKV])
            delta_gates(nc, ab, qkv_nat, dt_bias, a_log, masks, tri_s, same_s, spread_s, ones, qkv, g, big_g,
                        last_decay, last_decay_s, fac)
            delta_prompt(nc, g, big_g, last_decay, fac, qkv, masks, ident, mixed, delta_p)
            delta_sample(nc, g, big_g, last_decay_s, fac, qkv, tri_s, level_s, spread_s, ident, state_delta, mixed, delta_s)
        y = whole.sb("y", [P, NT + 1, D], side="right")
        mix_out(nc, mixed, gate_nat, dn_norm, sb_norm, w_o, y, ident)
        mix.close()
        uh, ul = whole.sb("uh", [P, KC, T], F32R), whole.sb("ul", [P, KC, T], F32R)
        seam(nc, "n3", y, h1, norms[3], 1.0, h2, norms[4], uh, ul, ident)
        ffn(nc, "f2", uh, ul, ffn2_gu, ffn2_d, y)
        seam(nc, "n4", y, h2, norms[5], 0.5, y_out, None, None, None, ident)


def kernel(x_prompt, x_sample, cache_sb_k, cache_sb_v, page_table, state_delta, state_conv, norms, ffn1_w_gate_up,
           ffn1_w_down, w_in, conv_w, a_log, dt_bias, dn_out_norm, sb_logit_bias, sb_out_norm, w_o, ffn2_w_gate_up,
           ffn2_w_down):
    import numpy as np
    import concourse.bacc as bacc
    from concourse.bass_utils import run_bass_kernel_spmd

    n_phys, page = cache_sb_k.shape[:2]
    arrays = {
        "x": np.concatenate([np.asarray(x_prompt).reshape(T_P, D), np.asarray(x_sample).reshape(T_S, D)]),
        "cache_k": np.asarray(cache_sb_k).reshape(n_phys, page, SB),
        "cache_v": np.asarray(cache_sb_v).reshape(n_phys, page, SB),
        "page_table": np.asarray(page_table),
        "state_delta": np.asarray(state_delta)[0],
        "state_conv": np.asarray(state_conv).reshape(3 * N_B, QKV),
        "norms": np.asarray(norms)[0],
        "ffn1_gu": np.asarray(ffn1_w_gate_up)[0],
        "ffn1_d": np.asarray(ffn1_w_down)[0],
        "w_in": np.asarray(w_in)[0],
        "conv_w": np.asarray(conv_w)[0],
        "a_log": np.asarray(a_log)[0],
        "dt_bias": np.asarray(dt_bias)[0],
        "dn_norm": np.asarray(dn_out_norm)[0],
        "sb_bias": np.asarray(sb_logit_bias)[0],
        "sb_norm": np.asarray(sb_out_norm)[0],
        "w_o": np.asarray(w_o)[0],
        "ffn2_gu": np.asarray(ffn2_w_gate_up)[0],
        "ffn2_d": np.asarray(ffn2_w_down)[0],
    }
    outs = {
        "y_out": (T, D),
        "k_rows": (T, SB),
        "v_rows": (T, SB),
        "delta_p": (H_DN, P, P),
        "delta_s": (N_B, H_DN, P, P),
        "conv_rows": (TAIL, QKV),
    }
    nc = bacc.Bacc("TRN2", target_bir_lowering=False, num_devices=1)
    in_maps, args = {}, []
    for name, a in arrays.items():
        in_maps[f"in_{name}"] = np.ascontiguousarray(a)
        args.append(nc.dram_tensor(f"in_{name}", a.shape, mybir.dt.from_np(a.dtype), kind="ExternalInput").ap())
    for name, shape in outs.items():
        args.append(nc.dram_tensor(f"out_{name}", shape, F32, kind="ExternalOutput").ap())
    hymba_step(nc, *args)
    got = run_bass_kernel_spmd(nc, [in_maps], core_ids=[0]).results[0]
    y, k, v = (got[f"out_{n}"] for n in ("y_out", "k_rows", "v_rows"))
    conv = got["out_conv_rows"]
    heads = lambda r, b, n: r.reshape(b, n, 1, H_SB, DH)
    return (y[:T_P].reshape(1, T_P, D), y[T_P:].reshape(N_B, L_S, D),
            heads(k[:T_P], 1, T_P), heads(v[:T_P], 1, T_P), heads(k[T_P:], N_B, L_S), heads(v[T_P:], N_B, L_S),
            got["out_delta_p"].reshape(1, 1, H_DN, P, P), got["out_delta_s"].reshape(1, N_B, H_DN, P, P),
            conv[:3].reshape(1, 1, 3, QKV), conv[3:].reshape(1, N_B, 3, QKV))
```
